# Optimizing a Trainium2 kernel written in Bass

```python
import math
import jax, jax.numpy as jnp
from jax import lax
import numpy as np

D_MODEL = 1024
BATCH = 1
SEQ = 1024
DEPTH = 1

HEAD_DIM = 64
NSA_HEADS = 8
NSA_KV_GROUPS = 2
NSA_HPG = NSA_HEADS // NSA_KV_GROUPS
NSA_WIDTH = NSA_HEADS * HEAD_DIM
CMP_BLOCK = 32
CMP_STRIDE = 16
SLC_BLOCK = 64
SLC_TOPK = 16
WIN = 512
FORCE_SCORE = 1.0e4
DIL_HEADS = 8
DIL_WIDTH = DIL_HEADS * HEAD_DIM
DIL_PATTERNS = ((128, 1), (512, 4), (2048, 16))
Q_BLOCK = 128
RMS_EPS = 1e-6
N_ALIBI_HEADS = NSA_HEADS + DIL_HEADS
C_NSA_Q = NSA_WIDTH
C_NSA_KV = 6 * NSA_KV_GROUPS * HEAD_DIM
C_NSA_GATE = 3 * NSA_HEADS
C_NSA_Z = NSA_WIDTH
C_DIL_QKV = 3 * DIL_WIDTH
C_DIL_Z = DIL_WIDTH
C_MERGE = 2 * D_MODEL
C_IN = C_NSA_Q + C_NSA_KV + C_NSA_GATE + C_NSA_Z + C_DIL_QKV + C_DIL_Z + C_MERGE

kernel_name = 'nsa_dilated_hybrid_block'

def rmsnorm(x, g):
    xf = x.astype(jnp.float32)
    y = xf * lax.rsqrt(jnp.mean(xf * xf, axis=-1, keepdims=True) + RMS_EPS)
    return (y * g.astype(jnp.float32)).astype(x.dtype)

def masked_softmax(s, mask):
    s = jnp.where(mask, s, -jnp.inf)
    m = jnp.max(s, axis=-1, keepdims=True)
    m = jnp.where(jnp.isfinite(m), m, 0.0)
    e = jnp.exp(s - m)
    l = jnp.sum(e, axis=-1, keepdims=True)
    p = e / jnp.maximum(l, 1e-30)
    lse = m[..., 0] + jnp.log(l[..., 0])
    return p, lse

def alibi_slopes():
    s = 2.0 ** (-8.0 * np.arange(1, N_ALIBI_HEADS + 1) / N_ALIBI_HEADS)
    return jnp.asarray(s[0::2], jnp.float32), jnp.asarray(s[1::2], jnp.float32)

def overlap_matrix(n_cmp, n_sel):
    i = np.arange(n_cmp)[:, None]
    j = np.arange(n_sel)[None, :]
    lo = np.maximum(i * CMP_STRIDE, j * SLC_BLOCK)
    hi = np.minimum(i * CMP_STRIDE + CMP_BLOCK, (j + 1) * SLC_BLOCK)
    return (np.clip(hi - lo, 0, None) / CMP_BLOCK).astype(np.float32)

def nsa_compress(src, pos, w1, w2):
    S = src.shape[1]
    n_cmp = (S - CMP_BLOCK) // CMP_STRIDE + 1
    idx = np.arange(n_cmp)[:, None] * CMP_STRIDE + np.arange(CMP_BLOCK)[None, :]
    blocks = src[:, idx] + pos[None, None, :, None, :]
    hid = jax.nn.gelu(jnp.einsum('bnlgd,lde->bgne', blocks, w1))
    return jnp.einsum('bgne,ef->bgnf', hid, w2)

def nsa_attention(q, kv, gates, pos_k, w1_k, w2_k, pos_v, w1_v, w2_v, slopes):
    B, S, H, dh = q.shape
    G, hpg = NSA_KV_GROUPS, NSA_HPG
    qg = q.reshape(B, S, G, hpg, dh).transpose(0, 2, 3, 1, 4)
    k_cmp = nsa_compress(kv[:, :, 0], pos_k, w1_k, w2_k)
    v_cmp = nsa_compress(kv[:, :, 1], pos_v, w1_v, w2_v)
    n_cmp = k_cmp.shape[2]
    n_sel = S // SLC_BLOCK
    top_k = min(SLC_TOPK, n_sel)
    k_slc = kv[:, :, 2].transpose(0, 2, 1, 3).reshape(B, G, n_sel, SLC_BLOCK, dh)
    v_slc = kv[:, :, 3].transpose(0, 2, 1, 3).reshape(B, G, n_sel, SLC_BLOCK, dh)
    pad = ((0, 0), (0, 0), (WIN, 0), (0, 0))
    k_win = jnp.pad(kv[:, :, 4].transpose(0, 2, 1, 3), pad)
    v_win = jnp.pad(kv[:, :, 5].transpose(0, 2, 1, 3), pad)
    cmp_end = jnp.asarray(np.arange(n_cmp) * CMP_STRIDE + CMP_BLOCK - 1, jnp.int32)
    overlap = jnp.asarray(overlap_matrix(n_cmp, n_sel))
    slope = slopes.reshape(G, hpg)
    b_idx = jnp.arange(B)[:, None, None, None]
    g_idx = jnp.arange(G)[None, :, None, None]
    within = jnp.arange(SLC_BLOCK)
    win_off = jnp.arange(Q_BLOCK + WIN) - WIN
    blk_ids = jnp.arange(n_sel)

    def block(n):
        start = n * Q_BLOCK
        t = start + jnp.arange(Q_BLOCK)
        qb = lax.dynamic_slice_in_dim(qg, start, Q_BLOCK, axis=3)
        dist_c = t[:, None] - cmp_end[None, :]
        s_c = (jnp.einsum('bghqd,bgnd->bghqn', qb, k_cmp).astype(jnp.float32)
               - slope[None, :, :, None, None] * dist_c.astype(jnp.float32))
        p_c, _ = masked_softmax(s_c, dist_c >= 0)
        o_c = jnp.einsum('bghqn,bgnd->bghqd', p_c.astype(v_cmp.dtype), v_cmp)
        imp = jnp.einsum('bghqn,nj->bgqj', p_c, overlap)
        cur = t // SLC_BLOCK
        forced = (blk_ids[None] == 0) | (blk_ids[None] == cur[:, None]) | (blk_ids[None] == cur[:, None] - 1)
        valid = blk_ids[None] <= cur[:, None]
        score = jnp.where(valid, jnp.where(forced, FORCE_SCORE, imp), -1.0)
        top_val, top_idx = lax.top_k(score, top_k)
        kb = k_slc[b_idx, g_idx, top_idx]
        vb = v_slc[b_idx, g_idx, top_idx]
        pos_s = top_idx[..., None] * SLC_BLOCK + within
        dist_s = t[None, None, :, None, None] - pos_s
        mask_s = (top_val >= 0.0)[..., None] & (dist_s >= 0)
        s_s = (jnp.einsum('bghqd,bgqkld->bghqkl', qb, kb).astype(jnp.float32)
               - slope[None, :, :, None, None, None] * dist_s[:, :, None].astype(jnp.float32))
        shp = s_s.shape
        p_s, _ = masked_softmax(s_s.reshape(shp[:4] + (-1,)),
                                mask_s[:, :, None].reshape(B, G, 1, Q_BLOCK, -1))
        o_s = jnp.einsum('bghqkl,bgqkld->bghqd', p_s.reshape(shp).astype(vb.dtype), vb)
        kw = lax.dynamic_slice_in_dim(k_win, start, Q_BLOCK + WIN, axis=2)
        vw = lax.dynamic_slice_in_dim(v_win, start, Q_BLOCK + WIN, axis=2)
        pos_w = start + win_off
        dist_w = t[:, None] - pos_w[None, :]
        mask_w = (dist_w >= 0) & (dist_w < WIN) & (pos_w[None, :] >= 0)
        s_w = (jnp.einsum('bghqd,bgkd->bghqk', qb, kw).astype(jnp.float32)
               - slope[None, :, :, None, None] * dist_w.astype(jnp.float32))
        p_w, _ = masked_softmax(s_w, mask_w)
        o_w = jnp.einsum('bghqk,bgkd->bghqd', p_w.astype(vw.dtype), vw)
        return o_c, o_s, o_w

    o_c, o_s, o_w = lax.map(block, jnp.arange(S // Q_BLOCK))

    def to_seq(o):
        return o.transpose(1, 0, 4, 2, 3, 5).reshape(B, S, H, dh)

    return (gates[:, :, 0, :, None] * to_seq(o_c) + gates[:, :, 1, :, None] * to_seq(o_s)
            + gates[:, :, 2, :, None] * to_seq(o_w))

def dilated_branch(q, k, v, slopes, window, dilation):
    B, S, H, dh = q.shape
    L = S // dilation
    wd = window // dilation
    c = Q_BLOCK
    nbd = -(-L // c)
    Lp = nbd * c

    def phase(a):
        a = a.reshape(B, L, dilation, H, dh).transpose(0, 3, 2, 1, 4)
        return jnp.pad(a, ((0, 0), (0, 0), (0, 0), (c, Lp - L), (0, 0)))

    def band(a):
        prev = a[..., :Lp, :].reshape(B, H, dilation, nbd, c, dh)
        cur = a[..., c:, :].reshape(B, H, dilation, nbd, c, dh)
        return jnp.concatenate([prev, cur], axis=-2)

    qp = phase(q)[..., c:, :].reshape(B, H, dilation, nbd, c, dh)
    kb = band(phase(k))
    vb = band(phase(v))
    i = np.arange(c)[:, None]
    j = np.arange(2 * c)[None, :]
    kk = c + i - j
    key_l = (np.arange(nbd)[:, None, None] - 1) * c + j[None]
    mask = jnp.asarray((kk >= 0)[None] & (kk <= wd)[None] & (key_l >= 0))
    dist = jnp.asarray((kk * dilation).astype(np.float32))
    s = (jnp.einsum('bhpnqd,bhpnkd->bhpnqk', qp, kb).astype(jnp.float32)
         - slopes[None, :, None, None, None, None] * dist)
    p, lse = masked_softmax(s, mask[None, None, None])
    o = jnp.einsum('bhpnqk,bhpnkd->bhpnqd', p.astype(vb.dtype), vb)
    o = o.reshape(B, H, dilation, Lp, dh)[..., :L, :].transpose(0, 3, 2, 1, 4).reshape(B, S, H, dh)
    lse = lse.reshape(B, H, dilation, Lp)[..., :L].transpose(0, 3, 2, 1).reshape(B, S, H)
    return o, lse

def dilated_attention(q, k, v, slopes):
    outs, lses = [], []
    for window, dilation in DIL_PATTERNS:
        o, lse = dilated_branch(q, k, v, slopes, window, dilation)
        outs.append(o)
        lses.append(lse)
    w = jax.nn.softmax(jnp.stack(lses, axis=0), axis=0)
    return jnp.sum(w[..., None].astype(q.dtype) * jnp.stack(outs, axis=0), axis=0)

def hybrid_layer(xn, w_in, cmp_pos_k, cmp_w1_k, cmp_w2_k, cmp_pos_v, cmp_w1_v, cmp_w2_v,
                 w_br_nsa, w_br_dil, w_out):
    B, S, _ = xn.shape
    proj = jnp.einsum('bsd,dc->bsc', xn, w_in)
    offs = np.cumsum([C_NSA_Q, C_NSA_KV, C_NSA_GATE, C_NSA_Z, C_DIL_QKV, C_DIL_Z]).tolist()
    q_n, kv_n, g_n, z_n, qkv_d, z_d, mg = jnp.split(proj, offs, axis=-1)
    scale = HEAD_DIM ** -0.5
    slopes_nsa, slopes_dil = alibi_slopes()
    o_nsa = nsa_attention(q_n.reshape(B, S, NSA_HEADS, HEAD_DIM) * scale,
                          kv_n.reshape(B, S, 6, NSA_KV_GROUPS, HEAD_DIM),
                          jax.nn.sigmoid(g_n.reshape(B, S, 3, NSA_HEADS)),
                          cmp_pos_k, cmp_w1_k, cmp_w2_k, cmp_pos_v, cmp_w1_v, cmp_w2_v, slopes_nsa)
    o_nsa = o_nsa.reshape(B, S, NSA_WIDTH) * jax.nn.silu(z_n)
    qkv_d = qkv_d.reshape(B, S, 3, DIL_HEADS, HEAD_DIM)
    o_dil = dilated_attention(qkv_d[:, :, 0] * scale, qkv_d[:, :, 1], qkv_d[:, :, 2], slopes_dil)
    o_dil = o_dil.reshape(B, S, DIL_WIDTH) * jax.nn.silu(z_d)
    mg = jax.nn.sigmoid(mg.reshape(B, S, 2, D_MODEL))
    merged = (mg[:, :, 0] * jnp.einsum('bsc,cd->bsd', o_nsa, w_br_nsa)
              + mg[:, :, 1] * jnp.einsum('bsc,cd->bsd', o_dil, w_br_dil))
    return jnp.einsum('bsd,de->bse', merged, w_out)

def setup_inputs(seed: int = 0) -> dict:
    key = jax.random.key(seed)
    ks = jax.random.split(key, 13)
    hd = HEAD_DIM

    def nrm(k, shape, scale):
        return jax.random.normal(k, shape, jnp.float32) * scale

    return {
        'x': nrm(ks[0], (BATCH, SEQ, D_MODEL), 1.0),
        'norm_g': 1.0 + nrm(ks[1], (DEPTH, D_MODEL), 0.05),
        'w_in': nrm(ks[2], (DEPTH, D_MODEL, C_IN), D_MODEL ** -0.5),
        'cmp_pos_k': nrm(ks[3], (DEPTH, CMP_BLOCK, hd), 0.1),
        'cmp_w1_k': nrm(ks[4], (DEPTH, CMP_BLOCK, hd, hd), (CMP_BLOCK * hd) ** -0.5),
        'cmp_w2_k': nrm(ks[5], (DEPTH, hd, hd), hd ** -0.5),
        'cmp_pos_v': nrm(ks[6], (DEPTH, CMP_BLOCK, hd), 0.1),
        'cmp_w1_v': nrm(ks[7], (DEPTH, CMP_BLOCK, hd, hd), (CMP_BLOCK * hd) ** -0.5),
        'cmp_w2_v': nrm(ks[8], (DEPTH, hd, hd), hd ** -0.5),
        'w_br_nsa': nrm(ks[9], (DEPTH, NSA_WIDTH, D_MODEL), NSA_WIDTH ** -0.5),
        'w_br_dil': nrm(ks[10], (DEPTH, DIL_WIDTH, D_MODEL), DIL_WIDTH ** -0.5),
        'w_out': nrm(ks[11], (DEPTH, D_MODEL, D_MODEL), D_MODEL ** -0.5),
        'final_g': 1.0 + nrm(ks[12], (D_MODEL,), 0.05),
    }

def reference(x, norm_g, w_in, cmp_pos_k, cmp_w1_k, cmp_w2_k, cmp_pos_v, cmp_w1_v, cmp_w2_v,
              w_br_nsa, w_br_dil, w_out, final_g):
    h = x
    for layer in range(DEPTH):
        xn = rmsnorm(h, norm_g[layer])
        h = h + hybrid_layer(xn, w_in[layer], cmp_pos_k[layer], cmp_w1_k[layer], cmp_w2_k[layer],
                             cmp_pos_v[layer], cmp_w1_v[layer], cmp_w2_v[layer],
                             w_br_nsa[layer], w_br_dil[layer], w_out[layer])
    return rmsnorm(h, final_g)


_drawn_inputs = setup_inputs


def setup_inputs(seed=0):
    import zlib

    import numpy as np

    out = dict(_drawn_inputs(seed))
    spreads = {}
    factors = {'norm_g': 3.587, 'cmp_pos_k': 8.0, 'cmp_w1_k': 3.6, 'cmp_w2_k': 3.553, 'cmp_pos_v': 5.347}
    for name, (base, spread) in spreads.items():
        noise = np.random.default_rng([zlib.crc32(name.encode()), seed]).standard_normal(out[name].shape)
        drawn = base * np.exp(spread * noise) if base else spread * noise
        out[name] = __import__('jax').numpy.asarray(drawn.astype(out[name].dtype))
    for name, factor in factors.items():
        out[name] = (out[name] * factor).astype(out[name].dtype)
    return out
```

```python
import concourse.bass as bass
from concourse import mybir
from contextlib import ExitStack

P = 128
D = 1024
T = 1024
NT = T // P
KT = D // P
DH = 64
NH = 8
NG = 2
HPG = NH // NG
CMP_BLOCK, CMP_STRIDE = 32, 16
NCMP = (T - CMP_BLOCK) // CMP_STRIDE + 1
CP = 64
WIN_TILES = 512 // P
AUG = 20
VW = 66
VL = VW + DH
NTILE = 24
NEG = -1.0e38
FLOOR = -1.0e37
EPS = 1e-6

C_Q, C_KCMP, C_VCMP, C_KSLC, C_VSLC, C_KWIN, C_VWIN = 0, 512, 640, 768, 896, 1024, 1152
C_GATE, C_ZN, C_DQ, C_DK, C_DV, C_ZD, C_MG = 1280, 1304, 1816, 2328, 2840, 3352, 3864
NGATE = 3 * NH

U_KSLC, U_KWIN, U_Q, U_DQ, U_DK = 0, 1, 2, 6, 10
NUNIT = 14


def program(nc, x, norm_g, w_in, pos_k, w1_k, w2_k, pos_v, w1_v, w2_v, w_br_nsa, w_br_dil, w_out, final_g,
            ident_in, masks_in, kaug_in, kaug_cmp_in, qaug_in, out):
    f32, r32, b16 = mybir.dt.float32, mybir.dt.float32r, mybir.dt.bfloat16
    ALU, ACT, AX = mybir.AluOpType, mybir.ActivationFunctionType, mybir.AxisListType

    w_in_v = w_in[0].rearrange("(k p) c -> p k c", p=P)
    x_v = x[0].rearrange("(n p) d -> n p d", p=P)
    out_v = out[0].rearrange("(n p) d -> n p d", p=P)

    qk_hi = nc.dram_tensor("qk_hi", (NUNIT, P, T), f32, kind="Internal").ap()
    qk_lo = nc.dram_tensor("qk_lo", (NUNIT, P, T), f32, kind="Internal").ap()
    v_dil = nc.dram_tensor("v_dil", (T, NH, VL), f32, kind="Internal").ap()
    o_dil = nc.dram_tensor("o_dil", (3, T, NH, VW), f32, kind="Internal").ap()

    top = ExitStack()
    with top:
        def sbuf(ctx, name, shape, dt=f32):
            return ctx.enter_context(nc.sbuf_tensor(name, shape, dt))

        def sem(ctx, name):
            return ctx.enter_context(nc.semaphore(name))

        ps = top.enter_context(nc.psum_tensor("ps", [P, 4, 1024], f32))
        psb = ps[:, :, :].rearrange("p s (b c) -> p (s b) c", c=512)

        ident = sbuf(top, "ident", [P, P])
        identb = sbuf(top, "identb", [P, P], b16)
        masks = sbuf(top, "masks", [P, 4 * P + NT * CP], b16)
        m_diag, m_win, m_prev, m_phase = (masks[:, i * P:(i + 1) * P] for i in range(4))
        m_cmp = masks[:, 4 * P:]
        o_nsa = sbuf(top, "o_nsa", [P, NT, NH * DH])
        xh = sbuf(top, "xh", [P, KT, T], r32)
        xl = sbuf(top, "xl", [P, KT, T], r32)

        scope_v = ExitStack()
        v_nsa = sbuf(scope_v, "v_nsa", [P, NT, 2, NG, VL], r32)
        gates = sbuf(scope_v, "gates", [P, NT, 3, NH])
        kc = sbuf(scope_v, "kc", [P, NG, 2, CP], r32)
        vc = sbuf(scope_v, "vc", [P, NG, 2, 2 * VW], r32)
        scope = ExitStack()
        NRAW = 3
        raw = [sbuf(scope, f"raw{i}", [P, KT * P]) for i in range(NRAW)]
        wth = [sbuf(scope, f"wth{i}", [P, KT, P], r32) for i in range(2)]
        wtl = [sbuf(scope, f"wtl{i}", [P, KT, P], r32) for i in range(2)]
        wnh = sbuf(scope, "wnh", [P, KT, 512], r32)
        wnl = sbuf(scope, "wnl", [P, KT, 512], r32)
        evh = [sbuf(scope, f"evh{i}", [P, T], r32) for i in range(2)]
        evl = [sbuf(scope, f"evl{i}", [P, T], r32) for i in range(2)]
        src = sbuf(scope, "src", [P, 2, T])
        srcb = sbuf(scope, "srcb", [P, CMP_BLOCK, CP])
        w1bd = o_nsa[:, :, :].rearrange("p n (a e) -> p (n a) e", e=P)
        w2bd = sbuf(scope, "w2bd", [P, 2, P])
        posT = sbuf(scope, "posT", [P, 2, CMP_BLOCK])
        hid = sbuf(scope, "hid", [P, 2, CP])
        cth = sbuf(scope, "cth", [P, CP], r32)
        ctl = sbuf(scope, "ctl", [P, CP], r32)
        gb = sbuf(scope, "gb", [P, D])
        xt = [srcb[:, 0:16, :].rearrange("p a b -> p (a b)"), srcb[:, 16:32, :].rearrange("p a b -> p (a b)")]
        xn = [src[:, 0, :], src[:, 1, :]]
        mraw = w1bd[:, 0:8, :].rearrange("p a b -> p (a b)")
        junk = w1bd[:, 8:16, :].rearrange("p a b -> p (a b)")
        stat = sbuf(scope, "stat", [P, 4, NT])

        TU = [(C_KCMP, "src0"), (C_VCMP, "src1"), (C_KSLC, U_KSLC), (C_KWIN, U_KWIN)]
        TU += [(C_Q + P * i, U_Q + i) for i in range(4)]
        TD = [(C_DQ + P * i, U_DQ + i) for i in range(4)] + [(C_DK + P * i, U_DK + i) for i in range(4)]
        NN = (C_VSLC, 128), (C_VWIN, 128 + NGATE)
        PLAN = [("t",) + u for u in TU[0:4]] + [("c", 0)] + [("t",) + TU[4]] + [("c", 1)] + [("t",) + TU[5]]
        PLAN += [("c", 2)] + [("t",) + TU[6]] + [("c", 3)] + [("t",) + TU[7]] + [("n", 0)]
        PLAN += [("t",) + u for u in TD] + [("n", 1)]
        NPIECE = {"t": 1, "n": 4, "c": 0}
        NUSE = {"t": 1, "n": NT, "c": 1}
        piece0, use0, tun, spill, a, b, c, d = [], [], [], [], 0, NT, 0, 0
        for step in PLAN:
            piece0.append(a)
            use0.append(b)
            tun.append(c)
            spill.append(d)
            a += NPIECE[step[0]]
            b += NUSE[step[0]]
            c += step[0] == "t"
            d += (step[0] == "t" and not isinstance(step[2], str)) or (step[0] == "n" and step[1] == 1) * NT

        def nwidth(which):
            return 256 + NGATE if which == 0 else 512

        s_const = sem(scope, "s_const")
        s_aug = sem(scope, "s_aug")
        s_x = [sem(scope, f"s_x{i}") for i in range(2)]
        s_raw = [sem(scope, f"s_raw{i}") for i in range(NRAW)]
        s_w1 = sem(scope, "s_w1")
        s_cst = sem(scope, "s_cst")
        s_sq, s_ms, s_rt, s_ri, s_xs, s_xn = (sem(scope, n) for n in ("s_sq", "s_ms", "s_rt", "s_ri", "s_xs", "s_xn"))
        s_zero = sem(scope, "s_zero")
        s_blk = sem(scope, "s_blk")
        s_whi, s_wlo = sem(scope, "s_whi"), sem(scope, "s_wlo")
        s_mm = sem(scope, "s_mm")
        s_hi, s_lo = sem(scope, "s_hi"), sem(scope, "s_lo")
        s_sp = [sem(scope, f"s_sp{i}") for i in range(2)]
        s_kc = sem(scope, "s_kc")
        s_pos = sem(scope, "s_pos")

        block = nc.Block()
        with block:
            def words(ap):
                return ap.bitcast(f32)

            def pieces(i):
                step = PLAN[i]
                if step[0] == "t":
                    yield w_in_v[:, :, step[1]:step[1] + P], 0
                elif step[0] == "n":
                    for q in range(4):
                        yield step[1], q

            @block.sync
            def _(sp):
                sp.dma_start(ident[:, :], ident_in).then_inc(s_const, 16)
                sp.dma_start(mraw, masks_in).then_inc(s_const, 16)
                sp.dma_start(gb[:, :], norm_g[0:1, :].partition_broadcast(P)).then_inc(s_const, 16)
                for n in range(NT):
                    if n >= 2:
                        sp.wait_ge(s_xn, n - 1)
                    sp.dma_start(xt[n % 2], x_v[n]).then_inc(s_x[n % 2], 16)
                for i, pos in enumerate((pos_k, pos_v)):
                    for g in range(NG):
                        with nc.allow_non_contiguous_dma(reason="positions, transposed, once"):
                            sp.dma_start(posT[g * DH:(g + 1) * DH, i, :], pos[0].rearrange("l d -> d l")).then_inc(s_pos, 16)
                p = 0
                for i, step in enumerate(PLAN):
                    for view, q in pieces(i):
                        if p >= NRAW:
                            sp.wait_ge(s_wlo, p - NRAW + 1)
                        if step[0] == "t":
                            sp.dma_start(raw[p % NRAW][:, :].rearrange("p (k c) -> p k c", k=KT), view).then_inc(s_raw[p % NRAW], 16)
                        elif step[1] == 1:
                            sp.dma_start(raw[p % NRAW][:, :].rearrange("p (k c) -> p k c", k=2),
                                         w_in_v[:, 2 * q:2 * q + 2, C_DV:C_DV + 512]).then_inc(s_raw[p % NRAW], 16)
                        else:
                            dst = raw[p % NRAW][:, 0:2 * nwidth(0)].rearrange("p (k c) -> p k c", k=2)
                            sp.dma_start(dst[:, :, 0:P], w_in_v[:, 2 * q:2 * q + 2, C_VSLC:C_VSLC + P]).then_inc(s_raw[p % NRAW], 16)
                            sp.dma_start(dst[:, :, P:], w_in_v[:, 2 * q:2 * q + 2, C_VWIN:C_VWIN + P + NGATE]).then_inc(s_raw[p % NRAW], 16)
                        p += 1

            def raw_count(p):
                count = 0
                for i, step in enumerate(PLAN):
                    for q in range(NPIECE[step[0]]):
                        if (piece0[i] + q) % NRAW == p % NRAW:
                            count += 32 if step == ("n", 0) else 16
                        if piece0[i] + q == p:
                            return count

            def halves(i, buf_t, buf_n, q):
                step = PLAN[i]
                p = piece0[i] + q
                if step[0] == "t":
                    return raw[p % NRAW][:, :], buf_t[tun[i] % 2][:, :, :].rearrange("p k c -> p (k c)")
                w = nwidth(step[1])
                return raw[p % NRAW][:, 0:2 * w].rearrange("p (k c) -> p k c", k=2), buf_n[:, 2 * q:2 * q + 2, 0:w]

            @block.gpsimd
            def _(pool):
                pool.dma_start(kc[DH:DH + AUG, 0, 1, :], kaug_cmp_in).then_inc(s_aug, 16)
                pool.dma_start(kc[DH:DH + AUG, 1, 1, :], kaug_cmp_in).then_inc(s_aug, 16)
                pool.memset(v_nsa[:, :, :, :, DH:VW].bitcast(f32), 1.0).then_inc(s_zero, 1)
                pool.memset(vc[:, :, :, :].bitcast(f32), 0.0).then_inc(s_zero, 1)
                pool.memset(w2bd[:, :, :], 0.0).then_inc(s_zero, 1)
                pool.wait_ge(s_zero, 3)
                for h in range(2):
                    for g in range(NG):
                        pool.memset(vc[h * DH:(h + 1) * DH, g, 0, h * VW + DH:(h + 1) * VW].bitcast(f32), 1.0).then_inc(s_zero, 1)
                for i, w2 in enumerate((w2_k, w2_v)):
                    for g in range(NG):
                        pool.dma_start(w2bd[g * DH:(g + 1) * DH, i, g * DH:(g + 1) * DH], w2[0]).then_inc(s_w1, 16)
                pool.wait_ge(s_xn, NT)
                pool.wait_ge(s_cst, 2)
                pool.wait_ge(s_zero, 7)
                pool.memset(w1bd[:, :, :], 0.0).then_inc(s_zero, 1)
                pool.wait_ge(s_zero, 8)
                for g in range(NG):
                    pool.dma_start(w1bd[g * DH:(g + 1) * DH, :, g * DH:(g + 1) * DH],
                                   w1_k[0].rearrange("l d e -> d l e")).then_inc(s_w1, 16)
                ns = 0
                for i, step in enumerate(PLAN):
                    if step[0] == "t" and not isinstance(step[2], str):
                        pool.wait_ge(s_lo, use0[i] + 1)
                        pool.dma_start(qk_hi[step[2]], words(evh[ns % 2][:, :])).then_inc(s_sp[ns % 2], 16)
                        pool.dma_start(qk_lo[step[2]], words(evl[ns % 2][:, :])).then_inc(s_sp[ns % 2], 16)
                        ns += 1
                    if step == ("n", 1):
                        for n in range(NT):
                            pool.wait_ge(s_lo, use0[i] + n + 1)
                            pool.dma_start(v_dil[n * P:(n + 1) * P, :, 0:DH],
                                           words(evh[ns % 2][:, 0:512]).rearrange("p (h d) -> p h d", d=DH)).then_inc(s_sp[ns % 2], 16)
                            pool.dma_start(v_dil[n * P:(n + 1) * P, :, VW:VL],
                                           words(evl[ns % 2][:, 0:512]).rearrange("p (h d) -> p h d", d=DH)).then_inc(s_sp[ns % 2], 16)
                            ns += 1
                    if step == ("c", 0):
                        pool.wait_ge(s_mm, use0[i] + 1)
                        for g in range(NG):
                            pool.dma_start(w1bd[g * DH:(g + 1) * DH, :, g * DH:(g + 1) * DH],
                                           w1_v[0].rearrange("l d e -> d l e")).then_inc(s_w1, 16)
                    if step == ("c", 1):
                        pool.wait_ge(s_lo, use0[i] + 1)
                        for g in range(NG):
                            for r in range(2):
                                pool.dma_start(words(kc[r * DH:(r + 1) * DH, g, 0, :]), words(cth[g * DH:(g + 1) * DH, :])).then_inc(s_kc, 16)
                            pool.dma_start(words(kc[0:DH, g, 1, :]), words(ctl[g * DH:(g + 1) * DH, :])).then_inc(s_kc, 16)
                    if step == ("c", 3):
                        pool.wait_ge(s_lo, use0[i] + 1)
                        pool.wait_ge(s_kc, 96)
                        for g in range(NG):
                            for part in range(2):
                                pool.dma_start(words(vc[DH:P, g, part, VW:VW + DH]), words(vc[0:DH, g, part, 0:DH])).then_inc(s_kc, 16)
                for n in range(NT):
                    pool.dma_start(v_dil[n * P:(n + 1) * P, :, DH:VW],
                                   words(v_nsa[:, 0:4, :, :, DH:VW]).rearrange("p n a b c -> p (n a b) c")[:, 0:NH, :]).then_inc(s_kc, 16)
                pool.wait_ge(s_sp[0], 16 * ns)
                pool.wait_ge(s_sp[1], 16 * ns)
                pool.wait_ge(s_kc, 96 + 64 + 16 * NT)
                pool.wait_ge(s_aug, 32)

            @block.scalar
            def _(act):
                act.wait_ge(s_const, 16 * 3)
                nc.scalar.activation(identb[:, :], ident[:, :], ACT.Copy).then_inc(s_cst, 1)
                nc.scalar.activation(masks[:, :], mraw, ACT.Copy).then_inc(s_cst, 1)

                def sumsq(n):
                    act.wait_ge(s_x[n % 2], 16 * (n // 2 + 1))
                    if n:
                        act.wait_ge(s_sq, n)
                    nc.scalar.activation(junk, xt[n % 2], ACT.Square, accum_out=stat[:, 0, n:n + 1]).then_inc(s_sq, 1)
                    act.wait_ge(s_ms, n + 1)
                    nc.scalar.activation(stat[:, 2, n:n + 1], stat[:, 1, n:n + 1], ACT.Sqrt).then_inc(s_rt, 1)

                for n in range(NT + 1):
                    if n < NT:
                        sumsq(n)
                    if n:
                        act.wait_ge(s_mm, n)
                        nc.scalar.activation(xh[:, :, (n - 1) * P:n * P], ps[:, (n - 1) % 4, :].rearrange("p (k t) -> p k t", k=KT),
                                             ACT.Copy).then_inc(s_hi, 1)

                def split(i):
                    step = PLAN[i]
                    for q in range(NPIECE[step[0]]):
                        p = piece0[i] + q
                        act.wait_ge(s_raw[p % NRAW], raw_count(p))
                        if step[0] == "t" and tun[i] >= 2:
                            before = max(j for j in range(i) if PLAN[j][0] == "t" and tun[j] == tun[i] - 2)
                            act.wait_ge(s_mm, use0[before] + 1)
                        if step == ("n", 1):
                            act.wait_ge(s_mm, use0[PLAN.index(("n", 0))] + NT)
                        s, h = halves(i, wth, wnh, q)
                        nc.scalar.activation(h, s, ACT.Copy).then_inc(s_whi, 1)

                def evict(i):
                    step = PLAN[i]
                    if step[0] == "t" and not isinstance(step[2], str):
                        scaled = step[2] in range(U_Q, U_Q + 4) or step[2] in range(U_DQ, U_DQ + 4)
                        u, e = use0[i], spill[i]
                        act.wait_ge(s_mm, u + 1)
                        if e >= 2:
                            act.wait_ge(s_sp[e % 2], 32 * (e // 2))
                        nc.scalar.activation(evh[e % 2][:, :], ps[:, u % 4, :], ACT.Copy,
                                             scale=DH ** -0.5 if scaled else 1.0).then_inc(s_hi, 1)
                    elif step[0] == "t":
                        act.wait_ge(s_mm, use0[i] + 1)
                        nc.scalar.activation(src[:, int(step[2][3]), :], ps[:, use0[i] % 4, :], ACT.Copy).then_inc(s_hi, 1)
                    elif step[0] == "n":
                        for n in range(NT):
                            u = use0[i] + n
                            act.wait_ge(s_mm, u + 1)
                            if step[1] == 0:
                                nc.scalar.activation(gates[:, n, :, :].rearrange("p a h -> p (a h)"), ps[:, u % 4, 256:256 + NGATE], ACT.Sigmoid)
                                nc.scalar.activation(v_nsa[:, n, :, :, 0:DH].rearrange("p a g d -> p (a g) d"),
                                                     ps[:, u % 4, 0:256].rearrange("p (a d) -> p a d", d=DH), ACT.Copy).then_inc(s_hi, 1)
                            else:
                                e = spill[i] + n
                                act.wait_ge(s_sp[e % 2], 32 * (e // 2))
                                nc.scalar.activation(evh[e % 2][:, 0:512], ps[:, u % 4, 0:512], ACT.Copy).then_inc(s_hi, 1)
                    else:
                        u, c = use0[i], step[1]
                        act.wait_ge(s_mm, u + 1)
                        if c % 2 == 0:
                            nc.scalar.activation(hid[:, c // 2, :], ps[:, u % 4, 0:CP], ACT.Gelu_apprx_tanh).then_inc(s_hi, 1)
                        elif c == 1:
                            nc.scalar.activation(cth[:, :], ps[:, u % 4, 0:CP], ACT.Copy).then_inc(s_hi, 1)
                        else:
                            act.wait_ge(s_zero, 7)
                            nc.scalar.activation(vc[0:DH, :, 0, 0:DH], ps[0:DH, u % 4, 0:P].rearrange("p (g d) -> p g d", g=NG),
                                                 ACT.Copy).then_inc(s_hi, 1)

                split(0)
                for i in range(len(PLAN)):
                    if i + 1 < len(PLAN) and PLAN[i + 1][0] != "c":
                        split(i + 1)
                    evict(i)

            @block.vector
            def _(dve):
                dve.wait_ge(s_const, 16 * 3)

                for n in range(NT + 1):
                    if n < NT:
                        dve.wait_ge(s_sq, n + 1)
                        nc.vector.tensor_scalar(stat[:, 1, n:n + 1], stat[:, 0, n:n + 1], 1.0 / D, EPS, ALU.mult, ALU.add).then_inc(s_ms, 1)
                        dve.wait_ge(s_rt, n + 1)
                        nc.vector.reciprocal(stat[:, 3, n:n + 1], stat[:, 2, n:n + 1]).then_inc(s_ri, 1)
                        dve.wait_ge(s_ri, n + 1)
                        if n >= 2:
                            dve.wait_ge(s_mm, n - 1)
                        nc.vector.scalar_tensor_tensor(xn[n % 2], xt[n % 2], stat[:, 3, n:n + 1], gb[:, :], ALU.mult, ALU.mult).then_inc(s_xn, 1)
                    if n:
                        dve.wait_ge(s_hi, n)
                        nc.vector.tensor_tensor(xl[:, :, (n - 1) * P:n * P], ps[:, (n - 1) % 4, :].rearrange("p (k t) -> p k t", k=KT),
                                                xh[:, :, (n - 1) * P:n * P].bitcast(f32), ALU.subtract).then_inc(s_lo, 1)

                def split(i):
                    for q in range(NPIECE[PLAN[i][0]]):
                        p = piece0[i] + q
                        dve.wait_ge(s_whi, p + 1)
                        s, h = halves(i, wth, wnh, q)
                        _, l = halves(i, wtl, wnl, q)
                        nc.vector.tensor_tensor(l, s, h.bitcast(f32), ALU.subtract).then_inc(s_wlo, 1)

                def evict(i):
                    step = PLAN[i]
                    if step[0] == "t" and not isinstance(step[2], str):
                        scaled = step[2] in range(U_Q, U_Q + 4) or step[2] in range(U_DQ, U_DQ + 4)
                        u, e = use0[i], spill[i]
                        dve.wait_ge(s_hi, u + 1)
                        nc.vector.scalar_tensor_tensor(evl[e % 2][:, :], ps[:, u % 4, :], DH ** -0.5 if scaled else 1.0,
                                                       evh[e % 2][:, :].bitcast(f32), ALU.mult, ALU.subtract).then_inc(s_lo, 1)
                    elif step[0] == "t":
                        dve.wait_ge(s_hi, use0[i] + 1)
                        dve.wait_ge(s_lo, use0[i])
                        dve.sem_inc(s_lo, 1)
                    elif step[0] == "n":
                        for n in range(NT):
                            u = use0[i] + n
                            dve.wait_ge(s_hi, u + 1)
                            if step[1] == 0:
                                nc.vector.tensor_tensor(v_nsa[:, n, :, :, VW:VL].rearrange("p a g d -> p (a g) d"),
                                                        ps[:, u % 4, 0:256].rearrange("p (a d) -> p a d", d=DH),
                                                        v_nsa[:, n, :, :, 0:DH].bitcast(f32).rearrange("p a g d -> p (a g) d"),
                                                        ALU.subtract).then_inc(s_lo, 1)
                            else:
                                e = spill[i] + n
                                nc.vector.tensor_tensor(evl[e % 2][:, 0:512], ps[:, u % 4, 0:512],
                                                        evh[e % 2][:, 0:512].bitcast(f32), ALU.subtract).then_inc(s_lo, 1)
                    else:
                        u, c = use0[i], step[1]
                        dve.wait_ge(s_hi, u + 1)
                        if c % 2 == 0:
                            dve.wait_ge(s_lo, u)
                            dve.sem_inc(s_lo, 1)
                        elif c == 1:
                            nc.vector.tensor_tensor(ctl[:, :], ps[:, u % 4, 0:CP], cth[:, :].bitcast(f32), ALU.subtract).then_inc(s_lo, 1)
                        else:
                            nc.vector.tensor_tensor(vc[0:DH, :, 1, 0:DH], ps[0:DH, u % 4, 0:P].rearrange("p (g d) -> p g d", g=NG),
                                                    vc[0:DH, :, 0, 0:DH].bitcast(f32), ALU.subtract).then_inc(s_lo, 1)

                def blocks(c):
                    if c == 1:
                        dve.wait_ge(s_mm, use0[PLAN.index(("c", 0))] + 1)
                    if c == 0:
                        dve.wait_ge(s_pos, 64)
                        dve.wait_ge(s_hi, use0[1] + 1)
                    a = src[:, c, :].rearrange("p (n s) -> p s n", s=CMP_STRIDE)
                    for r in range(2):
                        nc.vector.tensor_tensor(srcb[:, r * CMP_STRIDE:(r + 1) * CMP_STRIDE, 0:NCMP], a[:, :, r:r + NCMP],
                                                posT[:, c, r * CMP_STRIDE:(r + 1) * CMP_STRIDE].unsqueeze(2).to_broadcast([P, CMP_STRIDE, NCMP]),
                                                ALU.add).then_inc(s_blk, 1)

                split(0)
                for i in range(len(PLAN)):
                    if i + 1 < len(PLAN) and PLAN[i + 1][0] != "c":
                        split(i + 1)
                    if i == 1:
                        nc.vector.memset(srcb[:, :, NCMP:CP], 0.0).then_inc(s_blk, 1)
                        blocks(0)
                    evict(i)
                    if PLAN[i] == ("c", 0):
                        blocks(1)

            @block.tensor
            def _(pe):
                pe.wait_ge(s_const, 16 * 3)

                def slot_free(u):
                    if u >= 4:
                        pe.wait_ge(s_lo, u - 3)

                for n in range(NT):
                    slot_free(n)
                    pe.wait_ge(s_xn, n + 1)
                    for k in range(KT):
                        last = nc.tensor.transpose(ps[:, n % 4, k * P:(k + 1) * P], xn[n % 2][:, k * P:(k + 1) * P], ident[:, :])
                    last.then_inc(s_mm, 1)
                pe.wait_ge(s_lo, NT)
                for i, step in enumerate(PLAN):
                    if step[0] == "t":
                        u, w = use0[i], tun[i] % 2
                        slot_free(u)
                        pe.wait_ge(s_wlo, piece0[i] + 1)
                        for half in range(2):
                            cols = slice(half * 512, half * 512 + 512)
                            for k in range(KT):
                                nc.tensor.matmul(ps[:, u % 4, cols], wth[w][:, k, :], xh[:, k, cols], start=(k == 0), stop=False)
                                nc.tensor.matmul(ps[:, u % 4, cols], wth[w][:, k, :], xl[:, k, cols], start=False, stop=False)
                                last = nc.tensor.matmul(ps[:, u % 4, cols], wtl[w][:, k, :], xh[:, k, cols], start=False, stop=(k == KT - 1))
                        last.then_inc(s_mm, 1)
                    elif step[0] == "n":
                        pe.wait_ge(s_wlo, piece0[i] + 4)
                        w = nwidth(step[1])
                        for n in range(NT):
                            u = use0[i] + n
                            slot_free(u)
                            rows = slice(n * P, n * P + P)
                            for k in range(KT):
                                nc.tensor.matmul(ps[:, u % 4, 0:w], xh[:, k, rows], wnh[:, k, 0:w], start=(k == 0), stop=False)
                                nc.tensor.matmul(ps[:, u % 4, 0:w], xh[:, k, rows], wnl[:, k, 0:w], start=False, stop=False)
                                last = nc.tensor.matmul(ps[:, u % 4, 0:w], xl[:, k, rows], wnh[:, k, 0:w], start=False, stop=(k == KT - 1))
                            last.then_inc(s_mm, 1)
                    else:
                        u, c = use0[i], step[1]
                        slot_free(u)
                        if c % 2 == 0:
                            pe.wait_ge(s_w1, 16 * 6 + 32 * (c // 2))
                            pe.wait_ge(s_blk, 3 + c)
                            for l in range(CMP_BLOCK):
                                last = nc.tensor.matmul(ps[:, u % 4, 0:CP], w1bd[:, l, :], srcb[:, l, :], start=(l == 0), stop=(l == CMP_BLOCK - 1))
                        else:
                            pe.wait_ge(s_hi, use0[i - 2] + 1)
                            if c == 1:
                                last = nc.tensor.matmul(ps[:, u % 4, 0:CP], w2bd[:, 0, :], hid[:, 0, :], start=True, stop=True)
                            else:
                                last = nc.tensor.matmul(ps[0:CP, u % 4, 0:P], hid[:, 1, :], w2bd[:, 1, :], start=True, stop=True)
                        last.then_inc(s_mm, 1)
        scope.close()

        def attention(kind, tag):
            scope = ExitStack()
            qa = [sbuf(scope, f"{tag}_qa{i}", [P, T], r32) for i in range(2)]
            qb = [sbuf(scope, f"{tag}_qb{i}", [P, T], r32) for i in range(2)]
            nk = 4 if kind == "nsa" else 2
            ka = [sbuf(scope, f"{tag}_ka{i}", [P, T], r32) for i in range(nk)]
            kb = [sbuf(scope, f"{tag}_kb{i}", [P, T], r32) for i in range(nk)]
            if kind == "dil":
                vd = [sbuf(scope, f"{tag}_v{i}", [P, 3, NT, VL], r32) for i in range(2)]
            NPT = 3
            prob = [sbuf(scope, f"{tag}_prob{i}", [P, 1024]) for i in range(2)]
            pth = [sbuf(scope, f"{tag}_pth{i}", [P, 512], r32) for i in range(NPT)]
            ptl = [sbuf(scope, f"{tag}_ptl{i}", [P, 512], r32) for i in range(NPT)]
            if kind == "nsa":
                oraw = [sbuf(scope, f"{tag}_oraw{i}", [P, NTILE, 1, VW]) for i in range(2)]
                coef = [sbuf(scope, f"{tag}_coef{i}", [P, NT, 3]) for i in range(2)]
                term = [sbuf(scope, f"{tag}_term{i}", [P, NT, DH]) for i in range(2)]
            else:
                oraw = [sbuf(scope, f"{tag}_oraw{i}", [P, NTILE, 2, VW]) for i in range(2)]
            negm = sbuf(scope, f"{tag}_negm", [P, 2, NTILE])
            s_load = [sem(scope, f"{tag}_load{i}") for i in range(2)]
            s_aug = [sem(scope, f"{tag}_aug{i}") for i in range(2)]
            s_k, s_kaug = sem(scope, f"{tag}_k"), sem(scope, f"{tag}_kaug")
            s_s, s_max, s_sub, s_exp = (sem(scope, f"{tag}_{n}") for n in ("s", "max", "sub", "exp"))
            s_t, s_hi, s_lo, s_pv, s_ev = (sem(scope, f"{tag}_{n}") for n in ("t", "hi", "lo", "pv", "ev"))
            s_floor, s_rec, s_mst, s_post, s_od = (sem(scope, f"{tag}_{n}") for n in ("floor", "rec", "mst", "post", "od"))

            S = [ps[:, 0, :], ps[:, 1, :]]
            TP = [psb[:, 4, :], psb[:, 5, :]]
            OP = [psb[:, 6, :], psb[:, 7, :]]

            jobs, groups = [], []
            for h in range(NH):
                b = h % 2
                if kind == "nsa":
                    g = h // HPG
                    for n in range(NT):
                        gr = len(groups)
                        for br in range(2):
                            first = 0 if br == 0 else max(0, n - WIN_TILES)
                            kk = 2 * g + br
                            tile = dict(q=[x_[b][:, n * P:(n + 1) * P] for x_ in (qa, qb)],
                                        k=[x_[kk][:, first * P:(n + 1) * P] for x_ in (ka, kb)],
                                        mask=[((n - first) * P, m_diag)] + ([(0, m_win)] if br and n >= WIN_TILES else []),
                                        v=[v_nsa[:, m, br, g, :] for m in range(first, n + 1)])
                            jobs.append(dict(h=h, w=(n + 1 - first) * P, n=1, tiles=[tile], mode="bias", og=gr,
                                             oat=br, t0=2 * n + br))
                        groups.append(dict(h=h, n=2, t0=2 * n, last=len(jobs) - 1))
                    for half in range(2):
                        tiles = [dict(q=[x_[b][:, n * P:(n + 1) * P] for x_ in (qa, qb)],
                                      k=[kc[:, g, 0, :], kc[0:DH + AUG, g, 1, :]], mask=[(0, m_cmp[:, n * CP:(n + 1) * CP])],
                                      v=None) for n in range(4 * half, 4 * half + 4)]
                        jobs.append(dict(h=h, w=CP, n=4, tiles=tiles, mode="sub", og=len(groups), oat=0, t0=16 + 4 * half, cmp=g))
                        groups.append(dict(h=h, n=4, t0=16 + 4 * half, last=len(jobs) - 1))
                else:
                    def near(n):
                        return dict(q=[x_[b][:, n * P:(n + 1) * P] for x_ in (qa, qb)],
                                    k=[x_[b][:, max(n - 1, 0) * P:(n + 1) * P] for x_ in (ka, kb)],
                                    mask=[(0, m_diag)] if n == 0 else [(0, m_prev), (P, m_diag)],
                                    v=[vd[b][:, 0, m, :] for m in range(max(n - 1, 0), n + 1)])

                    def four(i, p):
                        return dict(q=[x_[b][:, :].rearrange("p (l r) -> p r l", r=4)[:, p, i * P:(i + 1) * P] for x_ in (qa, qb)],
                                    k=[x_[b][:, :].rearrange("p (l r) -> p r l", r=4)[:, p, 0:(i + 1) * P] for x_ in (ka, kb)],
                                    mask=[(0, m_diag)] if i == 0 else [(0, m_prev), (P, m_diag)],
                                    v=[vd[b][:, 1, 4 * m + p, :] for m in range(i + 1)])

                    def sixteen(j):
                        return dict(q=[x_[b][:, :].rearrange("p (l r) -> p r l", r=NT)[:, j, :] for x_ in (qa, qb)],
                                    k=[x_[b][:, :].rearrange("p (l r) -> p r l", r=NT)[:, j, :] for x_ in (ka, kb)],
                                    mask=[(0, m_phase)], v=[vd[b][:, 2, j, :]])

                    for tiles, w, mode in (([near(n) for n in range(1, 5)], 256, "bias"), ([near(n) for n in range(5, 8)], 256, "bias"),
                                           ([four(1, p) for p in range(4)], 256, "bias"),
                                           ([four(0, p) for p in range(4)] + [near(0)], 128, "sub"),
                                           ([sixteen(j) for j in range(4)], 128, "sub"), ([sixteen(j) for j in range(4, 8)], 128, "sub")):
                        t0 = sum(j["n"] for j in jobs if j["h"] == h)
                        jobs.append(dict(h=h, w=w, n=len(tiles), tiles=tiles, mode=mode, og=len(groups), oat=0, t0=t0))
                        groups.append(dict(h=h, n=len(tiles), t0=t0, last=len(jobs) - 1))
            NJ = len(jobs)
            chunk0, nsub = [], []
            c = s = 0
            for j in jobs:
                chunk0.append(c)
                nsub.append(s)
                c += -(-j["w"] * j["n"] // 512)
                s += j["mode"] == "sub"
            chunk0.append(c)
            head_first = [next(i for i, j in enumerate(jobs) if j["h"] == h) for h in range(NH)]
            head_last = [max(i for i, j in enumerate(jobs) if j["h"] == h) for h in range(NH)]
            n_load = 3 if kind == "nsa" else 10

            def chunks(j):
                cols = jobs[j]["w"] * jobs[j]["n"]
                return [(chunk0[j] + i, 512 * i, min(512, cols - 512 * i)) for i in range(chunk0[j + 1] - chunk0[j])]

            block = nc.Block()
            with block:
                @block.sync
                def _(sp):
                    if kind == "nsa":
                        for g in range(NG):
                            for br in range(2):
                                kk, rows = 2 * g + br, slice(g * DH, (g + 1) * DH)
                                sp.dma_start(ka[kk][0:DH, :].bitcast(f32), qk_hi[U_KSLC + br, rows, :]).then_inc(s_k, 16)
                                sp.dma_start(ka[kk][DH:P, :].bitcast(f32), qk_hi[U_KSLC + br, rows, :]).then_inc(s_k, 16)
                                sp.dma_start(kb[kk][0:DH, :].bitcast(f32), qk_lo[U_KSLC + br, rows, :]).then_inc(s_k, 16)
                    for h in range(NH):
                        b = h % 2
                        if h >= 2:
                            sp.wait_ge(s_pv, head_last[h - 2] + 1)
                        rows = slice(b * DH, (b + 1) * DH)
                        u = (U_Q if kind == "nsa" else U_DQ) + h // 2
                        sp.dma_start(qa[b][0:DH, :].bitcast(f32), qk_hi[u, rows, :]).then_inc(s_load[b], 16)
                        sp.dma_start(qb[b][0:DH, :].bitcast(f32), qk_hi[u, rows, :]).then_inc(s_load[b], 16)
                        sp.dma_start(qa[b][DH:P, :].bitcast(f32), qk_lo[u, rows, :]).then_inc(s_load[b], 16)
                        if kind == "dil":
                            u = U_DK + h // 2
                            sp.dma_start(ka[b][0:DH, :].bitcast(f32), qk_hi[u, rows, :]).then_inc(s_load[b], 16)
                            sp.dma_start(ka[b][DH:P, :].bitcast(f32), qk_hi[u, rows, :]).then_inc(s_load[b], 16)
                            sp.dma_start(kb[b][0:DH, :].bitcast(f32), qk_lo[u, rows, :]).then_inc(s_load[b], 16)
                            sp.dma_start(vd[b][:, 0, :, :].bitcast(f32), v_dil[:, h, :].rearrange("(n p) c -> p n c", p=P)).then_inc(s_load[b], 16)
                            for i in range(2):
                                sp.dma_start(vd[b][:, 1, 4 * i:4 * i + 4, :].bitcast(f32),
                                             v_dil[512 * i:512 * i + 512, h, :].rearrange("(l r) c -> l r c", r=4)).then_inc(s_load[b], 16)
                            sp.dma_start(vd[b][:, 2, :, :].bitcast(f32), v_dil[:, h, :].rearrange("(l j) c -> l j c", j=NT)).then_inc(s_load[b], 16)

                def post(pool, h):
                    if kind == "nsa":
                        o, co, te, b = oraw[h % 2], coef[h % 2], term, h % 2
                        heads = slice(h * DH, (h + 1) * DH)
                        pool.wait_ge(s_rec, h + 1)
                        if h:
                            pool.wait_ge(s_post, 7 * h)
                        gate = gates[:, :, :, h].rearrange("p n a -> p a n")
                        cf = co[:, :, :]
                        nc.gpsimd.tensor_tensor(cf[:, :, 0:2], cf[:, :, 0:2], gates[:, :, 1:3, h], ALU.mult).then_inc(s_post, 1)
                        nc.gpsimd.tensor_tensor(cf[:, :, 2], cf[:, :, 2], gates[:, :, 0, h], ALU.mult).then_inc(s_post, 1)
                        pool.wait_ge(s_post, 7 * h + 2)
                        r = [o[:, 0:16, 0, 0:DH].rearrange("p (n a) d -> p n a d", a=2)[:, :, i, :] for i in range(2)] + [o[:, 16:24, 0, 0:DH]]
                        for i in range(3):
                            dst = o_nsa[:, :, heads] if i == 0 else te[i - 1][:, :, :]
                            nc.gpsimd.tensor_tensor(dst, r[i], cf[:, :, i].unsqueeze(2).to_broadcast([P, NT, DH]), ALU.mult).then_inc(s_post, 1)
                        for i in range(2):
                            pool.wait_ge(s_post, 7 * h + 5 + i)
                            nc.gpsimd.tensor_tensor(o_nsa[:, :, heads], o_nsa[:, :, heads], te[i][:, :, :], ALU.add).then_inc(s_post, 1)
                    elif h % 2 == 1:
                        pair = slice(h - 1, h + 1)
                        pool.wait_ge(s_mst, h + 1)
                        o = oraw[h // 2 % 2]
                        od = o_dil[:, :, pair, :]
                        pool.dma_start(od[0, P:T].rearrange("(n p) a c -> p n (a c)", p=P), o[:, 0:7, :, :].rearrange("p n a c -> p n (a c)")).then_inc(s_od, 16)
                        pool.dma_start(od[0, 0:P].rearrange("p a c -> p (a c)"), o[:, 15, :, :].rearrange("p a c -> p (a c)")).then_inc(s_od, 16)
                        for i in range(2):
                            t0 = 7 if i == 1 else 11
                            pool.dma_start(od[1, 512 * i:512 * i + 512].rearrange("(l r) a c -> l r (a c)", r=4),
                                           o[:, t0:t0 + 4, :, :].rearrange("p n a c -> p n (a c)")).then_inc(s_od, 16)
                        pool.dma_start(od[2].rearrange("(l j) a c -> l j (a c)", j=NT),
                                       o[:, 16:24, :, :].rearrange("p n a c -> p n (a c)")).then_inc(s_od, 16)

                @block.gpsimd
                def _(pool):
                    for i in range(nk):
                        pool.dma_start(kb[i][DH:DH + AUG, :], kaug_in).then_inc(s_kaug, 16)
                    for h in range(NH):
                        b = h % 2
                        if h >= 2:
                            pool.wait_ge(s_pv, head_last[h - 2] + 1)
                        pool.dma_start(qb[b][DH:DH + AUG, :], qaug_in[(0 if kind == "nsa" else NH) + h]).then_inc(s_aug[b], 16)
                        if h:
                            post(pool, h - 1)
                    post(pool, NH - 1)
                    if kind == "dil":
                        pool.wait_ge(s_od, 5 * 16 * (NH // 2))

                @block.tensor
                def _(pe):
                    def scores(j):
                        job = jobs[j]
                        if j == head_first[job["h"]]:
                            if job["h"] == 0:
                                pe.wait_ge(s_kaug, 16 * nk)
                                if kind == "nsa":
                                    pe.wait_ge(s_k, 16 * 12)
                            pe.wait_ge(s_load[job["h"] % 2], 16 * n_load * (job["h"] // 2 + 1))
                            pe.wait_ge(s_aug[job["h"] % 2], 16 * (job["h"] // 2 + 1))
                        if j >= 2:
                            pe.wait_ge(s_exp, j - 1)
                        for i, t in enumerate(job["tiles"]):
                            at = i * job["w"]
                            k0 = 0
                            while k0 < job["w"]:
                                kn = min(512, job["w"] - k0)
                                dst = S[j % 2][:, at + k0:at + k0 + kn]
                                ms = [(mc - k0, m) for mc, m in t["mask"] if k0 <= mc < k0 + kn]
                                for part, hi in ((0, P), (1, DH + AUG)):
                                    kk = t["k"][part][0:hi]
                                    kk = kk if len(kk.shape) > 2 else kk[:, k0:k0 + kn]
                                    last = nc.tensor.matmul(dst, t["q"][part][0:hi], kk, start=(part == 0),
                                                            stop=(part == 1 and not ms))
                                for x_, (mc, m) in enumerate(ms):
                                    last = nc.tensor.matmul(S[j % 2][:, at + k0 + mc:at + k0 + mc + m.shape[1]], identb[:, :], m,
                                                            start=False, stop=(x_ == len(ms) - 1))
                                k0 += kn
                        last.then_inc(s_s, 1)

                    def transposes(j):
                        pe.wait_ge(s_exp, j + 1)
                        for c, at, w in chunks(j):
                            if c >= 2:
                                pe.wait_ge(s_lo, c - 1)
                            for i in range(w // P):
                                last = nc.tensor.transpose(TP[c % 2][:, i * P:(i + 1) * P], prob[j % 2][:, at + i * P:at + (i + 1) * P], ident[:, :])
                            last.then_inc(s_t, 1)

                    def values(j):
                        job = jobs[j]
                        if job["og"] >= 2 and job["oat"] == 0:
                            pe.wait_ge(s_ev, job["og"] - 1)
                        o = OP[job["og"] % 2]
                        for c, at, w in chunks(j):
                            pe.wait_ge(s_lo, c + 1)
                            for i in range(w // P):
                                hi, lo = pth[c % NPT][:, i * P:(i + 1) * P], ptl[c % NPT][:, i * P:(i + 1) * P]
                                if "cmp" in job:
                                    dst = o[:, i * 2 * VW:(i + 1) * 2 * VW]
                                    v = vc[:, job["cmp"], :, :]
                                    nc.tensor.matmul(dst, hi, v[:, 0, :], start=True, stop=False)
                                    nc.tensor.matmul(dst, hi, v[:, 1, :], start=False, stop=False)
                                    last = nc.tensor.matmul(dst, lo, v[:, 0, :], start=False, stop=True)
                                    continue
                                t, m = divmod(at + i * P, job["w"])
                                v = job["tiles"][t]["v"]
                                m //= P
                                dst = o[:, (t + job["oat"]) * VW:(t + job["oat"] + 1) * VW]
                                nc.tensor.matmul(dst, hi, v[m][:, 0:VW], start=(m == 0), stop=False)
                                nc.tensor.matmul(dst[:, 0:DH], hi, v[m][:, VW:VL], start=False, stop=False)
                                last = nc.tensor.matmul(dst, lo, v[m][:, 0:VW], start=False, stop=(m == len(v) - 1))
                        last.then_inc(s_pv, 1)

                    scores(0)
                    for j in range(NJ + 1):
                        if j:
                            transposes(j - 1)
                        if j + 1 < NJ:
                            scores(j + 1)
                        if j:
                            values(j - 1)

                @block.scalar
                def _(act):
                    def exps(j):
                        job = jobs[j]
                        b, t0 = job["h"] % 2, job["t0"]
                        if job["mode"] == "sub":
                            act.wait_ge(s_sub, nsub[j] + 1)
                            cols = job["w"] * job["n"]
                            nc.scalar.activation(prob[j % 2][:, 0:cols], prob[j % 2][:, 0:cols], ACT.Exp).then_inc(s_exp, 1)
                            return
                        act.wait_ge(s_max, j + 1)
                        if j >= 2:
                            act.wait_ge(s_t, chunk0[j - 1])
                        for i in range(job["n"]):
                            cols = slice(i * job["w"], (i + 1) * job["w"])
                            last = nc.scalar.activation(prob[j % 2][:, cols], S[j % 2][:, cols], ACT.Exp, bias=negm[:, b, t0 + i:t0 + i + 1])
                        last.then_inc(s_exp, 1)

                    def hi_part(j):
                        for c, at, w in chunks(j):
                            act.wait_ge(s_t, c + 1)
                            if c >= NPT:
                                act.wait_ge(s_pv, max(i for i in range(NJ) if chunk0[i] <= c - NPT) + 1)
                            nc.scalar.activation(pth[c % NPT][:, 0:w], TP[c % 2][:, 0:w], ACT.Copy).then_inc(s_hi, 1)

                    def take(gr):
                        g = groups[gr]
                        h = g["h"]
                        act.wait_ge(s_pv, g["last"] + 1)
                        first = gr == 0 or groups[gr - 1]["h"] != h
                        if kind == "nsa":
                            if first and h >= 2:
                                act.wait_ge(s_post, 7 * (h - 1))
                            dst = oraw[h % 2][:, g["t0"]:g["t0"] + g["n"], 0, :]
                        else:
                            if first and h >= 4 and h % 2 == 0:
                                act.wait_ge(s_od, 5 * 16 * (h // 2 - 1))
                            dst = oraw[h // 2 % 2][:, g["t0"]:g["t0"] + g["n"], h % 2, :]
                        nc.scalar.activation(dst, OP[gr % 2][:, 0:g["n"] * VW].rearrange("p (n c) -> p n c", c=VW), ACT.Copy).then_inc(s_ev, 1)

                    done = 0
                    for j in range(NJ + 2):
                        if 1 <= j <= NJ:
                            hi_part(j - 1)
                        if j < NJ:
                            exps(j)
                        while done < len(groups) and groups[done]["last"] <= j - 2:
                            take(done)
                            done += 1
                    while done < len(groups):
                        take(done)
                        done += 1

                @block.vector
                def _(dve):
                    def nfloor(j):
                        return sum(1 for i in range(j + 1) if "cmp" in jobs[i])

                    def maxima(j):
                        job = jobs[j]
                        b, t0, n, w = job["h"] % 2, job["t0"], job["n"], job["w"]
                        dve.wait_ge(s_s, j + 1)
                        if j == head_first[job["h"]] and kind == "dil" and job["h"] >= 2:
                            dve.wait_ge(s_mst, job["h"] - 1)
                        m = negm[:, b, t0:t0 + n]
                        s = S[j % 2][:, 0:n * w].rearrange("p (n w) -> p n w", n=n)
                        if j == head_first[job["h"]] and job["h"] >= 2:
                            dve.wait_ge(s_exp, head_last[job["h"] - 2] + 1)
                        nc.vector.tensor_reduce(m, s, AX.X, ALU.max, negate=True).then_inc(s_max, 1)
                        if job["mode"] == "sub":
                            dve.wait_ge(s_max, j + 1)
                            if "cmp" in job:
                                nc.vector.tensor_scalar(m, m, -FLOOR, None, ALU.min).then_inc(s_floor, 1)
                                dve.wait_ge(s_floor, nfloor(j))
                            if j >= 2:
                                dve.wait_ge(s_t, chunk0[j - 1])
                            nc.vector.tensor_tensor(prob[j % 2][:, 0:n * w].rearrange("p (n w) -> p n w", n=n), s,
                                                    m.unsqueeze(2).to_broadcast([P, n, w]), ALU.add).then_inc(s_sub, 1)

                    def lo_part(j):
                        for c, at, w in chunks(j):
                            dve.wait_ge(s_hi, c + 1)
                            nc.vector.tensor_tensor(ptl[c % NPT][:, 0:w], TP[c % 2][:, 0:w], pth[c % NPT][:, 0:w].bitcast(f32),
                                                    ALU.subtract).then_inc(s_lo, 1)

                    def finish(h):
                        last_group = max(i for i, g in enumerate(groups) if g["h"] == h)
                        dve.wait_ge(s_ev, last_group + 1)
                        if kind == "nsa":
                            o, cf = oraw[h % 2], coef[h % 2]
                            if h >= 2:
                                dve.wait_ge(s_post, 7 * (h - 1))
                            nc.vector.tensor_scalar(cf[:, :, 0:2], o[:, 0:16, 0, DH].rearrange("p (n a) -> p n a", a=2), 1e-30, None, ALU.max).then_inc(s_mst, 1)
                            nc.vector.tensor_scalar(cf[:, :, 2], o[:, 16:24, 0, DH], 1e-30, None, ALU.max).then_inc(s_mst, 1)
                            dve.wait_ge(s_mst, 2 * (h + 1))
                            nc.vector.reciprocal(cf[:, :, :], cf[:, :, :]).then_inc(s_rec, 1)
                        else:
                            nc.vector.tensor_copy(oraw[h // 2 % 2][:, :, h % 2, DH + 1], negm[:, h % 2, :]).then_inc(s_mst, 1)

                    fin = 0
                    for j in range(NJ + 2):
                        if j < NJ:
                            maxima(j)
                        if 1 <= j <= NJ:
                            lo_part(j - 1)
                        if fin < NH and j >= head_last[fin] + 4:
                            finish(fin)
                            fin += 1
                    while fin < NH:
                        finish(fin)
                        fin += 1
            scope.close()

        attention("nsa", "a")
        scope_v.close()
        attention("dil", "d")

        scope_g = ExitStack()
        gh = sbuf(scope_g, "gh", [P, 2 * NH // 2, T], r32)
        gl = sbuf(scope_g, "gl", [P, 2 * NH // 2, T], r32)
        scope = ExitStack()
        NRAW2 = 2
        raw = [sbuf(scope, f"z_raw{i}", [P, KT, P]) for i in range(NRAW2)]
        wth = [sbuf(scope, f"z_wth{i}", [P, KT, P], r32) for i in range(2)]
        wtl = [sbuf(scope, f"z_wtl{i}", [P, KT, P], r32) for i in range(2)]
        zs = sbuf(scope, "zs", [P, T])
        gf = sbuf(scope, "gf", [P, T])
        o_d = sbuf(scope, "o_d", [P, NT, NH * DH])
        parts = sbuf(scope, "parts", [P, 3, NH, VW])
        small = sbuf(scope, "small", [P, 4, 3 * NH])
        s_raw = [sem(scope, f"z_raw{i}") for i in range(NRAW2)]
        s_whi, s_wlo, s_mm, s_tr, s_zs, s_gf, s_gh, s_gl = (sem(scope, f"z_{n}") for n in ("whi", "wlo", "mm", "tr", "zs", "gf", "gh", "gl"))
        s_part, s_c, s_e, s_r, s_od = (sem(scope, f"z_{n}") for n in ("part", "c", "e", "r", "od"))
        NZ = NH
        z_cols = [C_ZN + P * i for i in range(4)] + [C_ZD + P * i for i in range(4)]
        block = nc.Block()
        with block:
            @block.sync
            def _(sp):
                for i, col in enumerate(z_cols):
                    if i >= NRAW2:
                        sp.wait_ge(s_wlo, i - NRAW2 + 1)
                    sp.dma_start(raw[i % NRAW2][:, :, :], w_in_v[:, :, col:col + P]).then_inc(s_raw[i % NRAW2], 16)

            @block.gpsimd
            def _(pool):
                def combine(n):
                    if n:
                        pool.wait_ge(s_od, 3 * n)
                    pool.dma_start(parts[:, :, :, :].rearrange("p b h c -> p b (h c)"),
                                   o_dil[:, n * P:(n + 1) * P, :, :].rearrange("b p h c -> p b (h c)")).then_inc(s_part, 16)
                    pool.wait_ge(s_c, 6 * (n + 1))
                    v = parts[:, :, :, 0:DH].rearrange("p b h d -> p (b h) d")
                    w = small[:, 1, :].unsqueeze(2).to_broadcast([P, 3 * NH, DH])
                    nc.gpsimd.tensor_tensor(v, v, w, ALU.mult).then_inc(s_od, 1)
                    pool.wait_ge(s_od, 3 * n + 1)
                    dst = o_d[:, n, :].rearrange("p (h d) -> p h d", d=DH)
                    nc.gpsimd.tensor_tensor(dst, parts[:, 0, :, 0:DH], parts[:, 1, :, 0:DH], ALU.add).then_inc(s_od, 1)
                    pool.wait_ge(s_od, 3 * n + 2)
                    nc.gpsimd.tensor_tensor(dst, dst, parts[:, 2, :, 0:DH], ALU.add).then_inc(s_od, 1)

                for i in range(NZ):
                    if i < 4:
                        combine(2 * i)
                        combine(2 * i + 1)
                    pool.wait_ge(s_gh, i + 1)
                    nc.gpsimd.tensor_tensor(gl[:, i, :], gf[:, :], gh[:, i, :].bitcast(f32), ALU.subtract).then_inc(s_gl, 1)

            @block.scalar
            def _(act):
                def split(i):
                    act.wait_ge(s_raw[i % NRAW2], 16 * (i // NRAW2 + 1))
                    if i >= 2:
                        act.wait_ge(s_mm, i - 1)
                    nc.scalar.activation(wth[i % 2][:, :, :], raw[i % NRAW2][:, :, :], ACT.Copy).then_inc(s_whi, 1)

                split(0)
                for i in range(NZ):
                    if i + 1 < NZ:
                        split(i + 1)
                    if i < 4:
                        for n in (2 * i, 2 * i + 1):
                            act.wait_ge(s_c, 6 * n + 3)
                            nc.scalar.activation(small[:, 1, :], small[:, 0, :], ACT.Exp).then_inc(s_e, 1)
                    act.wait_ge(s_mm, i + 1)
                    if i:
                        act.wait_ge(s_gf, i)
                    nc.scalar.activation(zs[:, :], ps[:, i % 2, :], ACT.Silu).then_inc(s_zs, 1)
                    act.wait_ge(s_gf, i + 1)
                    nc.scalar.activation(gh[:, i, :], gf[:, :], ACT.Copy).then_inc(s_gh, 1)

            @block.vector
            def _(dve):
                def split(i):
                    dve.wait_ge(s_whi, i + 1)
                    nc.vector.tensor_tensor(wtl[i % 2][:, :, :], raw[i % NRAW2][:, :, :], wth[i % 2][:, :, :].bitcast(f32), ALU.subtract).then_inc(s_wlo, 1)

                def weights(n):
                    dve.wait_ge(s_part, 16 * (n + 1))
                    if n:
                        dve.wait_ge(s_od, 3 * n)
                    nm = parts[:, :, :, DH + 1]
                    sm = [small[:, k, :] for k in range(4)]
                    b3 = [k.rearrange("p (b h) -> p b h", b=3) for k in sm]
                    nc.vector.tensor_tensor(sm[2][:, 0:NH], nm[:, 0, :], nm[:, 1, :], ALU.min).then_inc(s_c, 1)
                    dve.wait_ge(s_c, 6 * n + 1)
                    nc.vector.tensor_tensor(sm[2][:, NH:2 * NH], sm[2][:, 0:NH], nm[:, 2, :], ALU.min).then_inc(s_c, 1)
                    dve.wait_ge(s_c, 6 * n + 2)
                    nc.vector.tensor_tensor(b3[0], sm[2][:, NH:2 * NH].unsqueeze(1).to_broadcast([P, 3, NH]), nm, ALU.subtract).then_inc(s_c, 1)
                    dve.wait_ge(s_e, n + 1)
                    nc.vector.tensor_tensor(b3[3], b3[1], parts[:, :, :, DH], ALU.mult).then_inc(s_c, 1)
                    dve.wait_ge(s_c, 6 * n + 4)
                    nc.vector.tensor_reduce(sm[2][:, 0:NH], sm[3].rearrange("p (b h) -> p h b", b=3), AX.X, ALU.add).then_inc(s_c, 1)
                    dve.wait_ge(s_c, 6 * n + 5)
                    nc.vector.reciprocal(sm[2][:, NH:2 * NH], sm[2][:, 0:NH]).then_inc(s_r, 1)
                    dve.wait_ge(s_r, n + 1)
                    nc.vector.tensor_tensor(b3[1], b3[1], sm[2][:, NH:2 * NH].unsqueeze(1).to_broadcast([P, 3, NH]), ALU.mult).then_inc(s_c, 1)

                split(0)
                for i in range(NZ):
                    if i + 1 < NZ:
                        split(i + 1)
                    if i < 4:
                        weights(2 * i)
                        weights(2 * i + 1)
                    dve.wait_ge(s_zs, i + 1)
                    dve.wait_ge(s_tr, i + 1)
                    if i:
                        dve.wait_ge(s_gl, i)
                    nc.vector.tensor_tensor(gf[:, :], ps[:, 2 + i % 2, :], zs[:, :], ALU.mult).then_inc(s_gf, 1)

            @block.tensor
            def _(pe):
                for i in range(NZ):
                    pe.wait_ge(s_wlo, i + 1)
                    if i >= 2:
                        pe.wait_ge(s_zs, i - 1)
                    for half in range(2):
                        cols = slice(half * 512, half * 512 + 512)
                        for k in range(KT):
                            nc.tensor.matmul(ps[:, i % 2, cols], wth[i % 2][:, k, :], xh[:, k, cols], start=(k == 0), stop=False)
                            nc.tensor.matmul(ps[:, i % 2, cols], wth[i % 2][:, k, :], xl[:, k, cols], start=False, stop=False)
                            last = nc.tensor.matmul(ps[:, i % 2, cols], wtl[i % 2][:, k, :], xh[:, k, cols], start=False, stop=(k == KT - 1))
                    last.then_inc(s_mm, 1)
                    if i >= 2:
                        pe.wait_ge(s_gf, i - 1)
                    if i == 4:
                        pe.wait_ge(s_od, 3 * NT)
                    o = o_nsa if i < 4 else o_d
                    for n in range(NT):
                        last = nc.tensor.transpose(ps[:, 2 + i % 2, n * P:(n + 1) * P], o[:, n, (i % 4) * P:(i % 4 + 1) * P], ident[:, :])
                    last.then_inc(s_tr, 1)
        scope.close()

        merged = sbuf(scope_g, "merged", [P, KT, T])
        scope = ExitStack()
        raw = [sbuf(scope, f"m_raw{i}", [P, KT, P]) for i in range(3)]
        wth = [sbuf(scope, f"m_wth{i}", [P, KT, P], r32) for i in range(2)]
        wtl = [sbuf(scope, f"m_wtl{i}", [P, KT, P], r32) for i in range(2)]
        sg = [o_nsa[:, 2 * i:2 * i + 2, :].rearrange("p a b -> p (a b)") for i in range(2)]
        s_raw = [sem(scope, f"m_raw{i}") for i in range(3)]
        s_whi, s_wlo, s_mm, s_sg, s_y, s_mrg = (sem(scope, f"m_{n}") for n in ("whi", "wlo", "mm", "sg", "y", "mrg"))
        NPC = 3 * KT
        br_v = [w[0].rearrange("(k p) c -> p k c", p=P) for w in (w_br_nsa, w_br_dil)]
        block = nc.Block()
        with block:
            @block.sync
            def _(sp):
                for i in range(NPC):
                    m, part = divmod(i, 3)
                    if i >= 3:
                        sp.wait_ge(s_wlo, i - 2)
                    if part < 2:
                        col = C_MG + part * D + m * P
                        sp.dma_start(raw[i % 3][:, :, :], w_in_v[:, :, col:col + P]).then_inc(s_raw[i % 3], 16)
                    else:
                        for b in range(2):
                            sp.dma_start(raw[i % 3][:, 4 * b:4 * b + 4, :], br_v[b][:, :, m * P:(m + 1) * P]).then_inc(s_raw[i % 3], 16)

            @block.gpsimd
            def _(pool):
                for m in range(KT):
                    pool.wait_ge(s_y, 2 * (m + 1))
                    nc.gpsimd.tensor_tensor(merged[:, m, :], sg[0], sg[1], ALU.add).then_inc(s_mrg, 1)

            @block.scalar
            def _(act):
                def split(i):
                    m, part = divmod(i, 3)
                    act.wait_ge(s_raw[i % 3], 16 * (m + 1) * (2 if part == 2 else 1))
                    if i >= 2:
                        mm, pp = divmod(i - 2, 3)
                        act.wait_ge(s_mm, 4 * mm + (1, 2, 4)[pp])
                    nc.scalar.activation(wth[i % 2][:, :, :], raw[i % 3][:, :, :], ACT.Copy).then_inc(s_whi, 1)

                split(0)
                for i in range(NPC):
                    m, part = divmod(i, 3)
                    if i + 1 < NPC:
                        split(i + 1)
                    if part < 2:
                        act.wait_ge(s_mm, 4 * m + part + 1)
                        if m:
                            act.wait_ge(s_mrg, m)
                        nc.scalar.activation(sg[part], ps[:, part, :], ACT.Sigmoid).then_inc(s_sg, 1)

            @block.vector
            def _(dve):
                def split(i):
                    dve.wait_ge(s_whi, i + 1)
                    nc.vector.tensor_tensor(wtl[i % 2][:, :, :], raw[i % 3][:, :, :], wth[i % 2][:, :, :].bitcast(f32), ALU.subtract).then_inc(s_wlo, 1)

                split(0)
                for i in range(NPC):
                    m, part = divmod(i, 3)
                    if i + 1 < NPC:
                        split(i + 1)
                    if part == 2:
                        for b in range(2):
                            dve.wait_ge(s_sg, 2 * m + b + 1)
                            dve.wait_ge(s_mm, 4 * m + 3 + b)
                            nc.vector.tensor_tensor(sg[b], ps[:, 2 + b, :], sg[b], ALU.mult).then_inc(s_y, 1)

            @block.tensor
            def _(pe):
                def product(slot, w, ks, right_h, right_l):
                    for half in range(2):
                        cols = slice(half * 512, half * 512 + 512)
                        for k in ks:
                            nc.tensor.matmul(ps[:, slot, cols], wth[w][:, k, :], right_h[:, k, cols], start=(k == ks[0]), stop=False)
                            nc.tensor.matmul(ps[:, slot, cols], wth[w][:, k, :], right_l[:, k, cols], start=False, stop=False)
                            last = nc.tensor.matmul(ps[:, slot, cols], wtl[w][:, k, :], right_h[:, k, cols], start=False, stop=(k == ks[-1]))
                    last.then_inc(s_mm, 1)

                for i in range(NPC):
                    m, part = divmod(i, 3)
                    pe.wait_ge(s_wlo, i + 1)
                    if part < 2:
                        if m:
                            pe.wait_ge(s_sg, 2 * (m - 1) + part + 1)
                        product(part, i % 2, range(KT), xh, xl)
                    else:
                        for b in range(2):
                            if m:
                                pe.wait_ge(s_y, 2 * (m - 1) + b + 1)
                            product(2 + b, i % 2, range(4 * b, 4 * b + 4), gh, gl)
        scope.close()

        scope = ExitStack()
        raw = [sbuf(scope, f"f_raw{i}", [P, D]) for i in range(3)]
        res = [sbuf(scope, f"res{i}", [P, D]) for i in range(2)]
        ot = [sbuf(scope, f"ot{i}", [P, D]) for i in range(2)]
        fstat = sbuf(scope, "fstat", [P, 4, NT])
        s_raw = [sem(scope, f"f_raw{i}") for i in range(3)]
        s_res = [sem(scope, f"f_res{i}") for i in range(2)]
        s_st = [sem(scope, f"f_st{i}") for i in range(2)]
        s_fg, s_whi, s_wlo, s_mh, s_ml, s_mm, s_h, s_sq, s_ms, s_rt, s_ri, s_fin = (sem(scope, f"f_{n}") for n in (
            "fg", "whi", "wlo", "mh", "ml", "mm", "h", "sq", "ms", "rt", "ri", "fin"))
        woh, wol = xh, xl
        mhs = [gh[:, i, :].rearrange("p (k t) -> p k t", k=KT) for i in range(2)]
        mls = [gl[:, i, :].rearrange("p (k t) -> p k t", k=KT) for i in range(2)]
        fgb = o_nsa[:, 0:2, :].rearrange("p a b -> p (a b)")
        junk = o_nsa[:, 2:4, :].rearrange("p a b -> p (a b)")
        wo_v = w_out[0].rearrange("(k p) e -> p k e", p=P)
        block = nc.Block()
        with block:
            @block.sync
            def _(sp):
                for k in range(KT):
                    if k >= 3:
                        sp.wait_ge(s_wlo, k - 2)
                    sp.dma_start(raw[k % 3][:, :], wo_v[:, k, :]).then_inc(s_raw[k % 3], 16)
                sp.dma_start(fgb, final_g.rearrange("(a d) -> a d", a=1).partition_broadcast(P)).then_inc(s_fg, 16)
                for n in range(NT):
                    if n >= 2:
                        sp.wait_ge(s_fin, n - 1)
                    sp.dma_start(res[n % 2][:, :], x_v[n]).then_inc(s_res[n % 2], 16)
                    if n >= 1:
                        sp.wait_ge(s_fin, n)
                        sp.dma_start(out_v[n - 1], ot[(n - 1) % 2][:, :]).then_inc(s_st[(n - 1) % 2], 16)
                sp.wait_ge(s_fin, NT)
                sp.dma_start(out_v[NT - 1], ot[(NT - 1) % 2][:, :]).then_inc(s_st[(NT - 1) % 2], 16)
                for i in range(2):
                    sp.wait_ge(s_st[i], 16 * NT // 2)

            @block.scalar
            def _(act):
                def msplit(n):
                    if n >= 2:
                        act.wait_ge(s_mm, n - 1)
                    nc.scalar.activation(mhs[n % 2], merged[:, :, n * P:(n + 1) * P], ACT.Copy).then_inc(s_mh, 1)

                msplit(0)
                for k in range(KT):
                    act.wait_ge(s_raw[k % 3], 16 * (k // 3 + 1))
                    nc.scalar.activation(woh[:, k, :], raw[k % 3][:, :], ACT.Copy).then_inc(s_whi, 1)
                for n in range(NT):
                    if n + 1 < NT:
                        msplit(n + 1)
                    act.wait_ge(s_h, n + 1)
                    if n:
                        act.wait_ge(s_sq, n)
                    nc.scalar.activation(junk, ot[n % 2][:, :], ACT.Square, accum_out=fstat[:, 0, n:n + 1]).then_inc(s_sq, 1)
                    act.wait_ge(s_ms, n + 1)
                    nc.scalar.activation(fstat[:, 2, n:n + 1], fstat[:, 1, n:n + 1], ACT.Sqrt).then_inc(s_rt, 1)

            @block.vector
            def _(dve):
                def msplit(n):
                    dve.wait_ge(s_mh, n + 1)
                    nc.vector.tensor_tensor(mls[n % 2], merged[:, :, n * P:(n + 1) * P], mhs[n % 2].bitcast(f32), ALU.subtract).then_inc(s_ml, 1)

                msplit(0)
                for k in range(KT):
                    dve.wait_ge(s_whi, k + 1)
                    nc.vector.tensor_tensor(wol[:, k, :], raw[k % 3][:, :], woh[:, k, :].bitcast(f32), ALU.subtract).then_inc(s_wlo, 1)
                dve.wait_ge(s_fg, 16)
                for n in range(NT):
                    if n + 1 < NT:
                        msplit(n + 1)
                    dve.wait_ge(s_mm, n + 1)
                    dve.wait_ge(s_res[n % 2], 16 * (n // 2 + 1))
                    if n >= 2:
                        dve.wait_ge(s_st[n % 2], 16 * (n // 2))
                    nc.vector.tensor_tensor(ot[n % 2][:, :], ps[:, n % 4, :], res[n % 2][:, :], ALU.add).then_inc(s_h, 1)
                    dve.wait_ge(s_sq, n + 1)
                    nc.vector.tensor_scalar(fstat[:, 1, n:n + 1], fstat[:, 0, n:n + 1], 1.0 / D, EPS, ALU.mult, ALU.add).then_inc(s_ms, 1)
                    dve.wait_ge(s_rt, n + 1)
                    nc.vector.reciprocal(fstat[:, 3, n:n + 1], fstat[:, 2, n:n + 1]).then_inc(s_ri, 1)
                    dve.wait_ge(s_ri, n + 1)
                    nc.vector.scalar_tensor_tensor(ot[n % 2][:, :], ot[n % 2][:, :], fstat[:, 3, n:n + 1], fgb, ALU.mult, ALU.mult).then_inc(s_fin, 1)

            @block.tensor
            def _(pe):
                for n in range(NT):
                    pe.wait_ge(s_ml, n + 1)
                    if n >= 4:
                        pe.wait_ge(s_h, n - 3)
                    for k in range(KT):
                        if n == 0:
                            pe.wait_ge(s_wlo, k + 1)
                        for half in range(2):
                            cols = slice(half * 512, half * 512 + 512)
                            nc.tensor.matmul(ps[:, n % 4, cols], mhs[n % 2][:, k, :], woh[:, k, cols], start=(k == 0), stop=False)
                            nc.tensor.matmul(ps[:, n % 4, cols], mhs[n % 2][:, k, :], wol[:, k, cols], start=False, stop=False)
                            last = nc.tensor.matmul(ps[:, n % 4, cols], mls[n % 2][:, k, :], woh[:, k, cols], start=False, stop=(k == KT - 1))
                    last.then_inc(s_mm, 1)
        scope.close()
        scope_g.close()


_INS = ['x', 'norm_g', 'w_in', 'cmp_pos_k', 'cmp_w1_k', 'cmp_w2_k', 'cmp_pos_v', 'cmp_w1_v', 'cmp_w2_v',
        'w_br_nsa', 'w_br_dil', 'w_out', 'final_g']


def constants():
    import numpy as np
    q, k = np.arange(P)[:, None], np.arange(P)[None, :]
    diag = np.where(k > q, NEG, 0.0)
    win = np.where(k <= q, NEG, 0.0)
    prev = np.where(k < q, NEG, 0.0)
    phase = np.where((k % 2 == q % 2) & (k <= q), 0.0, NEG)
    t = np.arange(T).reshape(NT, P)
    c = np.arange(CP)
    end = c * CMP_STRIDE + CMP_BLOCK - 1
    cmp = np.where((end[None, None] <= t[:, :, None]) & (c < NCMP)[None, None], 0.0, NEG)
    masks = np.concatenate([diag, win, prev, phase, cmp.transpose(1, 0, 2).reshape(P, NT * CP)], axis=1).astype(np.float32)

    def keys(at):
        local, tile = at % P, at // P
        one = (tile[None, :] == np.arange(NT)[:, None]).astype(np.float32)
        ones = np.ones((2, at.size))
        return np.concatenate([ones, np.stack([local, local]), one, one]).astype(np.float32)

    def cut(a):
        a = a.astype(np.float32)
        hi = ((a.view(np.uint32) + 0x800) & np.uint32(0xFFFFF000)).view(np.float32)
        return hi, a - hi

    n_all = 2 * NH
    s = (2.0 ** (-8.0 * np.arange(1, n_all + 1) / n_all)).astype(np.float32)
    tt = np.arange(T)
    rows = []
    for slope in np.concatenate([s[0::2], s[1::2]]):
        a, b = cut(-slope * (tt % P).astype(np.float32))
        c_, d = cut(np.full(T, slope))
        e, f = cut(-slope * (P * (tt[None, :] // P - np.arange(NT)[:, None])).astype(np.float32))
        rows.append(np.concatenate([a[None], b[None], c_[None], d[None], e, f]))
    return np.eye(P, dtype=np.float32), masks, keys(tt), keys(end), np.stack(rows).astype(np.float32)


def kernel(**inputs):
    import numpy as _np
    import concourse.bacc as _bacc
    from concourse import mybir as _mybir
    from concourse.bass_utils import run_bass_kernel_spmd as _run

    nc = _bacc.Bacc("TRN2", target_bir_lowering=False, num_devices=1)
    arrays, args = {}, []
    given = [(name, _np.ascontiguousarray(inputs[name])) for name in _INS]
    given += list(zip(("ident", "masks", "kaug", "kaug_cmp", "qaug"), constants()))
    for name, a in given:
        arrays[f"in_{name}_dram"] = a
        args.append(nc.dram_tensor(f"in_{name}_dram", a.shape, _mybir.dt.from_np(a.dtype), kind="ExternalInput").ap())
    args.append(nc.dram_tensor("out_0_dram", (1, T, D), _mybir.dt.float32, kind="ExternalOutput").ap())
    program(nc, *args)
    r = _run(nc, [arrays], core_ids=[0])
    return r.results[0]["out_0_dram"]
```

```python
import concourse.bass as bass
from concourse import mybir
from contextlib import ExitStack

P = 128
D = 1024
T = 1024
NT = T // P
KT = D // P
DH = 64
NH = 8
NG = 2
HPG = NH // NG
CMP_BLOCK, CMP_STRIDE = 32, 16
NCMP = (T - CMP_BLOCK) // CMP_STRIDE + 1
CP = 64
WIN_TILES = 512 // P
AUG = 20
MROW = 96
KBR = 3
VS = 2 * DH
LOG_DEGREE = 8
NEAR = 5
NEG = -1.0e38
FLOOR = -1.0e37
EPS = 1e-6

C_Q, C_KCMP, C_VCMP, C_KSLC, C_VSLC, C_KWIN, C_VWIN = 0, 512, 640, 768, 896, 1024, 1152
C_GATE, C_ZN, C_DQ, C_DK, C_DV, C_ZD, C_MG = 1280, 1304, 1816, 2328, 2840, 3352, 3864
NGATE = 3 * NH

U_KSLC, U_KWIN, U_Q, U_DQ, U_DK = 0, 1, 2, 6, 10
NUNIT = 14


def program(nc, x, norm_g, w_in, pos_k, w1_k, w2_k, pos_v, w1_v, w2_v, w_br_nsa, w_br_dil, w_out, final_g,
            ident_in, masks_in, kaug_in, kaug_cmp_in, qaug_in, dil_log_in, out):
    f32, r32, b16 = mybir.dt.float32, mybir.dt.float32r, mybir.dt.bfloat16
    ALU, ACT, AX = mybir.AluOpType, mybir.ActivationFunctionType, mybir.AxisListType

    import numpy as np

    LN2 = float(np.log(2.0))
    LOG_POLY = [float(c) for c in np.polynomial.chebyshev.Chebyshev.interpolate(
        lambda u: np.log(1.5 + u), LOG_DEGREE, domain=[-0.5, 0.5]).convert(kind=np.polynomial.Polynomial).coef]

    w_in_v = w_in[0].rearrange("(k p) c -> p k c", p=P)
    x_v = x[0].rearrange("(n p) d -> n p d", p=P)
    out_v = out[0].rearrange("(n p) d -> n p d", p=P)

    qk_hi = nc.dram_tensor("qk_hi", (NUNIT, P, T), f32, kind="Internal").ap()
    qk_lo = nc.dram_tensor("qk_lo", (NUNIT, P, T), f32, kind="Internal").ap()
    v_dil = nc.dram_tensor("v_dil", (T, NH, 2, DH), f32, kind="Internal").ap()

    top = ExitStack()
    with top:
        def sbuf(ctx, name, shape, dt=f32):
            return ctx.enter_context(nc.sbuf_tensor(name, shape, dt))

        def sem(ctx, name):
            return ctx.enter_context(nc.semaphore(name))

        ps = top.enter_context(nc.psum_tensor("ps", [P, 4, 1024], f32))
        psb = ps[:, :, :].rearrange("p s (b c) -> p (s b) c", c=512)

        ident = sbuf(top, "ident", [P, P])
        identb = sbuf(top, "identb", [P, P], b16)
        identr = sbuf(top, "identr", [P, P], r32)
        o_nsa = sbuf(top, "o_nsa", [P, NH // 2, T])
        xh = sbuf(top, "xh", [P, KT, T], r32)
        xl = sbuf(top, "xl", [P, KT, T], r32)

        def logarithm(dve, dst, src, tmp, least, done, base):
            a, b, c = tmp
            bits = mybir.dt.int32
            count = [base]

            def step(op, *args):
                if count[0] > base:
                    dve.wait_ge(done, count[0])
                op(*args).then_inc(done, 1)
                count[0] += 1

            step(nc.vector.tensor_scalar, a, src, least, None, ALU.max)
            step(nc.vector.tensor_scalar, b.bitcast(bits), a.bitcast(bits), 0x7FFFFF, 0x3F800000, ALU.bitwise_and, ALU.bitwise_or)
            step(nc.vector.tensor_scalar, a.bitcast(bits), a.bitcast(bits), 23, None, ALU.logical_shift_right)
            step(nc.vector.tensor_scalar, dst, a.bitcast(bits), -127.0, LN2, ALU.add, ALU.mult)
            step(nc.vector.tensor_scalar, b, b, -1.5, None, ALU.add)
            step(nc.vector.tensor_scalar, c, b, LOG_POLY[LOG_DEGREE], None, ALU.mult)
            for k in range(LOG_DEGREE - 1, 0, -1):
                step(nc.vector.scalar_tensor_tensor, c, c, LOG_POLY[k], b, ALU.add, ALU.mult)
            step(nc.vector.scalar_tensor_tensor, dst, c, LOG_POLY[0], dst, ALU.add, ALU.add)
            return count[0]

        scope_v = ExitStack()
        masks = sbuf(scope_v, "masks", [P, 4 * P + NT * CP + T], b16)
        m_diag, m_win, m_diag_t, m_win_t = (masks[:, i * P:(i + 1) * P] for i in range(4))
        m_cmp, m_cmp_t = masks[:, 4 * P:4 * P + NT * CP], masks[0:CP, 4 * P + NT * CP:]
        v_nsa = sbuf(scope_v, "v_nsa", [P, NT, 2, NG, VS], r32)
        lgate = sbuf(scope_v, "lgate", [P, NT, KBR, NH])
        kc = sbuf(scope_v, "kc", [P, NG, 2, CP], r32)
        vc = sbuf(scope_v, "vc", [CP, NG, VS], r32)
        scope = ExitStack()
        NRAW = 3
        raw = [sbuf(scope, f"raw{i}", [P, KT * P]) for i in range(NRAW)]
        wth = [sbuf(scope, f"wth{i}", [P, KT, P], r32) for i in range(2)]
        wtl = [sbuf(scope, f"wtl{i}", [P, KT, P], r32) for i in range(2)]
        wnh = sbuf(scope, "wnh", [P, KT, 512], r32)
        wnl = sbuf(scope, "wnl", [P, KT, 512], r32)
        evh = [sbuf(scope, f"evh{i}", [P, T], r32) for i in range(2)]
        evl = [sbuf(scope, f"evl{i}", [P, T], r32) for i in range(2)]
        src = sbuf(scope, "src", [P, 2, T])
        srcb = sbuf(scope, "srcb", [P, CMP_BLOCK, CP])
        w1bd = o_nsa[:, :, :].rearrange("p n (a e) -> p (n a) e", e=P)
        w2bd = sbuf(scope, "w2bd", [P, 2, P])
        posT = sbuf(scope, "posT", [P, 2, CMP_BLOCK])
        hid = sbuf(scope, "hid", [P, 2, CP])
        cth = sbuf(scope, "cth", [P, CP], r32)
        ctl = sbuf(scope, "ctl", [P, CP], r32)
        gates = sbuf(scope, "gates", [P, NT, NGATE])
        lg_tmp = [sbuf(scope, f"lg_tmp{i}", [P, NT, NGATE]) for i in range(3)]
        gel = sbuf(scope, "gel", [P, 3, CP])
        xt = [srcb[:, 0:16, :].rearrange("p a b -> p (a b)"), srcb[:, 16:32, :].rearrange("p a b -> p (a b)")]
        xn = [src[:, 0, :], src[:, 1, :]]
        gb = w1bd[:, 0:8, :].rearrange("p a b -> p (a b)")
        junk = w1bd[:, 8:16, :].rearrange("p a b -> p (a b)")
        stat = sbuf(scope, "stat", [P, 4, NT])

        TU = [(C_KCMP, "src0"), (C_VCMP, "src1"), (C_KSLC, U_KSLC), (C_KWIN, U_KWIN)]
        TU += [(C_Q + P * i, U_Q + i) for i in range(4)]
        TD = [(C_DQ + P * i, U_DQ + i) for i in range(4)] + [(C_DK + P * i, U_DK + i) for i in range(4)]
        NN = (C_VSLC, 128), (C_VWIN, 128 + NGATE)
        PLAN = [("t",) + u for u in TU[0:4]] + [("c", 0)] + [("t",) + TU[4]] + [("c", 1)] + [("t",) + TU[5]]
        PLAN += [("c", 2)] + [("t",) + TU[6]] + [("c", 3)] + [("t",) + TU[7]] + [("n", 0)]
        PLAN += [("t",) + u for u in TD] + [("n", 1)]
        NPIECE = {"t": 1, "n": 4, "c": 0}
        NUSE = {"t": 1, "n": NT, "c": 1}
        piece0, use0, tun, spill, a, b, c, d = [], [], [], [], 0, NT, 0, 0
        for step in PLAN:
            piece0.append(a)
            use0.append(b)
            tun.append(c)
            spill.append(d)
            a += NPIECE[step[0]]
            b += NUSE[step[0]]
            c += step[0] == "t"
            d += (step[0] == "t" and not isinstance(step[2], str)) or (step[0] == "n" and step[1] == 1) * NT

        def nwidth(which):
            return 256 + NGATE if which == 0 else 512

        s_const = sem(scope, "s_const")
        s_aug = sem(scope, "s_aug")
        s_x = [sem(scope, f"s_x{i}") for i in range(2)]
        s_raw = [sem(scope, f"s_raw{i}") for i in range(NRAW)]
        s_w1 = sem(scope, "s_w1")
        s_cst = sem(scope, "s_cst")
        s_sq, s_ms, s_rt, s_ri, s_xs, s_xn = (sem(scope, n) for n in ("s_sq", "s_ms", "s_rt", "s_ri", "s_xs", "s_xn"))
        s_zero = sem(scope, "s_zero")
        s_blk = sem(scope, "s_blk")
        s_whi, s_wlo = sem(scope, "s_whi"), sem(scope, "s_wlo")
        s_mm = sem(scope, "s_mm")
        s_hi, s_lo = sem(scope, "s_hi"), sem(scope, "s_lo")
        s_sp = [sem(scope, f"s_sp{i}") for i in range(2)]
        s_kc = sem(scope, "s_kc")
        s_gel, s_tanh, s_hid = sem(scope, "s_gel"), sem(scope, "s_tanh"), sem(scope, "s_hid")
        s_pos = sem(scope, "s_pos")
        s_gate, s_log = sem(scope, "s_gate"), sem(scope, "s_log")

        block = nc.Block()
        with block:
            def words(ap):
                return ap.bitcast(f32)

            def pieces(i):
                step = PLAN[i]
                if step[0] == "t":
                    yield w_in_v[:, :, step[1]:step[1] + P], 0
                elif step[0] == "n":
                    for q in range(4):
                        yield step[1], q

            @block.sync
            def _(sp):
                sp.dma_start(ident[:, :], ident_in).then_inc(s_const, 16)
                sp.dma_start(gb[:, :], norm_g[0:1, :].partition_broadcast(P)).then_inc(s_const, 16)
                for n in range(NT):
                    if n >= 2:
                        sp.wait_ge(s_xn, n - 1)
                    sp.dma_start(xt[n % 2], x_v[n]).then_inc(s_x[n % 2], 16)
                for i, pos in enumerate((pos_k, pos_v)):
                    for g in range(NG):
                        with nc.allow_non_contiguous_dma(reason="positions, transposed, once"):
                            sp.dma_start(posT[g * DH:(g + 1) * DH, i, :], pos[0].rearrange("l d -> d l")).then_inc(s_pos, 16)
                p = 0
                for i, step in enumerate(PLAN):
                    for view, q in pieces(i):
                        if p >= NRAW:
                            sp.wait_ge(s_wlo, p - NRAW + 1)
                        if step[0] == "t":
                            sp.dma_start(raw[p % NRAW][:, :].rearrange("p (k c) -> p k c", k=KT), view).then_inc(s_raw[p % NRAW], 16)
                        elif step[1] == 1:
                            sp.dma_start(raw[p % NRAW][:, :].rearrange("p (k c) -> p k c", k=2),
                                         w_in_v[:, 2 * q:2 * q + 2, C_DV:C_DV + 512]).then_inc(s_raw[p % NRAW], 16)
                        else:
                            dst = raw[p % NRAW][:, 0:2 * nwidth(0)].rearrange("p (k c) -> p k c", k=2)
                            sp.dma_start(dst[:, :, 0:P], w_in_v[:, 2 * q:2 * q + 2, C_VSLC:C_VSLC + P]).then_inc(s_raw[p % NRAW], 16)
                            sp.dma_start(dst[:, :, P:], w_in_v[:, 2 * q:2 * q + 2, C_VWIN:C_VWIN + P + NGATE]).then_inc(s_raw[p % NRAW], 16)
                        p += 1

            def raw_count(p):
                count = 0
                for i, step in enumerate(PLAN):
                    for q in range(NPIECE[step[0]]):
                        if (piece0[i] + q) % NRAW == p % NRAW:
                            count += 32 if step == ("n", 0) else 16
                        if piece0[i] + q == p:
                            return count

            def halves(i, buf_t, buf_n, q):
                step = PLAN[i]
                p = piece0[i] + q
                if step[0] == "t":
                    return raw[p % NRAW][:, :], buf_t[tun[i] % 2][:, :, :].rearrange("p k c -> p (k c)")
                w = nwidth(step[1])
                return raw[p % NRAW][:, 0:2 * w].rearrange("p (k c) -> p k c", k=2), buf_n[:, 2 * q:2 * q + 2, 0:w]

            @block.gpsimd
            def _(pool):
                pool.dma_start(masks[:, :], masks_in).then_inc(s_aug, 16)
                pool.dma_start(identr[:, :], ident_in).then_inc(s_aug, 16)
                for g in range(NG):
                    pool.dma_start(kc[DH:MROW + 2 * KBR, g, 1, :], kaug_cmp_in).then_inc(s_aug, 16)
                pool.memset(w2bd[:, :, :], 0.0).then_inc(s_zero, 1)
                pool.wait_ge(s_zero, 1)
                for i, w2 in enumerate((w2_k, w2_v)):
                    for g in range(NG):
                        pool.dma_start(w2bd[g * DH:(g + 1) * DH, i, g * DH:(g + 1) * DH], w2[0]).then_inc(s_w1, 16)
                pool.wait_ge(s_xn, NT)
                pool.memset(w1bd[:, :, :], 0.0).then_inc(s_zero, 1)
                pool.wait_ge(s_zero, 2)
                for g in range(NG):
                    pool.dma_start(w1bd[g * DH:(g + 1) * DH, :, g * DH:(g + 1) * DH],
                                   w1_k[0].rearrange("l d e -> d l e")).then_inc(s_w1, 16)
                ns = 0
                for i, step in enumerate(PLAN):
                    if step[0] == "t" and not isinstance(step[2], str):
                        pool.wait_ge(s_lo, use0[i] + 1)
                        pool.dma_start(qk_hi[step[2]], words(evh[ns % 2][:, :])).then_inc(s_sp[ns % 2], 16)
                        pool.dma_start(qk_lo[step[2]], words(evl[ns % 2][:, :])).then_inc(s_sp[ns % 2], 16)
                        ns += 1
                    if step == ("n", 1):
                        for n in range(NT):
                            pool.wait_ge(s_lo, use0[i] + n + 1)
                            pool.dma_start(v_dil[n * P:(n + 1) * P, :, 0, :],
                                           words(evh[ns % 2][:, 0:512]).rearrange("p (h d) -> p h d", d=DH)).then_inc(s_sp[ns % 2], 16)
                            pool.dma_start(v_dil[n * P:(n + 1) * P, :, 1, :],
                                           words(evl[ns % 2][:, 0:512]).rearrange("p (h d) -> p h d", d=DH)).then_inc(s_sp[ns % 2], 16)
                            ns += 1
                    if step == ("c", 0):
                        pool.wait_ge(s_mm, use0[i] + 1)
                        for g in range(NG):
                            pool.dma_start(w1bd[g * DH:(g + 1) * DH, :, g * DH:(g + 1) * DH],
                                           w1_v[0].rearrange("l d e -> d l e")).then_inc(s_w1, 16)
                    if step == ("c", 1):
                        pool.wait_ge(s_lo, use0[i] + 1)
                        for g in range(NG):
                            for r in range(2):
                                pool.dma_start(words(kc[r * DH:(r + 1) * DH, g, 0, :]), words(cth[g * DH:(g + 1) * DH, :])).then_inc(s_kc, 16)
                            pool.dma_start(words(kc[0:DH, g, 1, :]), words(ctl[g * DH:(g + 1) * DH, :])).then_inc(s_kc, 16)
                pool.wait_ge(s_sp[0], 16 * ns)
                pool.wait_ge(s_sp[1], 16 * ns)
                pool.wait_ge(s_kc, 96)
                pool.wait_ge(s_aug, 64)

            @block.scalar
            def _(act):
                act.wait_ge(s_const, 16 * 2)
                nc.scalar.activation(identb[:, :], ident[:, :], ACT.Copy).then_inc(s_cst, 1)

                def sumsq(n):
                    act.wait_ge(s_x[n % 2], 16 * (n // 2 + 1))
                    if n:
                        act.wait_ge(s_sq, n)
                    nc.scalar.activation(junk, xt[n % 2], ACT.Square, accum_out=stat[:, 0, n:n + 1]).then_inc(s_sq, 1)
                    act.wait_ge(s_ms, n + 1)
                    nc.scalar.activation(stat[:, 2, n:n + 1], stat[:, 1, n:n + 1], ACT.Sqrt).then_inc(s_rt, 1)

                for n in range(NT + 1):
                    if n < NT:
                        sumsq(n)
                    if n:
                        act.wait_ge(s_mm, n)
                        nc.scalar.activation(xh[:, :, (n - 1) * P:n * P], ps[:, (n - 1) % 4, :].rearrange("p (k t) -> p k t", k=KT),
                                             ACT.Copy).then_inc(s_hi, 1)

                def split(i):
                    step = PLAN[i]
                    for q in range(NPIECE[step[0]]):
                        p = piece0[i] + q
                        act.wait_ge(s_raw[p % NRAW], raw_count(p))
                        if step[0] == "t" and tun[i] >= 2:
                            before = max(j for j in range(i) if PLAN[j][0] == "t" and tun[j] == tun[i] - 2)
                            act.wait_ge(s_mm, use0[before] + 1)
                        if step == ("n", 1):
                            act.wait_ge(s_mm, use0[PLAN.index(("n", 0))] + NT)
                        s, h = halves(i, wth, wnh, q)
                        nc.scalar.activation(h, s, ACT.Copy).then_inc(s_whi, 1)

                def evict(i):
                    step = PLAN[i]
                    if step[0] == "t" and not isinstance(step[2], str):
                        scaled = step[2] in range(U_Q, U_Q + 4) or step[2] in range(U_DQ, U_DQ + 4)
                        u, e = use0[i], spill[i]
                        act.wait_ge(s_mm, u + 1)
                        if e >= 2:
                            act.wait_ge(s_sp[e % 2], 32 * (e // 2))
                        nc.scalar.activation(evh[e % 2][:, :], ps[:, u % 4, :], ACT.Copy,
                                             scale=DH ** -0.5 if scaled else 1.0).then_inc(s_hi, 1)
                    elif step[0] == "t":
                        act.wait_ge(s_mm, use0[i] + 1)
                        nc.scalar.activation(src[:, int(step[2][3]), :], ps[:, use0[i] % 4, :], ACT.Copy).then_inc(s_hi, 1)
                    elif step[0] == "n":
                        for n in range(NT):
                            u = use0[i] + n
                            act.wait_ge(s_mm, u + 1)
                            if step[1] == 0:
                                nc.scalar.activation(gates[:, n, 0:2 * NH], ps[:, u % 4, 256 + NH:256 + NGATE], ACT.Sigmoid).then_inc(s_gate, 1)
                                nc.scalar.activation(gates[:, n, 2 * NH:NGATE], ps[:, u % 4, 256:256 + NH], ACT.Sigmoid).then_inc(s_gate, 1)
                                nc.scalar.activation(v_nsa[:, n, :, :, 0:DH].rearrange("p a g d -> p (a g) d"),
                                                     ps[:, u % 4, 0:256].rearrange("p (a d) -> p a d", d=DH), ACT.Copy).then_inc(s_hi, 1)
                            else:
                                e = spill[i] + n
                                act.wait_ge(s_sp[e % 2], 32 * (e // 2))
                                nc.scalar.activation(evh[e % 2][:, 0:512], ps[:, u % 4, 0:512], ACT.Copy).then_inc(s_hi, 1)
                    else:
                        u, c = use0[i], step[1]
                        act.wait_ge(s_mm, u + 1)
                        if c % 2 == 0:
                            if c:
                                act.wait_ge(s_hid, 1)
                            nc.scalar.activation(gel[:, 0, :], ps[:, u % 4, 0:CP], ACT.Copy).then_inc(s_hi, 1)
                            act.wait_ge(s_gel, 2 * c + 3)
                            nc.scalar.activation(gel[:, 2, :], gel[:, 1, :], ACT.Tanh, scale=(2.0 / np.pi) ** 0.5).then_inc(s_tanh, 1)
                        elif c == 1:
                            nc.scalar.activation(cth[:, :], ps[:, u % 4, 0:CP], ACT.Copy).then_inc(s_hi, 1)
                        else:
                            nc.scalar.activation(vc[:, :, 0:DH], ps[0:DH, u % 4, 0:P].rearrange("p (g d) -> p g d", g=NG),
                                                 ACT.Copy).then_inc(s_hi, 1)

                split(0)
                for i in range(len(PLAN)):
                    if i + 1 < len(PLAN) and PLAN[i + 1][0] != "c":
                        split(i + 1)
                    evict(i)

            @block.vector
            def _(dve):
                dve.wait_ge(s_const, 16 * 2)

                for n in range(NT + 1):
                    if n < NT:
                        dve.wait_ge(s_sq, n + 1)
                        nc.vector.tensor_scalar(stat[:, 1, n:n + 1], stat[:, 0, n:n + 1], 1.0 / D, EPS, ALU.mult, ALU.add).then_inc(s_ms, 1)
                        dve.wait_ge(s_rt, n + 1)
                        nc.vector.reciprocal(stat[:, 3, n:n + 1], stat[:, 2, n:n + 1]).then_inc(s_ri, 1)
                        dve.wait_ge(s_ri, n + 1)
                        if n >= 2:
                            dve.wait_ge(s_mm, n - 1)
                        nc.vector.scalar_tensor_tensor(xn[n % 2], xt[n % 2], stat[:, 3, n:n + 1], gb[:, :], ALU.mult, ALU.mult).then_inc(s_xn, 1)
                    if n:
                        dve.wait_ge(s_hi, n)
                        nc.vector.tensor_tensor(xl[:, :, (n - 1) * P:n * P], ps[:, (n - 1) % 4, :].rearrange("p (k t) -> p k t", k=KT),
                                                xh[:, :, (n - 1) * P:n * P].bitcast(f32), ALU.subtract).then_inc(s_lo, 1)

                def split(i):
                    for q in range(NPIECE[PLAN[i][0]]):
                        p = piece0[i] + q
                        dve.wait_ge(s_whi, p + 1)
                        s, h = halves(i, wth, wnh, q)
                        _, l = halves(i, wtl, wnl, q)
                        nc.vector.tensor_tensor(l, s, h.bitcast(f32), ALU.subtract).then_inc(s_wlo, 1)

                def evict(i):
                    step = PLAN[i]
                    if step[0] == "t" and not isinstance(step[2], str):
                        scaled = step[2] in range(U_Q, U_Q + 4) or step[2] in range(U_DQ, U_DQ + 4)
                        u, e = use0[i], spill[i]
                        dve.wait_ge(s_hi, u + 1)
                        nc.vector.scalar_tensor_tensor(evl[e % 2][:, :], ps[:, u % 4, :], DH ** -0.5 if scaled else 1.0,
                                                       evh[e % 2][:, :].bitcast(f32), ALU.mult, ALU.subtract).then_inc(s_lo, 1)
                    elif step[0] == "t":
                        dve.wait_ge(s_hi, use0[i] + 1)
                        dve.wait_ge(s_lo, use0[i])
                        dve.sem_inc(s_lo, 1)
                    elif step[0] == "n":
                        for n in range(NT):
                            u = use0[i] + n
                            dve.wait_ge(s_hi, u + 1)
                            if step[1] == 0:
                                nc.vector.tensor_tensor(v_nsa[:, n, :, :, DH:VS].rearrange("p a g d -> p (a g) d"),
                                                        ps[:, u % 4, 0:256].rearrange("p (a d) -> p a d", d=DH),
                                                        v_nsa[:, n, :, :, 0:DH].bitcast(f32).rearrange("p a g d -> p (a g) d"),
                                                        ALU.subtract).then_inc(s_lo, 1)
                            else:
                                e = spill[i] + n
                                nc.vector.tensor_tensor(evl[e % 2][:, 0:512], ps[:, u % 4, 0:512],
                                                        evh[e % 2][:, 0:512].bitcast(f32), ALU.subtract).then_inc(s_lo, 1)
                    else:
                        u, c = use0[i], step[1]
                        dve.wait_ge(s_hi, u + 1)
                        if c % 2 == 0:
                            dve.wait_ge(s_lo, u)
                            dve.sem_inc(s_lo, 1)
                            x0, x1, th, g0 = gel[:, 0, :], gel[:, 1, :], gel[:, 2, :], 2 * c
                            nc.vector.tensor_tensor(x1, x0, x0, ALU.mult).then_inc(s_gel, 1)
                            dve.wait_ge(s_gel, g0 + 1)
                            nc.vector.tensor_scalar(x1, x1, 0.044715, 1.0, ALU.mult, ALU.add).then_inc(s_gel, 1)
                            dve.wait_ge(s_gel, g0 + 2)
                            nc.vector.tensor_tensor(x1, x1, x0, ALU.mult).then_inc(s_gel, 1)
                            dve.wait_ge(s_tanh, c // 2 + 1)
                            nc.vector.scalar_tensor_tensor(th, th, 1.0, x0, ALU.add, ALU.mult).then_inc(s_gel, 1)
                            dve.wait_ge(s_gel, g0 + 4)
                            nc.vector.tensor_scalar(hid[:, c // 2, :], th, 0.5, None, ALU.mult).then_inc(s_hid, 1)
                        elif c == 1:
                            nc.vector.tensor_tensor(ctl[:, :], ps[:, u % 4, 0:CP], cth[:, :].bitcast(f32), ALU.subtract).then_inc(s_lo, 1)
                        else:
                            nc.vector.tensor_tensor(vc[:, :, DH:VS], ps[0:DH, u % 4, 0:P].rearrange("p (g d) -> p g d", g=NG),
                                                    vc[:, :, 0:DH].bitcast(f32), ALU.subtract).then_inc(s_lo, 1)

                def blocks(c):
                    if c == 1:
                        dve.wait_ge(s_mm, use0[PLAN.index(("c", 0))] + 1)
                    if c == 0:
                        dve.wait_ge(s_pos, 64)
                        dve.wait_ge(s_hi, use0[1] + 1)
                    a = src[:, c, :].rearrange("p (n s) -> p s n", s=CMP_STRIDE)
                    for r in range(2):
                        nc.vector.tensor_tensor(srcb[:, r * CMP_STRIDE:(r + 1) * CMP_STRIDE, 0:NCMP], a[:, :, r:r + NCMP],
                                                posT[:, c, r * CMP_STRIDE:(r + 1) * CMP_STRIDE].unsqueeze(2).to_broadcast([P, CMP_STRIDE, NCMP]),
                                                ALU.add).then_inc(s_blk, 1)

                split(0)
                for i in range(len(PLAN)):
                    if i + 1 < len(PLAN) and PLAN[i + 1][0] != "c":
                        split(i + 1)
                    if i == 1:
                        nc.vector.memset(srcb[:, :, NCMP:CP], 0.0).then_inc(s_blk, 1)
                        blocks(0)
                    evict(i)
                    if PLAN[i] == ("c", 0):
                        blocks(1)
                dve.wait_ge(s_gate, 2 * NT)
                logarithm(dve, lgate[:, :, :, :].rearrange("p n b h -> p (n b h)"), gates[:, :, :].rearrange("p n c -> p (n c)"),
                          [t[:, :, :].rearrange("p n c -> p (n c)") for t in lg_tmp], 1e-37, s_log, 0)

            @block.tensor
            def _(pe):
                pe.wait_ge(s_const, 16 * 2)

                def slot_free(u):
                    if u >= 4:
                        pe.wait_ge(s_lo, u - 3)

                for n in range(NT):
                    slot_free(n)
                    pe.wait_ge(s_xn, n + 1)
                    for k in range(KT):
                        last = nc.tensor.transpose(ps[:, n % 4, k * P:(k + 1) * P], xn[n % 2][:, k * P:(k + 1) * P], ident[:, :])
                    last.then_inc(s_mm, 1)
                pe.wait_ge(s_lo, NT)
                for i, step in enumerate(PLAN):
                    if step[0] == "t":
                        u, w = use0[i], tun[i] % 2
                        slot_free(u)
                        pe.wait_ge(s_wlo, piece0[i] + 1)
                        for half in range(2):
                            cols = slice(half * 512, half * 512 + 512)
                            for k in range(KT):
                                nc.tensor.matmul(ps[:, u % 4, cols], wth[w][:, k, :], xh[:, k, cols], start=(k == 0), stop=False)
                                nc.tensor.matmul(ps[:, u % 4, cols], wth[w][:, k, :], xl[:, k, cols], start=False, stop=False)
                                last = nc.tensor.matmul(ps[:, u % 4, cols], wtl[w][:, k, :], xh[:, k, cols], start=False, stop=(k == KT - 1))
                        last.then_inc(s_mm, 1)
                    elif step[0] == "n":
                        pe.wait_ge(s_wlo, piece0[i] + 4)
                        w = nwidth(step[1])
                        for n in range(NT):
                            u = use0[i] + n
                            slot_free(u)
                            rows = slice(n * P, n * P + P)
                            for k in range(KT):
                                nc.tensor.matmul(ps[:, u % 4, 0:w], xh[:, k, rows], wnh[:, k, 0:w], start=(k == 0), stop=False)
                                nc.tensor.matmul(ps[:, u % 4, 0:w], xh[:, k, rows], wnl[:, k, 0:w], start=False, stop=False)
                                last = nc.tensor.matmul(ps[:, u % 4, 0:w], xl[:, k, rows], wnh[:, k, 0:w], start=False, stop=(k == KT - 1))
                            last.then_inc(s_mm, 1)
                    else:
                        u, c = use0[i], step[1]
                        slot_free(u)
                        if c % 2 == 0:
                            pe.wait_ge(s_w1, 16 * 6 + 32 * (c // 2))
                            pe.wait_ge(s_blk, 3 + c)
                            for l in range(CMP_BLOCK):
                                last = nc.tensor.matmul(ps[:, u % 4, 0:CP], w1bd[:, l, :], srcb[:, l, :], start=(l == 0), stop=(l == CMP_BLOCK - 1))
                        else:
                            pe.wait_ge(s_hid, (c + 1) // 2)
                            if c == 1:
                                last = nc.tensor.matmul(ps[:, u % 4, 0:CP], w2bd[:, 0, :], hid[:, 0, :], start=True, stop=True)
                            else:
                                last = nc.tensor.matmul(ps[0:CP, u % 4, 0:P], hid[:, 1, :], w2bd[:, 1, :], start=True, stop=True)
                        last.then_inc(s_mm, 1)
        scope.close()

        def attention(kind, o_t):
            nsa = kind == "nsa"
            scope = ExitStack()
            NHL = 4
            NPR = 3
            NSL = 3
            LAG = 3
            LEAD, TAIL = (3, 4) if nsa else (2, 2)
            nbr = 3 if nsa else 1
            LOG = LOG_DEGREE + 6 + nsa
            SPL = 3 + nsa
            krows = MROW + 2 * nbr
            qa = [sbuf(scope, f"{kind}_qa{i}", [P, T], r32) for i in range(2)]
            qb = [sbuf(scope, f"{kind}_qb{i}", [P, T], r32) for i in range(2)]
            nk = 4 if nsa else 2
            ka = [sbuf(scope, f"{kind}_ka{i}", [P, T], r32) for i in range(nk)]
            kb = [sbuf(scope, f"{kind}_kb{i}", [P, T], r32) for i in range(nk)]
            prob = [sbuf(scope, f"{kind}_prob{i}", [P, T]) for i in range(NPR)]
            ph = [sbuf(scope, f"{kind}_ph{i}", [P, T], r32) for i in range(NHL)]
            pl = [sbuf(scope, f"{kind}_pl{i}", [P, T], r32) for i in range(NHL)]
            negm = sbuf(scope, f"{kind}_negm", [P, 2, NT, nbr])
            sums = sbuf(scope, f"{kind}_sums", [P, 2, NT, nbr])
            lsum = sbuf(scope, f"{kind}_lsum", [P, NT * nbr])
            lg_tmp = [sbuf(scope, f"{kind}_lg{i}", [P, NT * nbr]) for i in range(3)]
            negl = sbuf(scope, f"{kind}_negl", [P, NT, nbr])
            negl2 = sbuf(scope, f"{kind}_negl2", [P, NT, 2 * nbr], r32)
            if not nsa:
                vd = [sbuf(scope, f"dil_v{i}", [P, NT, VS], r32) for i in range(2)]
                dlog_h = [sbuf(scope, f"dil_logh{i}", [P, NT * P], r32) for i in range(2)]
                dlog_l = [sbuf(scope, f"dil_logl{i}", [P, NEAR * P], r32) for i in range(2)]
            s_load = [sem(scope, f"{kind}_load{i}") for i in range(2)]
            s_aug = [sem(scope, f"{kind}_aug{i}") for i in range(2)]
            s_vload = [sem(scope, f"{kind}_vload{i}") for i in range(2)]
            s_k, s_kaug = sem(scope, f"{kind}_k"), sem(scope, f"{kind}_kaug")
            s_s, s_ra, s_hi, s_lod, s_lop, s_pv, s_max, s_log, s_spl, s_cp, s_ev, s_m = (
                sem(scope, f"{kind}_{n}") for n in ("s", "ra", "hi", "lod", "lop", "pv", "max", "log", "spl", "cp", "ev", "m"))

            first, second = {}, {}
            for h in range(NH):
                if nsa:
                    first[h] = [("p1", h, n, br) for n in range(NT) for br in (0, 1)]
                    second[h] = [("p2", h, m, br) for br in (0, 1) for m in range(NT)] + [("p2", h, 0, 2)]
                else:
                    first[h] = [("p1", h, n, 0) for n in range(NT)]
                    second[h] = [("p2", h, m, 0) for m in range(NT)]
            order = first[0] + [("m", 0)]
            for h in range(NH):
                a, b = second[h], first.get(h + 1, [])
                spread, done = len(a) - LEAD - TAIL, 0
                for j, item in enumerate(a):
                    order.append(item)
                    upto = len(b) * min(max(j + 1 - LEAD, 0), spread) // spread
                    order += b[done:upto]
                    done = upto
                    if b and j == len(a) - 2:
                        order.append(("m", h + 1))
            events, waiting = [], []

            def flush(upto):
                while waiting and waiting[0][1] <= upto:
                    item = waiting.pop(0)[0]
                    events.append(("v",) + item[1:])
                    if item == second[item[1]][-1]:
                        events.append(("e", item[1]))

            for i, item in enumerate(order):
                events.append(item)
                if item[0] == "p2":
                    waiting.append((item, i + LAG))
                flush(i)
            flush(len(order) + LAG)
            items = order
            at = {e: i for i, e in enumerate(items)}
            p2s = [e for e in items if e[0] == "p2"]
            p2_at = {e: i for i, e in enumerate(p2s)}
            on_pool = [i % 5 in (1, 3) for i in range(len(p2s))]
            reads = [sum(2 if e[0] == "p1" and e[3] else 1 for e in items[:i + 1]) for i in range(len(items))]

            def low_done(eng, c):
                if on_pool[c]:
                    eng.wait_ge(s_lop, sum(on_pool[:c + 1]))
                else:
                    eng.wait_ge(s_lod, c + 1 - sum(on_pool[:c + 1]))

            def span(br, m):
                if br == 2:
                    return 0, T
                return m * P, (min(m + WIN_TILES + 1, NT) if br == 1 else NT) * P

            def banks(lo, hi):
                return [(c, min(c // 512 * 512 + 512, hi)) for c in sorted({lo} | {x for x in (512,) if lo < x < hi})]

            block = nc.Block()
            with block:
                @block.sync
                def _(sp):
                    if nsa:
                        for g in range(NG):
                            for br in range(2):
                                kk, rows = 2 * g + br, slice(g * DH, (g + 1) * DH)
                                sp.dma_start(ka[kk][0:DH, :].bitcast(f32), qk_hi[U_KSLC + br, rows, :]).then_inc(s_k, 16)
                                sp.dma_start(ka[kk][DH:P, :].bitcast(f32), qk_hi[U_KSLC + br, rows, :]).then_inc(s_k, 16)
                                sp.dma_start(kb[kk][0:DH, :].bitcast(f32), qk_lo[U_KSLC + br, rows, :]).then_inc(s_k, 16)
                    for h in range(NH):
                        b = h % 2
                        if h >= 2:
                            sp.wait_ge(s_s, at[second[h - 2][-1]] + 1)
                        rows = slice(b * DH, (b + 1) * DH)
                        u = (U_Q if nsa else U_DQ) + h // 2
                        sp.dma_start(qa[b][0:DH, :].bitcast(f32), qk_hi[u, rows, :]).then_inc(s_load[b], 16)
                        sp.dma_start(qb[b][0:DH, :].bitcast(f32), qk_hi[u, rows, :]).then_inc(s_load[b], 16)
                        sp.dma_start(qa[b][DH:P, :].bitcast(f32), qk_lo[u, rows, :]).then_inc(s_load[b], 16)
                        if not nsa:
                            u = U_DK + h // 2
                            sp.dma_start(ka[b][0:DH, :].bitcast(f32), qk_hi[u, rows, :]).then_inc(s_load[b], 16)
                            sp.dma_start(ka[b][DH:P, :].bitcast(f32), qk_hi[u, rows, :]).then_inc(s_load[b], 16)
                            sp.dma_start(kb[b][0:DH, :].bitcast(f32), qk_lo[u, rows, :]).then_inc(s_load[b], 16)
                            if h >= 2:
                                sp.wait_ge(s_pv, p2_at[second[h - 2][-1]] + 1)
                            sp.dma_start(vd[b][:, :, :].bitcast(f32),
                                         v_dil[:, h, :, :].rearrange("(n p) a c -> p n (a c)", p=P)).then_inc(s_vload[b], 16)

                @block.gpsimd
                def _(pool):
                    for i in range(nk):
                        pool.dma_start(kb[i][DH:MROW + 2 * KBR, :], kaug_in[i % 2 if nsa else 0]).then_inc(s_kaug, 16)

                    def alibi(h):
                        if h >= 2:
                            pool.wait_ge(s_s, at[second[h - 2][-1]] + 1)
                        pool.dma_start(qb[h % 2][DH:MROW, :], qaug_in[(0 if nsa else NH) + h]).then_inc(s_aug[h % 2], 16)

                    alibi(0)
                    if not nsa:
                        for i in range(2):
                            first_near = (NT - NEAR) * P if i == 0 else 0
                            pool.dma_start(dlog_h[i][:, :], dil_log_in[0, i]).then_inc(s_kaug, 16)
                            pool.dma_start(dlog_l[i][:, :], dil_log_in[1, i, :, first_near:first_near + NEAR * P]).then_inc(s_kaug, 16)
                    alibi(1)
                    for e in items:
                        if e[0] == "p2" and on_pool[p2_at[e]]:
                            c = p2_at[e]
                            lo, hi = span(e[3], e[2])
                            n = CP if e[3] == 2 else P
                            pool.wait_ge(s_hi, c + 1)
                            nc.gpsimd.tensor_tensor(pl[c % NHL][0:n, lo:hi], prob[c % NPR][0:n, lo:hi],
                                                    ph[c % NHL][0:n, lo:hi].bitcast(f32), ALU.subtract).then_inc(s_lop, 1)
                        if e == second.get(e[1], [None])[-1] and e[1] + 2 < NH:
                            alibi(e[1] + 2)

                @block.tensor
                def _(pe):
                    def scores(i, e):
                        slot = ps[:, i % NSL, :]
                        if i >= NSL:
                            pe.wait_ge(s_ra, reads[i - NSL])
                        if e[0] == "p1":
                            _, h, n, br = e
                            b, g = h % 2, h // HPG
                            if e == first[h][0]:
                                if h == 0:
                                    pe.wait_ge(s_kaug, 16 * (nk + (0 if nsa else 4)))
                                    if nsa:
                                        pe.wait_ge(s_k, 16 * 12)
                                pe.wait_ge(s_load[b], 16 * (3 if nsa else 6) * (h // 2 + 1))
                                pe.wait_ge(s_aug[b], 16 * (h // 2 + 1))
                            q = qa[b][:, n * P:(n + 1) * P], qb[b][0:DH + AUG, n * P:(n + 1) * P]
                            k0 = max(0, n - WIN_TILES) * P if br else 0
                            k1 = (n + 1) * P
                            kk = 2 * g + br if nsa else b
                            for c0, c1 in banks(0, k1 - k0):
                                keys = slice(k0 + c0, k0 + c1)
                                nc.tensor.matmul(slot[:, c0:c1], q[0], ka[kk][:, keys], start=True, stop=False)
                                if nsa:
                                    marks = [(n * P - k0, n * P - k0 + P, identb[:, :], m_diag)]
                                    if br and n >= WIN_TILES:
                                        marks.append((0, P, identb[:, :], m_win))
                                    marks = [mark for mark in marks if c0 <= mark[0] < c1]
                                else:
                                    t0 = (NT - 1 - n) * P
                                    marks = [(c0, c1, identr[:, :], dlog_h[0][:, t0 + c0:t0 + c1])]
                                    x = max(c0, (n + 1 - NEAR) * P)
                                    if x < c1:
                                        y0 = t0 - (NT - NEAR) * P
                                        marks.append((x, c1, identr[:, :], dlog_l[0][:, y0 + x:y0 + c1]))
                                last = nc.tensor.matmul(slot[:, c0:c1], q[1], kb[kk][0:DH + AUG, keys], start=False, stop=not marks)
                                for y, (x0, x1, one, mk) in enumerate(marks):
                                    last = nc.tensor.matmul(slot[:, x0:x1], one, mk, start=False, stop=y == len(marks) - 1)
                            if nsa and br:
                                dst = slot[:, k1 - k0:k1 - k0 + CP]
                                nc.tensor.matmul(dst, q[0], kc[:, g, 0, :], start=True, stop=False)
                                nc.tensor.matmul(dst, q[1], kc[0:DH + AUG, g, 1, :], start=False, stop=False)
                                last = nc.tensor.matmul(dst, identb[:, :], m_cmp[:, n * CP:(n + 1) * CP], start=False, stop=True)
                        elif e[0] == "m":
                            pe.wait_ge(s_spl, SPL * (e[1] + 1))
                            for n in range(NT):
                                last = nc.tensor.matmul(slot[0:2 * nbr, n * P:(n + 1) * P], negl2[:, n, :], identr[:, :], start=True, stop=True)
                        else:
                            _, h, m, br = e
                            b, g = h % 2, h // HPG
                            if e == second[h][0]:
                                pe.wait_ge(s_m, h + 1)
                            if br == 2:
                                k = kc[:, g, 0, :], kc[0:krows, g, 1, :]
                            else:
                                kk = 2 * g + br if nsa else b
                                k = ka[kk][:, m * P:(m + 1) * P], kb[kk][0:krows, m * P:(m + 1) * P]
                            n = CP if br == 2 else P
                            lo, hi = span(br, m)
                            for c0, c1 in banks(lo, hi):
                                nc.tensor.matmul(slot[0:n, c0:c1], k[0], qa[b][:, c0:c1], start=True, stop=False)
                                marks = []
                                if br == 2:
                                    marks.append((c0, c1, identb[0:CP, 0:CP], m_cmp_t[:, c0:c1]))
                                elif nsa:
                                    for x, mk in [(m * P, m_diag_t)] + [((m + WIN_TILES) * P, m_win_t)] * br:
                                        if c0 <= x < c1:
                                            marks.append((x, x + P, identb[:, :], mk))
                                else:
                                    marks.append((c0, c1, identr[:, :], dlog_h[1][:, c0 - m * P:c1 - m * P]))
                                    x = min(c1, (m + NEAR) * P)
                                    if c0 < x:
                                        marks.append((c0, x, identr[:, :], dlog_l[1][:, c0 - m * P:x - m * P]))
                                last = nc.tensor.matmul(slot[0:n, c0:c1], k[1], qb[b][0:krows, c0:c1], start=False, stop=not marks)
                                for y, (x0, x1, one, mk) in enumerate(marks):
                                    last = nc.tensor.matmul(slot[0:n, x0:x1], one, mk, start=False, stop=y == len(marks) - 1)
                        last.then_inc(s_s, 1)

                    def values(e):
                        _, h, m, br = e
                        c = p2_at[e]
                        o = ps[:, NSL, :]
                        start, end = e == second[h][0], e == second[h][-1]
                        if start and h:
                            pe.wait_ge(s_ev, h)
                        if start and not nsa:
                            pe.wait_ge(s_vload[h % 2], 16 * (h // 2 + 1))
                        pe.wait_ge(s_hi, c + 1)
                        low_done(pe, c)
                        if br == 2:
                            v, n = vc[:, h // HPG, :], CP
                        else:
                            v, n = (v_nsa[:, m, br, h // HPG, :] if nsa else vd[h % 2][:, m, :]), P
                        s0, s1 = span(br, m)
                        for c0, c1 in banks(s0, s1):
                            nc.tensor.matmul(o[:, c0:c1], v, ph[c % NHL][0:n, c0:c1], start=start, stop=False, skip_group_check=True)
                            last = nc.tensor.matmul(o[:, c0:c1], v, pl[c % NHL][0:n, c0:c1], start=False, stop=end, skip_group_check=True)
                        last.then_inc(s_pv, 1)

                    for e in events:
                        if e[0] == "v":
                            values(("p2",) + e[1:])
                        elif e[0] != "e":
                            scores(at[e], e)

                @block.scalar
                def _(act):
                    nmax = 0
                    for i, e in enumerate(items):
                        slot = ps[:, i % NSL, :]
                        if e[0] == "p1":
                            _, h, n, br = e
                            k1 = (n + 1 - (max(0, n - WIN_TILES) if br else 0)) * P
                            parts = [(br, 0, k1)] + ([(2, k1, k1 + CP)] if br else [])
                            nmax += len(parts)
                            act.wait_ge(s_max, nmax)
                            for j, c0, c1 in parts:
                                nc.scalar.activation(slot[:, c0:c1], slot[:, c0:c1], ACT.Exp, bias=negm[:, h % 2, n, j:j + 1],
                                                     accum_out=sums[:, h % 2, n, j:j + 1]).then_inc(s_ra, 1)
                        elif e[0] == "m":
                            act.wait_ge(s_s, i + 1)
                            nc.scalar.activation(qb[e[1] % 2][MROW:krows, :], slot[0:2 * nbr, :], ACT.Copy).then_inc(s_ra, 1)
                            act.wait_ge(s_ra, reads[i])
                            act.sem_inc(s_m, 1)
                        else:
                            _, h, m, br = e
                            c = p2_at[e]
                            lo, hi = span(br, m)
                            n = CP if br == 2 else P
                            act.wait_ge(s_s, i + 1)
                            if c >= NPR:
                                act.wait_ge(s_hi, c - NPR + 1)
                                low_done(act, c - NPR)
                            nc.scalar.activation(prob[c % NPR][0:n, lo:hi], slot[0:n, lo:hi], ACT.Exp).then_inc(s_ra, 1)

                @block.vector
                def _(dve):
                    def parts(c):
                        _, h, m, br = p2s[c]
                        lo, hi = span(br, m)
                        n = CP if br == 2 else P
                        dve.wait_ge(s_ra, reads[at[p2s[c]]])
                        if c >= NHL:
                            dve.wait_ge(s_pv, c - NHL + 1)
                        nc.vector.tensor_copy(ph[c % NHL][0:n, lo:hi], prob[c % NPR][0:n, lo:hi]).then_inc(s_hi, 1)
                        if not on_pool[c]:
                            dve.wait_ge(s_hi, c + 1)
                            nc.vector.tensor_tensor(pl[c % NHL][0:n, lo:hi], prob[c % NPR][0:n, lo:hi],
                                                    ph[c % NHL][0:n, lo:hi].bitcast(f32), ALU.subtract).then_inc(s_lod, 1)

                    def finish(h, nmax):
                        n2 = negl2[:, :, :].rearrange("p n (b t) -> p n b t", t=2)
                        dve.wait_ge(s_ra, reads[at[first[h][-1]]])
                        dve.wait_ge(s_max, nmax)
                        base = LOG * h + nsa
                        done = logarithm(dve, lsum[:, :], sums[:, h % 2, :, :].rearrange("p n b -> p (n b)"), [t[:, :] for t in lg_tmp], 0.5, s_log, base)
                        dve.wait_ge(s_log, done)
                        nc.vector.tensor_tensor(negl[:, :, :], negm[:, h % 2, :, :], lsum[:, :].rearrange("p (n b) -> p n b", b=nbr),
                                                ALU.subtract).then_inc(s_spl, 1)
                        dve.wait_ge(s_spl, SPL * h + 1)
                        if nsa:
                            nc.vector.tensor_tensor(negl[:, :, :], negl[:, :, :], lgate[:, :, :, h], ALU.add).then_inc(s_spl, 1)
                            dve.wait_ge(s_spl, SPL * h + 2)
                        if h:
                            dve.wait_ge(s_m, h)
                        nc.vector.tensor_copy(n2[:, :, :, 0], negl[:, :, :]).then_inc(s_spl, 1)
                        dve.wait_ge(s_spl, SPL * (h + 1) - 1)
                        nc.vector.tensor_tensor(n2[:, :, :, 1], negl[:, :, :], n2[:, :, :, 0].bitcast(f32), ALU.subtract).then_inc(s_spl, 1)

                    nmax, ready, summed = 0, [], None
                    for e in events:
                        if e[0] == "p1":
                            _, h, n, br = e
                            i = at[e]
                            slot = ps[:, i % NSL, :]
                            k1 = (n + 1 - (max(0, n - WIN_TILES) if br else 0)) * P
                            nm = negm[:, h % 2, n, :]
                            dve.wait_ge(s_s, i + 1)
                            if e == first[h][0] and h >= 2:
                                dve.wait_ge(s_spl, SPL * (h - 1))
                            if br and n == 0:
                                nc.vector.tensor_reduce(nm[:, 2:3], slot[:, k1:k1 + CP], AX.X, ALU.max, negate=True).then_inc(s_log, 1)
                                dve.wait_ge(s_log, LOG * h + 1)
                                nc.vector.tensor_scalar(nm[:, 2:3], nm[:, 2:3], -FLOOR, None, ALU.min).then_inc(s_max, 1)
                            elif br:
                                nc.vector.tensor_reduce(nm[:, 2:3], slot[:, k1:k1 + CP], AX.X, ALU.max, negate=True).then_inc(s_max, 1)
                            nc.vector.tensor_reduce(nm[:, br:br + 1], slot[:, 0:k1], AX.X, ALU.max, negate=True).then_inc(s_max, 1)
                            nmax += 2 if br else 1
                        if e[0] in ("p1", "p2"):
                            for c in ready:
                                parts(c)
                            ready = [p2_at[e]] if e[0] == "p2" else []
                        if summed is not None:
                            finish(summed, nmax)
                            summed = None
                        if e[0] == "p1" and e == first[e[1]][-1]:
                            summed = e[1]
                        if e[0] == "e":
                            h = e[1]
                            for c in ready:
                                parts(c)
                            ready = []
                            dve.wait_ge(s_pv, p2_at[second[h][-1]] + 1)
                            dst = o_t[h % 2 * DH:h % 2 * DH + DH, h // 2, :]
                            nc.vector.tensor_copy(dst, ps[DH:P, NSL, :]).then_inc(s_cp, 1)
                            dve.wait_ge(s_cp, h + 1)
                            nc.vector.tensor_tensor(dst, ps[0:DH, NSL, :], dst, ALU.add).then_inc(s_ev, 1)
                    for c in ready:
                        parts(c)
            scope.close()

        attention("nsa", o_nsa)
        scope_v.close()
        o_d = sbuf(top, "o_d", [P, NH // 2, T])
        attention("dil", o_d)

        scope_g = ExitStack()
        gh = sbuf(scope_g, "gh", [P, 2 * NH // 2, T], r32)
        gl = sbuf(scope_g, "gl", [P, 2 * NH // 2, T], r32)
        scope = ExitStack()
        NRAW2 = 2
        raw = [sbuf(scope, f"z_raw{i}", [P, KT, P]) for i in range(NRAW2)]
        wth = [sbuf(scope, f"z_wth{i}", [P, KT, P], r32) for i in range(2)]
        wtl = [sbuf(scope, f"z_wtl{i}", [P, KT, P], r32) for i in range(2)]
        zs = sbuf(scope, "zs", [P, T])
        gf = sbuf(scope, "gf", [P, T])
        s_raw = [sem(scope, f"z_raw{i}") for i in range(NRAW2)]
        s_whi, s_wlo, s_mm, s_zs, s_gf, s_gh, s_gl = (sem(scope, f"z_{n}") for n in ("whi", "wlo", "mm", "zs", "gf", "gh", "gl"))
        NZ = NH
        z_cols = [C_ZN + P * i for i in range(4)] + [C_ZD + P * i for i in range(4)]
        block = nc.Block()
        with block:
            @block.sync
            def _(sp):
                for i, col in enumerate(z_cols):
                    if i >= NRAW2:
                        sp.wait_ge(s_wlo, i - NRAW2 + 1)
                    sp.dma_start(raw[i % NRAW2][:, :, :], w_in_v[:, :, col:col + P]).then_inc(s_raw[i % NRAW2], 16)

            @block.gpsimd
            def _(pool):
                for i in range(NZ):
                    pool.wait_ge(s_gh, i + 1)
                    nc.gpsimd.tensor_tensor(gl[:, i, :], gf[:, :], gh[:, i, :].bitcast(f32), ALU.subtract).then_inc(s_gl, 1)

            @block.scalar
            def _(act):
                def split(i):
                    act.wait_ge(s_raw[i % NRAW2], 16 * (i // NRAW2 + 1))
                    if i >= 2:
                        act.wait_ge(s_mm, i - 1)
                    nc.scalar.activation(wth[i % 2][:, :, :], raw[i % NRAW2][:, :, :], ACT.Copy).then_inc(s_whi, 1)

                split(0)
                for i in range(NZ):
                    if i + 1 < NZ:
                        split(i + 1)
                    act.wait_ge(s_mm, i + 1)
                    if i:
                        act.wait_ge(s_gf, i)
                    nc.scalar.activation(zs[:, :], ps[:, i % 4, :], ACT.Silu).then_inc(s_zs, 1)
                    act.wait_ge(s_gf, i + 1)
                    nc.scalar.activation(gh[:, i, :], gf[:, :], ACT.Copy).then_inc(s_gh, 1)

            @block.vector
            def _(dve):
                def split(i):
                    dve.wait_ge(s_whi, i + 1)
                    nc.vector.tensor_tensor(wtl[i % 2][:, :, :], raw[i % NRAW2][:, :, :], wth[i % 2][:, :, :].bitcast(f32), ALU.subtract).then_inc(s_wlo, 1)

                split(0)
                for i in range(NZ):
                    if i + 1 < NZ:
                        split(i + 1)
                    dve.wait_ge(s_zs, i + 1)
                    if i:
                        dve.wait_ge(s_gl, i)
                    o = o_nsa if i < 4 else o_d
                    nc.vector.tensor_tensor(gf[:, :], o[:, i % 4, :], zs[:, :], ALU.mult).then_inc(s_gf, 1)

            @block.tensor
            def _(pe):
                for i in range(NZ):
                    pe.wait_ge(s_wlo, i + 1)
                    if i >= 4:
                        pe.wait_ge(s_zs, i - 3)
                    for half in range(2):
                        cols = slice(half * 512, half * 512 + 512)
                        for k in range(KT):
                            nc.tensor.matmul(ps[:, i % 4, cols], wth[i % 2][:, k, :], xh[:, k, cols], start=(k == 0), stop=False)
                            nc.tensor.matmul(ps[:, i % 4, cols], wth[i % 2][:, k, :], xl[:, k, cols], start=False, stop=False)
                            last = nc.tensor.matmul(ps[:, i % 4, cols], wtl[i % 2][:, k, :], xh[:, k, cols], start=False, stop=(k == KT - 1))
                    last.then_inc(s_mm, 1)
        scope.close()

        merged_a = sbuf(scope_g, "merged_a", [P, 4, T])

        def merged(k):
            return merged_a[:, k, :] if k < 4 else o_d[:, k - 4, :]

        scope = ExitStack()
        raw = [sbuf(scope, f"m_raw{i}", [P, KT, P]) for i in range(3)]
        wth = [sbuf(scope, f"m_wth{i}", [P, KT, P], r32) for i in range(2)]
        wtl = [sbuf(scope, f"m_wtl{i}", [P, KT, P], r32) for i in range(2)]
        sg = [o_nsa[:, i, :] for i in range(2)]
        s_raw = [sem(scope, f"m_raw{i}") for i in range(3)]
        s_whi, s_wlo, s_mm, s_sg, s_y, s_mrg = (sem(scope, f"m_{n}") for n in ("whi", "wlo", "mm", "sg", "y", "mrg"))
        NPC = 3 * KT
        br_v = [w[0].rearrange("(k p) c -> p k c", p=P) for w in (w_br_nsa, w_br_dil)]
        block = nc.Block()
        with block:
            @block.sync
            def _(sp):
                for i in range(NPC):
                    m, part = divmod(i, 3)
                    if i >= 3:
                        sp.wait_ge(s_wlo, i - 2)
                    if part < 2:
                        col = C_MG + part * D + m * P
                        sp.dma_start(raw[i % 3][:, :, :], w_in_v[:, :, col:col + P]).then_inc(s_raw[i % 3], 16)
                    else:
                        for b in range(2):
                            sp.dma_start(raw[i % 3][:, 4 * b:4 * b + 4, :], br_v[b][:, :, m * P:(m + 1) * P]).then_inc(s_raw[i % 3], 16)

            @block.gpsimd
            def _(pool):
                for m in range(KT):
                    pool.wait_ge(s_y, 2 * (m + 1))
                    nc.gpsimd.tensor_tensor(merged(m), sg[0], sg[1], ALU.add).then_inc(s_mrg, 1)

            @block.scalar
            def _(act):
                def split(i):
                    m, part = divmod(i, 3)
                    act.wait_ge(s_raw[i % 3], 16 * (m + 1) * (2 if part == 2 else 1))
                    if i >= 2:
                        mm, pp = divmod(i - 2, 3)
                        act.wait_ge(s_mm, 4 * mm + (1, 2, 4)[pp])
                    nc.scalar.activation(wth[i % 2][:, :, :], raw[i % 3][:, :, :], ACT.Copy).then_inc(s_whi, 1)

                split(0)
                for i in range(NPC):
                    m, part = divmod(i, 3)
                    if i + 1 < NPC:
                        split(i + 1)
                    if part < 2:
                        act.wait_ge(s_mm, 4 * m + part + 1)
                        if m:
                            act.wait_ge(s_mrg, m)
                        nc.scalar.activation(sg[part], ps[:, part, :], ACT.Sigmoid).then_inc(s_sg, 1)

            @block.vector
            def _(dve):
                def split(i):
                    dve.wait_ge(s_whi, i + 1)
                    nc.vector.tensor_tensor(wtl[i % 2][:, :, :], raw[i % 3][:, :, :], wth[i % 2][:, :, :].bitcast(f32), ALU.subtract).then_inc(s_wlo, 1)

                split(0)
                for i in range(NPC):
                    m, part = divmod(i, 3)
                    if i + 1 < NPC:
                        split(i + 1)
                    if part == 2:
                        for b in range(2):
                            dve.wait_ge(s_sg, 2 * m + b + 1)
                            dve.wait_ge(s_mm, 4 * m + 3 + b)
                            nc.vector.tensor_tensor(sg[b], ps[:, 2 + b, :], sg[b], ALU.mult).then_inc(s_y, 1)

            @block.tensor
            def _(pe):
                def product(slot, w, ks, right_h, right_l):
                    for half in range(2):
                        cols = slice(half * 512, half * 512 + 512)
                        for k in ks:
                            nc.tensor.matmul(ps[:, slot, cols], wth[w][:, k, :], right_h[:, k, cols], start=(k == ks[0]), stop=False)
                            nc.tensor.matmul(ps[:, slot, cols], wth[w][:, k, :], right_l[:, k, cols], start=False, stop=False)
                            last = nc.tensor.matmul(ps[:, slot, cols], wtl[w][:, k, :], right_h[:, k, cols], start=False, stop=(k == ks[-1]))
                    last.then_inc(s_mm, 1)

                for i in range(NPC):
                    m, part = divmod(i, 3)
                    pe.wait_ge(s_wlo, i + 1)
                    if part < 2:
                        if m:
                            pe.wait_ge(s_sg, 2 * (m - 1) + part + 1)
                        product(part, i % 2, range(KT), xh, xl)
                    else:
                        for b in range(2):
                            if m:
                                pe.wait_ge(s_y, 2 * (m - 1) + b + 1)
                            product(2 + b, i % 2, range(4 * b, 4 * b + 4), gh, gl)
        scope.close()

        scope = ExitStack()
        raw = [sbuf(scope, f"f_raw{i}", [P, D]) for i in range(3)]
        res = [sbuf(scope, f"res{i}", [P, D]) for i in range(2)]
        ot = [sbuf(scope, f"ot{i}", [P, D]) for i in range(2)]
        fstat = sbuf(scope, "fstat", [P, 4, NT])
        s_raw = [sem(scope, f"f_raw{i}") for i in range(3)]
        s_res = [sem(scope, f"f_res{i}") for i in range(2)]
        s_st = [sem(scope, f"f_st{i}") for i in range(2)]
        s_fg, s_whi, s_wlo, s_mh, s_ml, s_mm, s_h, s_sq, s_ms, s_rt, s_ri, s_fin = (sem(scope, f"f_{n}") for n in (
            "fg", "whi", "wlo", "mh", "ml", "mm", "h", "sq", "ms", "rt", "ri", "fin"))
        woh, wol = xh, xl
        mhs = [gh[:, i, :].rearrange("p (k t) -> p k t", k=KT) for i in range(2)]
        mls = [gl[:, i, :].rearrange("p (k t) -> p k t", k=KT) for i in range(2)]
        fgb, junk = o_nsa[:, 0, :], o_nsa[:, 1, :]
        wo_v = w_out[0].rearrange("(k p) e -> p k e", p=P)
        block = nc.Block()
        with block:
            @block.sync
            def _(sp):
                for k in range(KT):
                    if k >= 3:
                        sp.wait_ge(s_wlo, k - 2)
                    sp.dma_start(raw[k % 3][:, :], wo_v[:, k, :]).then_inc(s_raw[k % 3], 16)
                sp.dma_start(fgb, final_g.rearrange("(a d) -> a d", a=1).partition_broadcast(P)).then_inc(s_fg, 16)
                for n in range(NT):
                    if n >= 2:
                        sp.wait_ge(s_fin, n - 1)
                    sp.dma_start(res[n % 2][:, :], x_v[n]).then_inc(s_res[n % 2], 16)
                    if n >= 1:
                        sp.wait_ge(s_fin, n)
                        sp.dma_start(out_v[n - 1], ot[(n - 1) % 2][:, :]).then_inc(s_st[(n - 1) % 2], 16)
                sp.wait_ge(s_fin, NT)
                sp.dma_start(out_v[NT - 1], ot[(NT - 1) % 2][:, :]).then_inc(s_st[(NT - 1) % 2], 16)
                for i in range(2):
                    sp.wait_ge(s_st[i], 16 * NT // 2)

            @block.scalar
            def _(act):
                def msplit(n):
                    if n >= 2:
                        act.wait_ge(s_mm, n - 1)
                    for i, m in enumerate((merged_a, o_d)):
                        nc.scalar.activation(mhs[n % 2][:, 4 * i:4 * i + 4, :], m[:, :, n * P:(n + 1) * P], ACT.Copy).then_inc(s_mh, 1)

                msplit(0)
                for k in range(KT):
                    act.wait_ge(s_raw[k % 3], 16 * (k // 3 + 1))
                    nc.scalar.activation(woh[:, k, :], raw[k % 3][:, :], ACT.Copy).then_inc(s_whi, 1)
                for n in range(NT):
                    if n + 1 < NT:
                        msplit(n + 1)
                    act.wait_ge(s_h, n + 1)
                    if n:
                        act.wait_ge(s_sq, n)
                    nc.scalar.activation(junk, ot[n % 2][:, :], ACT.Square, accum_out=fstat[:, 0, n:n + 1]).then_inc(s_sq, 1)
                    act.wait_ge(s_ms, n + 1)
                    nc.scalar.activation(fstat[:, 2, n:n + 1], fstat[:, 1, n:n + 1], ACT.Sqrt).then_inc(s_rt, 1)

            @block.vector
            def _(dve):
                def msplit(n):
                    dve.wait_ge(s_mh, 2 * n + 2)
                    for i, m in enumerate((merged_a, o_d)):
                        part = slice(4 * i, 4 * i + 4)
                        nc.vector.tensor_tensor(mls[n % 2][:, part, :], m[:, :, n * P:(n + 1) * P], mhs[n % 2][:, part, :].bitcast(f32),
                                                ALU.subtract).then_inc(s_ml, 1)

                msplit(0)
                for k in range(KT):
                    dve.wait_ge(s_whi, k + 1)
                    nc.vector.tensor_tensor(wol[:, k, :], raw[k % 3][:, :], woh[:, k, :].bitcast(f32), ALU.subtract).then_inc(s_wlo, 1)
                dve.wait_ge(s_fg, 16)
                for n in range(NT):
                    if n + 1 < NT:
                        msplit(n + 1)
                    dve.wait_ge(s_mm, n + 1)
                    dve.wait_ge(s_res[n % 2], 16 * (n // 2 + 1))
                    if n >= 2:
                        dve.wait_ge(s_st[n % 2], 16 * (n // 2))
                    nc.vector.tensor_tensor(ot[n % 2][:, :], ps[:, n % 4, :], res[n % 2][:, :], ALU.add).then_inc(s_h, 1)
                    dve.wait_ge(s_sq, n + 1)
                    nc.vector.tensor_scalar(fstat[:, 1, n:n + 1], fstat[:, 0, n:n + 1], 1.0 / D, EPS, ALU.mult, ALU.add).then_inc(s_ms, 1)
                    dve.wait_ge(s_rt, n + 1)
                    nc.vector.reciprocal(fstat[:, 3, n:n + 1], fstat[:, 2, n:n + 1]).then_inc(s_ri, 1)
                    dve.wait_ge(s_ri, n + 1)
                    nc.vector.scalar_tensor_tensor(ot[n % 2][:, :], ot[n % 2][:, :], fstat[:, 3, n:n + 1], fgb, ALU.mult, ALU.mult).then_inc(s_fin, 1)

            @block.tensor
            def _(pe):
                for n in range(NT):
                    pe.wait_ge(s_ml, 2 * n + 2)
                    if n >= 4:
                        pe.wait_ge(s_h, n - 3)
                    for k in range(KT):
                        if n == 0:
                            pe.wait_ge(s_wlo, k + 1)
                        for half in range(2):
                            cols = slice(half * 512, half * 512 + 512)
                            nc.tensor.matmul(ps[:, n % 4, cols], mhs[n % 2][:, k, :], woh[:, k, cols], start=(k == 0), stop=False)
                            nc.tensor.matmul(ps[:, n % 4, cols], mhs[n % 2][:, k, :], wol[:, k, cols], start=False, stop=False)
                            last = nc.tensor.matmul(ps[:, n % 4, cols], mls[n % 2][:, k, :], woh[:, k, cols], start=False, stop=(k == KT - 1))
                    last.then_inc(s_mm, 1)
        scope.close()
        scope_g.close()


_INS = ['x', 'norm_g', 'w_in', 'cmp_pos_k', 'cmp_w1_k', 'cmp_w2_k', 'cmp_pos_v', 'cmp_w1_v', 'cmp_w2_v',
        'w_br_nsa', 'w_br_dil', 'w_out', 'final_g']


def constants():
    import numpy as np
    q, k = np.arange(P)[:, None], np.arange(P)[None, :]
    diag = np.where(k > q, NEG, 0.0)
    win = np.where(k <= q, NEG, 0.0)
    t = np.arange(T).reshape(NT, P)
    c = np.arange(CP)
    end = c * CMP_STRIDE + CMP_BLOCK - 1
    cmp = np.where((end[None, None] <= t[:, :, None]) & (c < NCMP)[None, None], 0.0, NEG)
    cmp_t = np.zeros((P, T))
    cmp_t[:CP] = cmp.reshape(T, CP).T
    masks = np.concatenate([diag, win, diag.T, win.T, cmp.transpose(1, 0, 2).reshape(P, NT * CP), cmp_t], axis=1).astype(np.float32)

    def held(dist):
        return sum(((dist >= 0) & (dist % r == 0) & (dist <= w)).astype(np.int64) for w, r in ((128, 1), (512, 4), (2048, 16)))

    tiles = np.arange(NT)
    by_q = held(q[:, None] - k[:, None] + P * (NT - 1 - tiles)[None, :, None])
    by_k = held(k[:, None] - q[:, None] + P * tiles[None, :, None])
    dil_log = np.stack([np.where(n > 0, np.log(np.maximum(n, 1)), NEG).reshape(P, T) for n in (by_q, by_k)]).astype(np.float32)

    def keys(at, branch):
        local, tile = at % P, at // P
        one = (tile[None, :] == np.arange(NT)[:, None]).astype(np.float32)
        ones = np.ones((2, at.size))
        rows = np.zeros((MROW + 2 * KBR - DH, at.size))
        rows[:AUG] = np.concatenate([ones, np.stack([local, local]), one, one])
        rows[MROW - DH + 2 * branch:MROW - DH + 2 * branch + 2] = 1.0
        return rows.astype(np.float32)

    def cut(a):
        a = a.astype(np.float32)
        hi = ((a.view(np.uint32) + 0x800) & np.uint32(0xFFFFF000)).view(np.float32)
        return hi, a - hi

    n_all = 2 * NH
    s = (2.0 ** (-8.0 * np.arange(1, n_all + 1) / n_all)).astype(np.float32)
    tt = np.arange(T)
    rows = []
    for slope in np.concatenate([s[0::2], s[1::2]]):
        a, b = cut(-slope * (tt % P).astype(np.float32))
        c_, d = cut(np.full(T, slope))
        e, f = cut(-slope * (P * (tt[None, :] // P - np.arange(NT)[:, None])).astype(np.float32))
        rows.append(np.concatenate([a[None], b[None], c_[None], d[None], e, f, np.zeros((MROW - DH - AUG, T))]))
    return (np.eye(P, dtype=np.float32), masks, np.stack([keys(tt, 0), keys(tt, 1)]), keys(end, 2), np.stack(rows).astype(np.float32),
            np.stack(cut(dil_log)))


def kernel(**inputs):
    import numpy as _np
    import concourse.bacc as _bacc
    from concourse import mybir as _mybir
    from concourse.bass_utils import run_bass_kernel_spmd as _run

    nc = _bacc.Bacc("TRN2", target_bir_lowering=False, num_devices=1)
    arrays, args = {}, []
    given = [(name, _np.ascontiguousarray(inputs[name])) for name in _INS]
    given += list(zip(("ident", "masks", "kaug", "kaug_cmp", "qaug", "dil_log"), constants()))
    for name, a in given:
        arrays[f"in_{name}_dram"] = a
        args.append(nc.dram_tensor(f"in_{name}_dram", a.shape, _mybir.dt.from_np(a.dtype), kind="ExternalInput").ap())
    args.append(nc.dram_tensor("out_0_dram", (1, T, D), _mybir.dt.float32, kind="ExternalOutput").ap())
    program(nc, *args)
    r = _run(nc, [arrays], core_ids=[0])
    return r.results[0]["out_0_dram"]
```

```python
import concourse.bass as bass
from concourse import mybir
from contextlib import ExitStack

P = 128
D = 1024
T = 1024
NT = T // P
KT = D // P
DH = 64
NH = 8
NG = 2
HPG = NH // NG
CMP_BLOCK, CMP_STRIDE = 32, 16
NCMP = (T - CMP_BLOCK) // CMP_STRIDE + 1
CP = 64
WIN_TILES = 512 // P
AUG = 20
MROW = 96
KBR = 3
VS = 2 * DH
LOG_DEGREE = 8
NEAR = 5
NEG = -1.0e38
FLOOR = -1.0e37
EPS = 1e-6

C_Q, C_KCMP, C_VCMP, C_KSLC, C_VSLC, C_KWIN, C_VWIN = 0, 512, 640, 768, 896, 1024, 1152
C_GATE, C_ZN, C_DQ, C_DK, C_DV, C_ZD, C_MG = 1280, 1304, 1816, 2328, 2840, 3352, 3864
NGATE = 3 * NH

U_KSLC, U_KWIN, U_Q, U_DQ, U_DK = 0, 1, 2, 6, 10
NUNIT = 14


def program(nc, x, norm_g, w_in, pos_k, w1_k, w2_k, pos_v, w1_v, w2_v, w_br_nsa, w_br_dil, w_out, final_g,
            ident_in, masks_in, kaug_in, kaug_cmp_in, qaug_in, dil_log_in, out):
    f32, r32, b16 = mybir.dt.float32, mybir.dt.float32r, mybir.dt.bfloat16
    ALU, ACT, AX = mybir.AluOpType, mybir.ActivationFunctionType, mybir.AxisListType

    import numpy as np

    LN2 = float(np.log(2.0))
    LOG_POLY = [float(c) for c in np.polynomial.chebyshev.Chebyshev.interpolate(
        lambda u: np.log(1.5 + u), LOG_DEGREE, domain=[-0.5, 0.5]).convert(kind=np.polynomial.Polynomial).coef]

    w_in_v = w_in[0].rearrange("(k p) c -> p k c", p=P)
    x_v = x[0].rearrange("(n p) d -> n p d", p=P)
    out_v = out[0].rearrange("(n p) d -> n p d", p=P)

    qk_hi = nc.dram_tensor("qk_hi", (NUNIT, P, T), f32, kind="Internal").ap()
    qk_lo = nc.dram_tensor("qk_lo", (NUNIT, P, T), f32, kind="Internal").ap()
    v_dil = nc.dram_tensor("v_dil", (T, NH, 2, DH), f32, kind="Internal").ap()

    kaug = nc.dram_tensor("kaug", (2, MROW + 2 * KBR - DH, T), f32, kind="Internal").ap()
    qaug = nc.dram_tensor("qaug", (2 * NH, MROW - DH, T), f32, kind="Internal").ap()
    dil_log = nc.dram_tensor("dil_log", (2, 2, P, T), f32, kind="Internal").ap()

    top = ExitStack()
    with top:
        def sbuf(ctx, name, shape, dt=f32):
            return ctx.enter_context(nc.sbuf_tensor(name, shape, dt))

        def sem(ctx, name):
            return ctx.enter_context(nc.semaphore(name))

        ps = top.enter_context(nc.psum_tensor("ps", [P, 4, 1024], f32))
        psf = ps[:, :, :].rearrange("p s c -> p (s c)")

        ident = sbuf(top, "ident", [P, P])
        identb = sbuf(top, "identb", [P, P], b16)
        identr = sbuf(top, "identr", [P, P], r32)
        o_nsa = sbuf(top, "o_nsa", [P, NH // 2, T])
        xh = sbuf(top, "xh", [P, KT, T], r32)
        xl = sbuf(top, "xl", [P, KT, T], r32)

        LOG_STEPS = (6, LOG_DEGREE + 2)

        def log_step(dve, done, count, need, op, *args):
            if need:
                dve.wait_ge(done, count + need)
            op(*args).then_inc(done, 1)

        def log_parts(dve, dst, src, tmp, least, done, base):
            a, u, c, _ = tmp
            bits = mybir.dt.int32
            log_step(dve, done, base, 0, nc.vector.tensor_scalar, a, src, least, None, ALU.max)
            log_step(dve, done, base, 1, nc.vector.tensor_scalar, u.bitcast(bits), a.bitcast(bits), 0x7FFFFF, 0x3F800000,
                     ALU.bitwise_and, ALU.bitwise_or)
            log_step(dve, done, base, 1, nc.vector.tensor_scalar, c.bitcast(bits), a.bitcast(bits), 23, None, ALU.logical_shift_right)
            log_step(dve, done, base, 2, nc.vector.tensor_scalar, u, u, -1.5, None, ALU.add)
            log_step(dve, done, base, 3, nc.vector.tensor_scalar, dst, c.bitcast(bits), -127.0, LN2, ALU.add, ALU.mult)
            log_step(dve, done, base, 4, nc.vector.tensor_tensor, a, u, u, ALU.mult)

        def log_polynomial(dve, dst, tmp, done, base):
            square, u, even, odd = tmp
            log_step(dve, done, base, 6, nc.vector.tensor_scalar, even, square, LOG_POLY[LOG_DEGREE], None, ALU.mult)
            log_step(dve, done, base, 6, nc.vector.tensor_scalar, odd, square, LOG_POLY[LOG_DEGREE - 1], None, ALU.mult)
            need = 7
            for k in range(LOG_DEGREE - 2, 0, -2):
                log_step(dve, done, base, need, nc.vector.scalar_tensor_tensor, even, even, LOG_POLY[k], square, ALU.add, ALU.mult)
                log_step(dve, done, base, need + 1, nc.vector.scalar_tensor_tensor, odd, odd, LOG_POLY[k - 1], square if k > 2 else u,
                         ALU.add, ALU.mult)
                need += 2
            log_step(dve, done, base, need, nc.vector.scalar_tensor_tensor, dst, even, LOG_POLY[0], dst, ALU.add, ALU.add)
            log_step(dve, done, base, need + 2, nc.vector.tensor_tensor, dst, odd, dst, ALU.add)

        shared = [sbuf(top, f"shared{i}", [P, T], r32) for i in range(4)]
        shared_w = [t[:, :].rearrange("p (k c) -> p k c", k=KT) for t in shared]
        s_first = {kind: sem(top, f"s_first_{kind}") for kind in ("nsa", "dil")}

        def load_first(sp, kind):
            rows = slice(0, DH)
            q, k = (U_Q, U_KSLC) if kind == "nsa" else (U_DQ, U_DK)
            qa, qb, ka, kb = shared
            for dst, given in ((qa[0:DH, :], qk_hi[q, rows, :]), (qb[0:DH, :], qk_hi[q, rows, :]), (qa[DH:P, :], qk_lo[q, rows, :]),
                               (qb[DH:MROW, :], qaug[0 if kind == "nsa" else NH]),
                               (ka[0:DH, :], qk_hi[k, rows, :]), (ka[DH:P, :], qk_hi[k, rows, :]), (kb[0:DH, :], qk_lo[k, rows, :]),
                               (kb[DH:MROW + 2 * KBR, :], kaug[0])):
                sp.dma_start(dst.bitcast(f32), given).then_inc(s_first[kind], 16)

        scope_v = ExitStack()
        masks = sbuf(scope_v, "masks", [P, 2 * P + NT * CP], b16)
        m_diag, m_win, m_cmp = masks[:, 0:P], masks[:, P:2 * P], masks[:, 2 * P:]
        v_nsa = sbuf(scope_v, "v_nsa", [P, NT, 2, NG, VS], r32)
        lgate = sbuf(scope_v, "lgate", [P, NT, KBR, NH])
        kc = sbuf(scope_v, "kc", [P, NG, 2, CP], r32)
        vc = sbuf(scope_v, "vc", [CP, NG, VS], r32)
        scope = ExitStack()
        NRAW = 3
        raw = [sbuf(scope, f"raw{i}", [P, KT * P]) for i in range(NRAW)]
        wth, wtl = shared_w[0:2], shared_w[2:4]
        wnh = sbuf(scope, "wnh", [P, KT, 512], r32)
        wnl = sbuf(scope, "wnl", [P, KT, 512], r32)
        evh = [sbuf(scope, f"evh{i}", [P, T], r32) for i in range(2)]
        evl = [sbuf(scope, f"evl{i}", [P, T], r32) for i in range(2)]
        src = sbuf(scope, "src", [P, 2, T])
        srcb = sbuf(scope, "srcb", [P, CMP_BLOCK, CP])
        w1bd = o_nsa[:, :, :].rearrange("p n (a e) -> p (n a) e", e=P)
        w2bd = sbuf(scope, "w2bd", [P, 2, P])
        posT = sbuf(scope, "posT", [P, 2, CMP_BLOCK])
        hid = sbuf(scope, "hid", [P, 2, CP])
        cth = sbuf(scope, "cth", [P, CP], r32)
        ctl = sbuf(scope, "ctl", [P, CP], r32)
        gates = sbuf(scope, "gates", [P, NT, NGATE])
        lg_tmp = [sbuf(scope, f"lg_tmp{i}", [P, NT, NGATE]) for i in range(4)]
        gel = sbuf(scope, "gel", [P, 3, CP])
        NXT = 4
        xt = [t.rearrange("p a b -> p (a b)") for t in (srcb[:, 0:16, :], srcb[:, 16:32, :], w1bd[:, 16:24, :], w1bd[:, 24:32, :])]
        xn = [src[:, 0, :], src[:, 1, :]]
        gb = w1bd[:, 0:8, :].rearrange("p a b -> p (a b)")
        junk = w1bd[:, 8:16, :].rearrange("p a b -> p (a b)")
        stat = sbuf(scope, "stat", [P, 4, NT])

        TU = [(C_KCMP, "src0"), (C_VCMP, "src1"), (C_KSLC, U_KSLC), (C_KWIN, U_KWIN)]
        TU += [(C_Q + P * i, U_Q + i) for i in range(4)]
        TD = [(C_DQ + P * i, U_DQ + i) for i in range(4)] + [(C_DK + P * i, U_DK + i) for i in range(4)]
        PLAN = [("t",) + u for u in TU[0:4]] + [("c", 0)] + [("t",) + TU[4]] + [("c", 1)] + [("t",) + TU[5]]
        PLAN += [("c", 2)] + [("t",) + TU[6]] + [("c", 3)] + [("t",) + TU[7]] + [("n", 0)]
        PLAN += [("t",) + u for u in TD] + [("n", 1)]
        NPIECE = {"t": 1, "n": 4, "c": 0}
        NUSE = {"t": 1, "n": NT, "c": 1}
        piece0, use0, tun, spill, a, b, c, d = [], [], [], [], 0, NT, 0, 0
        for step in PLAN:
            piece0.append(a)
            use0.append(b)
            tun.append(c)
            spill.append(d)
            a += NPIECE[step[0]]
            b += NUSE[step[0]]
            c += step[0] == "t"
            d += (step[0] == "t" and not isinstance(step[2], str)) or (step[0] == "n" and step[1] == 1) * NT

        def nwidth(which):
            return 256 + NGATE if which == 0 else 512

        s_const = sem(scope, "s_const")
        s_copy = sem(scope, "s_copy")
        s_aug = sem(scope, "s_aug")
        s_x = [sem(scope, f"s_x{i}") for i in range(NXT)]
        s_raw = [sem(scope, f"s_raw{i}") for i in range(NRAW)]
        s_w1 = sem(scope, "s_w1")
        s_cst = sem(scope, "s_cst")
        s_sq, s_ms, s_rt, s_ri, s_xs, s_xn = (sem(scope, n) for n in ("s_sq", "s_ms", "s_rt", "s_ri", "s_xs", "s_xn"))
        s_zero = sem(scope, "s_zero")
        s_blk = sem(scope, "s_blk")
        s_whi, s_wlo = sem(scope, "s_whi"), sem(scope, "s_wlo")
        s_mm = sem(scope, "s_mm")
        s_hi, s_lo = sem(scope, "s_hi"), sem(scope, "s_lo")
        s_sp = [sem(scope, f"s_sp{i}") for i in range(2)]
        s_kc = sem(scope, "s_kc")
        s_gel, s_tanh, s_hid = sem(scope, "s_gel"), sem(scope, "s_tanh"), sem(scope, "s_hid")
        s_pos = sem(scope, "s_pos")
        s_gate, s_log = sem(scope, "s_gate"), sem(scope, "s_log")

        block = nc.Block()
        with block:
            def words(ap):
                return ap.bitcast(f32)

            def pieces(i):
                step = PLAN[i]
                if step[0] == "t":
                    yield w_in_v[:, :, step[1]:step[1] + P], 0
                elif step[0] == "n":
                    for q in range(4):
                        yield step[1], q

            PIECES = [(step, piece) for i, step in enumerate(PLAN) for piece in pieces(i)]
            EARLY_AT = {NT - 4: 0, NT - 3: 1}

            @block.sync
            def _(sp):
                def load_piece(p):
                    step, (view, q) = PIECES[p]
                    if p >= NRAW:
                        sp.wait_ge(s_wlo, p - NRAW + 1)
                    if step[0] == "t":
                        sp.dma_start(raw[p % NRAW][:, :].rearrange("p (k c) -> p k c", k=KT), view).then_inc(s_raw[p % NRAW], 16)
                    elif step[1] == 1:
                        sp.dma_start(raw[p % NRAW][:, :].rearrange("p (k c) -> p k c", k=2),
                                     w_in_v[:, 2 * q:2 * q + 2, C_DV:C_DV + 512]).then_inc(s_raw[p % NRAW], 16)
                    else:
                        dst = raw[p % NRAW][:, 0:2 * nwidth(0)].rearrange("p (k c) -> p k c", k=2)
                        sp.dma_start(dst[:, :, 0:P], w_in_v[:, 2 * q:2 * q + 2, C_VSLC:C_VSLC + P]).then_inc(s_raw[p % NRAW], 16)
                        sp.dma_start(dst[:, :, P:], w_in_v[:, 2 * q:2 * q + 2, C_VWIN:C_VWIN + P + NGATE]).then_inc(s_raw[p % NRAW], 16)

                for n in range(NT):
                    if n >= NXT:
                        sp.wait_ge(s_xn, n - NXT + 1)
                    sp.dma_start(xt[n % NXT], x_v[n]).then_inc(s_x[n % NXT], 16)
                    if n == 0:
                        sp.dma_start(gb[:, :], norm_g[0:1, :].partition_broadcast(P)).then_inc(s_const, 16)
                        sp.dma_start(ident[:, :], ident_in).then_inc(s_const, 16)
                    if 3 <= n <= 4:
                        load_piece(n - 3)
                for i, pos in enumerate((pos_k, pos_v)):
                    for g in range(NG):
                        with nc.allow_non_contiguous_dma(reason="positions, transposed, once"):
                            sp.dma_start(posT[g * DH:(g + 1) * DH, i, :], pos[0].rearrange("l d -> d l")).then_inc(s_pos, 16)
                for p in range(2, len(PIECES)):
                    load_piece(p)
                sp.wait_ge(s_mm, use0[-2] + 1)
                sp.wait_ge(s_copy, 48)
                for b in range(2):
                    sp.wait_ge(s_sp[b], 16 * spill[-1])
                load_first(sp, "nsa")
                sp.wait_ge(s_first["nsa"], 16 * 8)

            def raw_count(p):
                count = 0
                for i, step in enumerate(PLAN):
                    for q in range(NPIECE[step[0]]):
                        if (piece0[i] + q) % NRAW == p % NRAW:
                            count += 32 if step == ("n", 0) else 16
                        if piece0[i] + q == p:
                            return count

            def halves(i, buf_t, buf_n, q):
                step = PLAN[i]
                p = piece0[i] + q
                if step[0] == "t":
                    return raw[p % NRAW][:, :], buf_t[tun[i] % 2][:, :, :].rearrange("p k c -> p (k c)")
                w = nwidth(step[1])
                return raw[p % NRAW][:, 0:2 * w].rearrange("p (k c) -> p k c", k=2), buf_n[:, 2 * q:2 * q + 2, 0:w]

            @block.gpsimd
            def _(pool):
                pool.dma_start(masks[:, :], masks_in).then_inc(s_aug, 16)
                pool.dma_start(identr[:, :], ident_in).then_inc(s_aug, 16)
                for g in range(NG):
                    pool.dma_start(kc[DH:MROW + 2 * KBR, g, 1, :], kaug_cmp_in).then_inc(s_aug, 16)
                pool.memset(w2bd[:, :, :], 0.0).then_inc(s_zero, 1)
                pool.wait_ge(s_zero, 1)
                for i, w2 in enumerate((w2_k, w2_v)):
                    for g in range(NG):
                        pool.dma_start(w2bd[g * DH:(g + 1) * DH, i, g * DH:(g + 1) * DH], w2[0]).then_inc(s_w1, 16)
                pool.wait_ge(s_xn, NT)
                pool.memset(w1bd[:, :, :], 0.0).then_inc(s_zero, 1)
                pool.wait_ge(s_zero, 2)
                for g in range(NG):
                    pool.dma_start(w1bd[g * DH:(g + 1) * DH, :, g * DH:(g + 1) * DH],
                                   w1_k[0].rearrange("l d e -> d l e")).then_inc(s_w1, 16)
                for copy, given in ((kaug, kaug_in), (qaug, qaug_in), (dil_log, dil_log_in)):
                    pool.dma_start(copy, given).then_inc(s_copy, 16)
                ns = 0
                for i, step in enumerate(PLAN):
                    if step[0] == "t" and not isinstance(step[2], str):
                        pool.wait_ge(s_lo, use0[i] + 1)
                        pool.dma_start(qk_hi[step[2]], words(evh[ns % 2][:, :])).then_inc(s_sp[ns % 2], 16)
                        pool.dma_start(qk_lo[step[2]], words(evl[ns % 2][:, :])).then_inc(s_sp[ns % 2], 16)
                        ns += 1
                    if step == ("n", 1):
                        for n in range(NT):
                            pool.wait_ge(s_lo, use0[i] + n + 1)
                            pool.dma_start(v_dil[n * P:(n + 1) * P, :, 0, :],
                                           words(evh[ns % 2][:, 0:512]).rearrange("p (h d) -> p h d", d=DH)).then_inc(s_sp[ns % 2], 16)
                            pool.dma_start(v_dil[n * P:(n + 1) * P, :, 1, :],
                                           words(evl[ns % 2][:, 0:512]).rearrange("p (h d) -> p h d", d=DH)).then_inc(s_sp[ns % 2], 16)
                            ns += 1
                    if step == ("c", 0):
                        pool.wait_ge(s_mm, use0[i] + 1)
                        for g in range(NG):
                            pool.dma_start(w1bd[g * DH:(g + 1) * DH, :, g * DH:(g + 1) * DH],
                                           w1_v[0].rearrange("l d e -> d l e")).then_inc(s_w1, 16)
                    if step == ("c", 1):
                        pool.wait_ge(s_lo, use0[i] + 1)
                        for g in range(NG):
                            for r in range(2):
                                pool.dma_start(words(kc[r * DH:(r + 1) * DH, g, 0, :]), words(cth[g * DH:(g + 1) * DH, :])).then_inc(s_kc, 16)
                            pool.dma_start(words(kc[0:DH, g, 1, :]), words(ctl[g * DH:(g + 1) * DH, :])).then_inc(s_kc, 16)
                pool.wait_ge(s_sp[0], 16 * ns)
                pool.wait_ge(s_sp[1], 16 * ns)
                pool.wait_ge(s_kc, 96)
                pool.wait_ge(s_aug, 64)
                pool.wait_ge(s_copy, 48)

            @block.scalar
            def _(act):
                act.wait_ge(s_const, 16 * 2)
                nc.scalar.activation(identb[:, :], ident[:, :], ACT.Copy).then_inc(s_cst, 1)

                def sumsq(n):
                    act.wait_ge(s_x[n % NXT], 16 * (n // NXT + 1))
                    if n:
                        act.wait_ge(s_sq, n)
                    nc.scalar.activation(junk, xt[n % NXT], ACT.Square, accum_out=stat[:, 0, n:n + 1]).then_inc(s_sq, 1)
                    act.wait_ge(s_ms, n + 1)
                    nc.scalar.activation(stat[:, 2, n:n + 1], stat[:, 1, n:n + 1], ACT.Sqrt).then_inc(s_rt, 1)

                def split(i):
                    step = PLAN[i]
                    for q in range(NPIECE[step[0]]):
                        p = piece0[i] + q
                        act.wait_ge(s_raw[p % NRAW], raw_count(p))
                        if step[0] == "t" and tun[i] >= 2:
                            before = max(j for j in range(i) if PLAN[j][0] == "t" and tun[j] == tun[i] - 2)
                            act.wait_ge(s_mm, use0[before] + 1)
                        if step == ("n", 1):
                            act.wait_ge(s_mm, use0[PLAN.index(("n", 0))] + NT)
                        s, h = halves(i, wth, wnh, q)
                        nc.scalar.activation(h, s, ACT.Copy).then_inc(s_whi, 1)

                for n in range(NT + 1):
                    if n < NT:
                        sumsq(n)
                    if n:
                        act.wait_ge(s_mm, n)
                        nc.scalar.activation(xh[:, :, (n - 1) * P:n * P], ps[:, (n - 1) % 4, :].rearrange("p (k t) -> p k t", k=KT),
                                             ACT.Copy).then_inc(s_hi, 1)
                    if n in EARLY_AT:
                        split(EARLY_AT[n])

                def evict(i):
                    step = PLAN[i]
                    if step[0] == "t" and not isinstance(step[2], str):
                        scaled = step[2] in range(U_Q, U_Q + 4) or step[2] in range(U_DQ, U_DQ + 4)
                        u, e = use0[i], spill[i]
                        act.wait_ge(s_mm, u + 1)
                        if e >= 2:
                            act.wait_ge(s_sp[e % 2], 32 * (e // 2))
                        nc.scalar.activation(evh[e % 2][:, :], ps[:, u % 4, :], ACT.Copy,
                                             scale=DH ** -0.5 if scaled else 1.0).then_inc(s_hi, 1)
                    elif step[0] == "t":
                        act.wait_ge(s_mm, use0[i] + 1)
                        nc.scalar.activation(src[:, int(step[2][3]), :], ps[:, use0[i] % 4, :], ACT.Copy).then_inc(s_hi, 1)
                    elif step[0] == "n":
                        for n in range(NT):
                            u = use0[i] + n
                            act.wait_ge(s_mm, u + 1)
                            if step[1] == 0:
                                nc.scalar.activation(gates[:, n, 0:2 * NH], ps[:, u % 4, 256 + NH:256 + NGATE], ACT.Sigmoid).then_inc(s_gate, 1)
                                nc.scalar.activation(gates[:, n, 2 * NH:NGATE], ps[:, u % 4, 256:256 + NH], ACT.Sigmoid).then_inc(s_gate, 1)
                                nc.scalar.activation(v_nsa[:, n, :, :, 0:DH].rearrange("p a g d -> p (a g) d"),
                                                     ps[:, u % 4, 0:256].rearrange("p (a d) -> p a d", d=DH), ACT.Copy).then_inc(s_hi, 1)
                            else:
                                e = spill[i] + n
                                act.wait_ge(s_sp[e % 2], 32 * (e // 2))
                                nc.scalar.activation(evh[e % 2][:, 0:512], ps[:, u % 4, 0:512], ACT.Copy).then_inc(s_hi, 1)
                    else:
                        u, c = use0[i], step[1]
                        act.wait_ge(s_mm, u + 1)
                        if c % 2 == 0:
                            if c:
                                act.wait_ge(s_hid, 1)
                            nc.scalar.activation(gel[:, 0, :], ps[:, u % 4, 0:CP], ACT.Copy).then_inc(s_hi, 1)
                            act.wait_ge(s_gel, 2 * c + 3)
                            nc.scalar.activation(gel[:, 2, :], gel[:, 1, :], ACT.Tanh, scale=(2.0 / np.pi) ** 0.5).then_inc(s_tanh, 1)
                        elif c == 1:
                            nc.scalar.activation(cth[:, :], ps[:, u % 4, 0:CP], ACT.Copy).then_inc(s_hi, 1)
                        else:
                            nc.scalar.activation(vc[:, :, 0:DH], ps[0:DH, u % 4, 0:P].rearrange("p (g d) -> p g d", g=NG),
                                                 ACT.Copy).then_inc(s_hi, 1)

                for i in range(len(PLAN)):
                    if 1 < i + 1 < len(PLAN) and PLAN[i + 1][0] != "c":
                        split(i + 1)
                    evict(i)

            @block.vector
            def _(dve):
                dve.wait_ge(s_const, 16 * 2)

                def split(i):
                    for q in range(NPIECE[PLAN[i][0]]):
                        p = piece0[i] + q
                        dve.wait_ge(s_whi, p + 1)
                        s, h = halves(i, wth, wnh, q)
                        _, l = halves(i, wtl, wnl, q)
                        nc.vector.tensor_tensor(l, s, h.bitcast(f32), ALU.subtract).then_inc(s_wlo, 1)

                for n in range(NT + 1):
                    if n < NT:
                        dve.wait_ge(s_sq, n + 1)
                        nc.vector.tensor_scalar(stat[:, 1, n:n + 1], stat[:, 0, n:n + 1], 1.0 / D, EPS, ALU.mult, ALU.add).then_inc(s_ms, 1)
                        dve.wait_ge(s_rt, n + 1)
                        nc.vector.reciprocal(stat[:, 3, n:n + 1], stat[:, 2, n:n + 1]).then_inc(s_ri, 1)
                        dve.wait_ge(s_ri, n + 1)
                        if n >= 2:
                            dve.wait_ge(s_mm, n - 1)
                        nc.vector.scalar_tensor_tensor(xn[n % 2], xt[n % NXT], stat[:, 3, n:n + 1], gb[:, :], ALU.mult, ALU.mult).then_inc(s_xn, 1)
                    if n:
                        dve.wait_ge(s_hi, n)
                        nc.vector.tensor_tensor(xl[:, :, (n - 1) * P:n * P], ps[:, (n - 1) % 4, :].rearrange("p (k t) -> p k t", k=KT),
                                                xh[:, :, (n - 1) * P:n * P].bitcast(f32), ALU.subtract).then_inc(s_lo, 1)
                    if n in EARLY_AT:
                        split(EARLY_AT[n])

                def evict(i):
                    step = PLAN[i]
                    if step[0] == "t" and not isinstance(step[2], str):
                        scaled = step[2] in range(U_Q, U_Q + 4) or step[2] in range(U_DQ, U_DQ + 4)
                        u, e = use0[i], spill[i]
                        dve.wait_ge(s_hi, u + 1)
                        nc.vector.scalar_tensor_tensor(evl[e % 2][:, :], ps[:, u % 4, :], DH ** -0.5 if scaled else 1.0,
                                                       evh[e % 2][:, :].bitcast(f32), ALU.mult, ALU.subtract).then_inc(s_lo, 1)
                    elif step[0] == "t":
                        dve.wait_ge(s_hi, use0[i] + 1)
                        dve.wait_ge(s_lo, use0[i])
                        dve.sem_inc(s_lo, 1)
                    elif step[0] == "n":
                        for n in range(NT):
                            u = use0[i] + n
                            dve.wait_ge(s_hi, u + 1)
                            if step[1] == 0:
                                nc.vector.tensor_tensor(v_nsa[:, n, :, :, DH:VS].rearrange("p a g d -> p (a g) d"),
                                                        ps[:, u % 4, 0:256].rearrange("p (a d) -> p a d", d=DH),
                                                        v_nsa[:, n, :, :, 0:DH].bitcast(f32).rearrange("p a g d -> p (a g) d"),
                                                        ALU.subtract).then_inc(s_lo, 1)
                            else:
                                e = spill[i] + n
                                nc.vector.tensor_tensor(evl[e % 2][:, 0:512], ps[:, u % 4, 0:512],
                                                        evh[e % 2][:, 0:512].bitcast(f32), ALU.subtract).then_inc(s_lo, 1)
                    else:
                        u, c = use0[i], step[1]
                        dve.wait_ge(s_hi, u + 1)
                        if c % 2 == 0:
                            dve.wait_ge(s_lo, u)
                            dve.sem_inc(s_lo, 1)
                            x0, x1, th, g0 = gel[:, 0, :], gel[:, 1, :], gel[:, 2, :], 2 * c
                            nc.vector.tensor_tensor(x1, x0, x0, ALU.mult).then_inc(s_gel, 1)
                            dve.wait_ge(s_gel, g0 + 1)
                            nc.vector.tensor_scalar(x1, x1, 0.044715, 1.0, ALU.mult, ALU.add).then_inc(s_gel, 1)
                            dve.wait_ge(s_gel, g0 + 2)
                            nc.vector.tensor_tensor(x1, x1, x0, ALU.mult).then_inc(s_gel, 1)
                            dve.wait_ge(s_tanh, c // 2 + 1)
                            nc.vector.scalar_tensor_tensor(th, th, 1.0, x0, ALU.add, ALU.mult).then_inc(s_gel, 1)
                            dve.wait_ge(s_gel, g0 + 4)
                            nc.vector.tensor_scalar(hid[:, c // 2, :], th, 0.5, None, ALU.mult).then_inc(s_hid, 1)
                        elif c == 1:
                            nc.vector.tensor_tensor(ctl[:, :], ps[:, u % 4, 0:CP], cth[:, :].bitcast(f32), ALU.subtract).then_inc(s_lo, 1)
                        else:
                            nc.vector.tensor_tensor(vc[:, :, DH:VS], ps[0:DH, u % 4, 0:P].rearrange("p (g d) -> p g d", g=NG),
                                                    vc[:, :, 0:DH].bitcast(f32), ALU.subtract).then_inc(s_lo, 1)

                def blocks(c):
                    if c == 1:
                        dve.wait_ge(s_mm, use0[PLAN.index(("c", 0))] + 1)
                    if c == 0:
                        dve.wait_ge(s_pos, 64)
                        dve.wait_ge(s_hi, use0[1] + 1)
                    a = src[:, c, :].rearrange("p (n s) -> p s n", s=CMP_STRIDE)
                    for r in range(2):
                        nc.vector.tensor_tensor(srcb[:, r * CMP_STRIDE:(r + 1) * CMP_STRIDE, 0:NCMP], a[:, :, r:r + NCMP],
                                                posT[:, c, r * CMP_STRIDE:(r + 1) * CMP_STRIDE].unsqueeze(2).to_broadcast([P, CMP_STRIDE, NCMP]),
                                                ALU.add).then_inc(s_blk, 1)

                for i in range(len(PLAN)):
                    if 1 < i + 1 < len(PLAN) and PLAN[i + 1][0] != "c":
                        split(i + 1)
                    if i == 1:
                        nc.vector.memset(srcb[:, :, NCMP:CP], 0.0).then_inc(s_blk, 1)
                        blocks(0)
                    evict(i)
                    if PLAN[i] == ("c", 0):
                        blocks(1)
                    if PLAN[i] == ("n", 0):
                        dve.wait_ge(s_gate, 2 * NT)
                        log, tmp = lgate[:, :, :, :].rearrange("p n b h -> p (n b h)"), [t[:, :, :].rearrange("p n c -> p (n c)") for t in lg_tmp]
                        log_parts(dve, log, gates[:, :, :].rearrange("p n c -> p (n c)"), tmp, 1e-37, s_log, 0)
                        log_polynomial(dve, log, tmp, s_log, 0)

            @block.tensor
            def _(pe):
                pe.wait_ge(s_const, 16 * 2)

                def slot_free(u):
                    if u >= 4:
                        pe.wait_ge(s_lo, u - 3)

                def half_unit(i, half, ks):
                    u, w = use0[i], tun[i] % 2
                    cols = slice(half * 512, half * 512 + 512)
                    slot_free(u)
                    pe.wait_ge(s_wlo, piece0[i] + 1)
                    for k in ks:
                        nc.tensor.matmul(ps[:, u % 4, cols], wth[w][:, k, :], xh[:, k, cols], start=(k == 0), stop=False)
                        nc.tensor.matmul(ps[:, u % 4, cols], wth[w][:, k, :], xl[:, k, cols], start=False, stop=False)
                        last = nc.tensor.matmul(ps[:, u % 4, cols], wtl[w][:, k, :], xh[:, k, cols], start=False, stop=(k == KT - 1))
                    return last

                for n in range(NT):
                    slot_free(n)
                    pe.wait_ge(s_xn, n + 1)
                    for k in range(KT):
                        last = nc.tensor.transpose(ps[:, n % 4, k * P:(k + 1) * P], xn[n % 2][:, k * P:(k + 1) * P], ident[:, :])
                    last.then_inc(s_mm, 1)
                    if n == NT - 3:
                        half_unit(0, 0, range(0, KT // 2))
                    elif n == NT - 2:
                        half_unit(0, 0, range(KT // 2, KT))
                    elif n == NT - 1:
                        half_unit(1, 0, range(KT))
                pe.wait_ge(s_lo, NT)
                for i, step in enumerate(PLAN):
                    if step[0] == "t":
                        for half in range(1 if i < 2 else 0, 2):
                            last = half_unit(i, half, range(KT))
                        last.then_inc(s_mm, 1)
                    elif step[0] == "n":
                        pe.wait_ge(s_wlo, piece0[i] + 4)
                        w = nwidth(step[1])
                        for n in range(NT):
                            u = use0[i] + n
                            slot_free(u)
                            rows = slice(n * P, n * P + P)
                            for k in range(KT):
                                nc.tensor.matmul(ps[:, u % 4, 0:w], xh[:, k, rows], wnh[:, k, 0:w], start=(k == 0), stop=False)
                                nc.tensor.matmul(ps[:, u % 4, 0:w], xh[:, k, rows], wnl[:, k, 0:w], start=False, stop=False)
                                last = nc.tensor.matmul(ps[:, u % 4, 0:w], xl[:, k, rows], wnh[:, k, 0:w], start=False, stop=(k == KT - 1))
                            last.then_inc(s_mm, 1)
                    else:
                        u, c = use0[i], step[1]
                        slot_free(u)
                        if c % 2 == 0:
                            pe.wait_ge(s_w1, 16 * 6 + 32 * (c // 2))
                            pe.wait_ge(s_blk, 3 + c)
                            for l in range(CMP_BLOCK):
                                last = nc.tensor.matmul(ps[:, u % 4, 0:CP], w1bd[:, l, :], srcb[:, l, :], start=(l == 0), stop=(l == CMP_BLOCK - 1))
                        else:
                            pe.wait_ge(s_hid, (c + 1) // 2)
                            if c == 1:
                                last = nc.tensor.matmul(ps[:, u % 4, 0:CP], w2bd[:, 0, :], hid[:, 0, :], start=True, stop=True)
                            else:
                                last = nc.tensor.matmul(ps[0:CP, u % 4, 0:P], hid[:, 1, :], w2bd[:, 1, :], start=True, stop=True)
                        last.then_inc(s_mm, 1)
        scope.close()

        def attention(kind, o_t):
            nsa = kind == "nsa"
            scope = ExitStack()
            NHL = 4
            NPR = 3
            NBK = 6
            NQB = 3 if nsa else 2
            LAG = 4
            AFTER_M = 3
            LEAD, TAIL, EARLY = (0, 5, 5) if nsa else (1, 4, 0)
            nbr = 3 if nsa else 1
            LOG = sum(LOG_STEPS) + nsa
            SPL = 3 + nsa
            krows = MROW + 2 * nbr
            qa = [shared[0]] + [sbuf(scope, f"{kind}_qa{i}", [P, T], r32) for i in range(1, NQB)]
            qb = [shared[1]] + [sbuf(scope, f"{kind}_qb{i}", [P, T], r32) for i in range(1, NQB)]
            nk = 4 if nsa else 2
            ka = [shared[2]] + [sbuf(scope, f"{kind}_ka{i}", [P, T], r32) for i in range(1, nk)]
            kb = [shared[3]] + [sbuf(scope, f"{kind}_kb{i}", [P, T], r32) for i in range(1, nk)]
            prob = [sbuf(scope, f"{kind}_prob{i}", [P, T]) for i in range(NPR)]
            ph = [sbuf(scope, f"{kind}_ph{i}", [P, T], r32) for i in range(NHL)]
            pl = [sbuf(scope, f"{kind}_pl{i}", [P, T], r32) for i in range(NHL)]
            res = sbuf(scope, f"{kind}_res", [P, T])
            negm = sbuf(scope, f"{kind}_negm", [P, 2, NT, nbr])
            sums = sbuf(scope, f"{kind}_sums", [P, 2, NT, nbr])
            lsum = sbuf(scope, f"{kind}_lsum", [P, NT * nbr])
            lg_tmp = [sbuf(scope, f"{kind}_lg{i}", [P, NT * nbr]) for i in range(4)]
            negl = sbuf(scope, f"{kind}_negl", [P, NT, nbr])
            negl2 = sbuf(scope, f"{kind}_negl2", [P, NT, 2 * nbr], r32)
            if not nsa:
                vd = [sbuf(scope, f"dil_v{i}", [P, NT, VS], r32) for i in range(2)]
                dlog_h = [sbuf(scope, f"dil_logh{i}", [P, NT * P], r32) for i in range(2)]
                dlog_l = [sbuf(scope, f"dil_logl{i}", [P, NEAR * P], r32) for i in range(2)]
            s_load = [sem(scope, f"{kind}_load{i}") for i in range(NQB)]
            s_vload = [sem(scope, f"{kind}_vload{i}") for i in range(2)]
            s_k = [sem(scope, f"{kind}_k{i}") for i in range(2)]
            s_dlog = [sem(scope, f"{kind}_dlog{i}") for i in range(2)]
            s_kaug = [sem(scope, f"{kind}_kaug{i}") for i in range(2)]
            s_s, s_ra, s_hi, s_lod, s_lop, s_pv, s_max, s_log, s_spl, s_ev, s_add, s_m = (
                sem(scope, f"{kind}_{n}") for n in ("s", "ra", "hi", "lod", "lop", "pv", "max", "log", "spl", "ev", "add", "m"))

            first, second = {}, {}
            P1_ORDER = list(reversed(range(NT)))
            if nsa:
                P2_ORDER = [(2, 0), (0, 0), (0, 2)] + [(0, m) for m in range(3, NT)] + [(1, m) for m in range(4, NT)]
                P2_ORDER += [(1, m) for m in range(4)] + [(0, 1)]
            else:
                P2_ORDER = [0, 3, 5, 6, 7, 4, 2, 1]
            for h in range(NH):
                if nsa:
                    first[h] = [("p1", h, n, br) for n in P1_ORDER for br in (0, 1)]
                    second[h] = [("p2", h, m, br) for br, m in P2_ORDER]
                else:
                    first[h] = [("p1", h, n, 0) for n in P1_ORDER]
                    second[h] = [("p2", h, m, 0) for m in P2_ORDER]
            first[0].sort(key=lambda e: e[3])
            order = first[0] + first[1][:EARLY] + [("m", 0)]
            for h in range(NH):
                a, b, c = second[h], first.get(h + 1, [])[EARLY:], first.get(h + 2, [])[:EARLY]
                spread, done, early = len(a) - LEAD - TAIL, 0, 0
                for j, item in enumerate(a):
                    order.append(item)
                    upto = len(b) * min(max(j + 1 - LEAD, 0), spread) // spread
                    order += b[done:upto]
                    done = upto
                    upto = len(c) * max(j + 1 - LEAD - spread, 0) // TAIL
                    order += c[early:upto]
                    early = upto
                if h + 1 < NH:
                    order.append(("m", h + 1))
            events, waiting = [], []

            def flush(upto, keep=0):
                while len(waiting) > keep and waiting[0][1] <= upto:
                    item = waiting.pop(0)[0]
                    events.append(("v",) + item[1:])
                    if item == second[item[1]][-1]:
                        events.append(("e", item[1]))

            for i, item in enumerate(order):
                if item[0] == "m" and i:
                    flush(len(order) + LAG, AFTER_M)
                events.append(item)
                if item[0] == "m":
                    flush(len(order) + LAG)
                if item[0] == "p2":
                    waiting.append((item, i + LAG))
                flush(i)
            flush(len(order) + LAG)
            items = order
            at = {e: i for i, e in enumerate(items)}
            p2s = [e for e in items if e[0] == "p2"]
            taken_before = {h: sum(e in at for e in events[:events.index(("e", h))]) + 1 for h in range(NH)}
            p2_at = {e: i for i, e in enumerate(p2s)}
            on_pool = [m in ((2, 4, 6), (0, 1, 3, 4, 5, 6, 7), ())[br] for _, _, m, br in p2s]
            act_order = list(range(len(items)))
            for i in range(len(items) - 1):
                if items[i][0] == "p1" and items[i + 1][0] == "p2":
                    act_order[i:i + 2] = [i + 1, i]
            reads, count = {}, 0
            for i in act_order:
                count += 2 if items[i][0] == "p1" and items[i][3] else 1
                reads[i] = count

            def low_done(eng, c):
                if on_pool[c]:
                    eng.wait_ge(s_lop, sum(on_pool[:c + 1]))
                else:
                    eng.wait_ge(s_lod, c + 1 - sum(on_pool[:c + 1]))

            def span(br, m):
                if br == 2:
                    return 0, T
                return m * P, (min(m + WIN_TILES + 1, NT) if br == 1 else NT) * P

            def columns(e):
                if e[0] == "m":
                    return 0, T
                if e[0] == "p2":
                    return span(e[3], e[2])
                return 0, (e[2] + 1) * P if e[3] == 0 else min(e[2] + 1, WIN_TILES + 1) * P + CP

            bank, frees, users, nxt = [], [], {}, 0
            for i, e in enumerate(items):
                lo, hi = columns(e)
                need = (hi - 1) // 512 - lo // 512 + 1
                if nxt + need > NBK:
                    nxt = 0
                bank.append((nxt, lo // 512 * 512))
                before = [users[b] for b in range(nxt, nxt + need) if b in users]
                frees.append(max([reads[j] for j in before], default=0))
                for b in range(nxt, nxt + need):
                    users[b] = i
                nxt = (nxt + need) % NBK

            def scores_at(i, rows, c0, c1):
                b, first_col = bank[i]
                return psf[rows, b * 512 + c0 - first_col:b * 512 + c1 - first_col]

            def banks(lo, hi):
                return [(c, min(c // 512 * 512 + 512, hi)) for c in sorted({lo} | {x for x in (512,) if lo < x < hi})]

            block = nc.Block()
            with block:
                @block.sync
                def _(sp):
                    def keys(i, u, rows, done, aug):
                        sp.dma_start(ka[i][0:DH, :].bitcast(f32), qk_hi[u, rows, :]).then_inc(done, 16)
                        sp.dma_start(ka[i][DH:P, :].bitcast(f32), qk_hi[u, rows, :]).then_inc(done, 16)
                        sp.dma_start(kb[i][0:DH, :].bitcast(f32), qk_lo[u, rows, :]).then_inc(done, 16)
                        if aug is not None:
                            sp.dma_start(kb[i][DH:MROW + 2 * KBR, :].bitcast(f32), kaug[aug]).then_inc(s_kaug[i // 2 if nsa else i], 16)

                    for h in range(NH):
                        if h == 2 and not nsa:
                            sp.dma_start(raw_z[:, :].rearrange("p (k c) -> p k c", k=KT), w_in_v[:, :, C_ZN:C_ZN + P]).then_inc(s_raw_z, 16)
                        b, bq = h % 2, h % NQB
                        if h >= NQB:
                            sp.wait_ge(s_s, at[second[h - NQB][-1]] + 1)
                        rows = slice(b * DH, (b + 1) * DH)
                        u = (U_Q if nsa else U_DQ) + h // 2
                        if h:
                            sp.dma_start(qa[bq][0:DH, :].bitcast(f32), qk_hi[u, rows, :]).then_inc(s_load[bq], 16)
                            sp.dma_start(qb[bq][0:DH, :].bitcast(f32), qk_hi[u, rows, :]).then_inc(s_load[bq], 16)
                            sp.dma_start(qa[bq][DH:P, :].bitcast(f32), qk_lo[u, rows, :]).then_inc(s_load[bq], 16)
                            sp.dma_start(qb[bq][DH:MROW, :].bitcast(f32), qaug[(0 if nsa else NH) + h]).then_inc(s_load[bq], 16)
                        if nsa:
                            if h < NG:
                                for br in range(0 if h else 1, 2):
                                    keys(NG * h + br, U_KSLC + br, slice(h * DH, (h + 1) * DH), s_k[h], br)
                        else:
                            if h:
                                keys(b, U_DK + h // 2, rows, s_load[b], 0 if h == 1 else None)
                            if h == 0:
                                for i in range(2):
                                    first_near = (NT - NEAR) * P if i == 0 else 0
                                    sp.dma_start(dlog_h[i][:, :].bitcast(f32), dil_log[0, i]).then_inc(s_dlog[i], 16)
                                    sp.dma_start(dlog_l[i][:, :].bitcast(f32), dil_log[1, i, :, first_near:first_near + NEAR * P]).then_inc(s_dlog[i], 16)
                            if h >= 2:
                                sp.wait_ge(s_pv, p2_at[second[h - 2][-1]] + 1)
                            sp.dma_start(vd[b][:, :, :].bitcast(f32),
                                         v_dil[:, h, :, :].rearrange("(n p) a c -> p n (a c)", p=P)).then_inc(s_vload[b], 16)
                    if nsa:
                        sp.wait_ge(s_s, at[second[NH - 2][-1]] + 1)
                        load_first(sp, "dil")
                        sp.wait_ge(s_first["dil"], 16 * 8)

                @block.gpsimd
                def _(pool):
                    def add(h):
                        rows = slice(h % 2 * DH, h % 2 * DH + DH)
                        pool.wait_ge(s_ev, 4 * h + 4)
                        if h:
                            pool.wait_ge(s_add, h)
                        if lows:
                            pool.wait_ge(s_lop, lows)
                        nc.gpsimd.tensor_tensor(o_t[rows, h // 2, :], o_t[rows, h // 2, :], res[rows, :], ALU.add).then_inc(s_add, 1)

                    lows = adds = 0
                    for i, e in enumerate(items):
                        for h, when in taken_before.items():
                            if when == i:
                                add(h)
                                adds += 1
                        if e[0] == "p2" and on_pool[p2_at[e]]:
                            c = p2_at[e]
                            lo, hi = span(e[3], e[2])
                            n = CP if e[3] == 2 else P
                            pool.wait_ge(s_hi, c + 1)
                            if adds:
                                pool.wait_ge(s_add, adds)
                            if lows:
                                pool.wait_ge(s_lop, lows)
                            lows += 1
                            nc.gpsimd.tensor_tensor(pl[c % NHL][0:n, lo:hi], prob[c % NPR][0:n, lo:hi],
                                                    ph[c % NHL][0:n, lo:hi].bitcast(f32), ALU.subtract).then_inc(s_lop, 1)
                    add(NH - 1)

                @block.tensor
                def _(pe):
                    def scores(i, e):
                        if frees[i]:
                            pe.wait_ge(s_ra, frees[i])
                        if e[0] == "p1":
                            _, h, n, br = e
                            b, bq, g = h % 2, h % NQB, h // HPG
                            if e == first[h][0]:
                                if h == 0:
                                    pe.wait_ge(s_first[kind], 16 * 8)
                                else:
                                    pe.wait_ge(s_load[bq], 16 * (4 if nsa else 7) * (h // NQB + (1 if bq else 0)))
                                if nsa and h == HPG:
                                    pe.wait_ge(s_k[g], 16 * 6)
                                    pe.wait_ge(s_kaug[g], 32)
                                if not nsa and h == 1:
                                    pe.wait_ge(s_kaug[h], 16)
                                if not nsa and h == 0:
                                    pe.wait_ge(s_dlog[0], 32)
                            if nsa and e == first[0][NT]:
                                pe.wait_ge(s_k[0], 16 * 3)
                                pe.wait_ge(s_kaug[0], 16)
                            q = qa[bq][:, n * P:(n + 1) * P], qb[bq][0:DH + AUG, n * P:(n + 1) * P]
                            k0 = max(0, n - WIN_TILES) * P if br else 0
                            k1 = (n + 1) * P
                            kk = 2 * g + br if nsa else b
                            for c0, c1 in banks(0, k1 - k0):
                                keys = slice(k0 + c0, k0 + c1)
                                nc.tensor.matmul(scores_at(i, slice(0, P), c0, c1), q[0], ka[kk][:, keys], start=True, stop=False)
                                if nsa:
                                    marks = [(n * P - k0, n * P - k0 + P, identb[:, :], m_diag)]
                                    if br and n >= WIN_TILES:
                                        marks.append((0, P, identb[:, :], m_win))
                                    marks = [mark for mark in marks if c0 <= mark[0] < c1]
                                else:
                                    t0 = (NT - 1 - n) * P
                                    marks = [(c0, c1, identr[:, :], dlog_h[0][:, t0 + c0:t0 + c1])]
                                    x = max(c0, (n + 1 - NEAR) * P)
                                    if x < c1:
                                        y0 = t0 - (NT - NEAR) * P
                                        marks.append((x, c1, identr[:, :], dlog_l[0][:, y0 + x:y0 + c1]))
                                last = nc.tensor.matmul(scores_at(i, slice(0, P), c0, c1), q[1], kb[kk][0:DH + AUG, keys], start=False, stop=not marks)
                                for y, (x0, x1, one, mk) in enumerate(marks):
                                    last = nc.tensor.matmul(scores_at(i, slice(0, P), x0, x1), one, mk, start=False, stop=y == len(marks) - 1)
                            if nsa and br:
                                dst = scores_at(i, slice(0, P), k1 - k0, k1 - k0 + CP)
                                nc.tensor.matmul(dst, q[0], kc[:, g, 0, :], start=True, stop=False)
                                nc.tensor.matmul(dst, q[1], kc[0:DH + AUG, g, 1, :], start=False, stop=False)
                                last = nc.tensor.matmul(dst, identb[:, :], m_cmp[:, n * CP:(n + 1) * CP], start=False, stop=True)
                        elif e[0] == "m":
                            pe.wait_ge(s_spl, SPL * (e[1] + 1))
                            for n in range(NT):
                                last = nc.tensor.matmul(scores_at(i, slice(0, 2 * nbr), n * P, (n + 1) * P), negl2[:, n, :], identr[:, :], start=True, stop=True)
                        else:
                            _, h, m, br = e
                            b, bq, g = h % 2, h % NQB, h // HPG
                            if e == second[0][0] and not nsa:
                                pe.wait_ge(s_dlog[1], 32)
                            if e == second[h][0]:
                                pe.wait_ge(s_m, h + 1)
                            if br == 2:
                                k = kc[:, g, 0, :], kc[0:krows, g, 1, :]
                            else:
                                kk = 2 * g + br if nsa else b
                                k = ka[kk][:, m * P:(m + 1) * P], kb[kk][0:krows, m * P:(m + 1) * P]
                            n = CP if br == 2 else P
                            lo, hi = span(br, m)
                            for c0, c1 in banks(lo, hi):
                                nc.tensor.matmul(scores_at(i, slice(0, n), c0, c1), k[0], qa[bq][:, c0:c1], start=True, stop=False)
                                marks = []
                                if br == 2:
                                    marks += [(x, x + P, m_cmp[:, x // P * CP:(x // P + 1) * CP], identb[:, :]) for x in range(c0, c1, P)]
                                elif nsa:
                                    for x, mk in [(m * P, m_diag)] + [((m + WIN_TILES) * P, m_win)] * br:
                                        if c0 <= x < c1:
                                            marks.append((x, x + P, mk, identb[:, :]))
                                else:
                                    marks.append((c0, c1, identr[:, :], dlog_h[1][:, c0 - m * P:c1 - m * P]))
                                    x = min(c1, (m + NEAR) * P)
                                    if c0 < x:
                                        marks.append((c0, x, identr[:, :], dlog_l[1][:, c0 - m * P:x - m * P]))
                                last = nc.tensor.matmul(scores_at(i, slice(0, n), c0, c1), k[1], qb[bq][0:krows, c0:c1], start=False, stop=not marks)
                                for y, (x0, x1, one, mk) in enumerate(marks):
                                    last = nc.tensor.matmul(scores_at(i, slice(0, n), x0, x1), one, mk, start=False, stop=y == len(marks) - 1)
                        last.then_inc(s_s, 1)

                    def values(e):
                        _, h, m, br = e
                        c = p2_at[e]
                        o = ps[:, 3, :]
                        start, end = e == second[h][0], e == second[h][-1]
                        if start and not nsa:
                            pe.wait_ge(s_vload[h % 2], 16 * (h // 2 + 1))
                        pe.wait_ge(s_hi, c + 1)
                        low_done(pe, c)
                        if br == 2:
                            v, n = vc[:, h // HPG, :], CP
                        else:
                            v, n = (v_nsa[:, m, br, h // HPG, :] if nsa else vd[h % 2][:, m, :]), P
                        s0, s1 = span(br, m)
                        for c0, c1 in banks(s0, s1):
                            if start and h:
                                pe.wait_ge(s_ev, 4 * h - (0 if c0 else 2))
                            nc.tensor.matmul(o[:, c0:c1], v, ph[c % NHL][0:n, c0:c1], start=start, stop=False, skip_group_check=True)
                            last = nc.tensor.matmul(o[:, c0:c1], v, pl[c % NHL][0:n, c0:c1], start=False, stop=end, skip_group_check=True)
                        last.then_inc(s_pv, 1)

                    for e in events:
                        if e[0] == "v":
                            values(("p2",) + e[1:])
                        elif e[0] != "e":
                            scores(at[e], e)

                @block.scalar
                def _(act):
                    nmax = 0

                    def take(h):
                        act.wait_ge(s_pv, p2_at[second[h][-1]] + 1)
                        if h >= 2:
                            act.wait_ge(s_add, h - 1)
                        rows = slice(h % 2 * DH, h % 2 * DH + DH)
                        for cols in (slice(0, 512), slice(512, T)):
                            nc.scalar.activation(res[rows, cols], ps[DH:P, 3, cols], ACT.Copy).then_inc(s_ev, 1)
                            nc.scalar.activation(o_t[rows, h // 2, cols], ps[0:DH, 3, cols], ACT.Copy).then_inc(s_ev, 1)

                    for i in act_order:
                        e = items[i]
                        for h, when in taken_before.items():
                            if when == i:
                                take(h)
                        if e[0] == "p1":
                            _, h, n, br = e
                            k1 = (n + 1 - (max(0, n - WIN_TILES) if br else 0)) * P
                            parts = [(br, 0, k1)] + ([(2, k1, k1 + CP)] if br else [])
                            nmax += len(parts)
                            act.wait_ge(s_max, nmax)
                            for j, c0, c1 in parts:
                                nc.scalar.activation(scores_at(i, slice(0, P), c0, c1), scores_at(i, slice(0, P), c0, c1), ACT.Exp, bias=negm[:, h % 2, n, j:j + 1],
                                                     accum_out=sums[:, h % 2, n, j:j + 1]).then_inc(s_ra, 1)
                        elif e[0] == "m":
                            act.wait_ge(s_s, i + 1)
                            nc.scalar.activation(qb[e[1] % NQB][MROW:krows, :], scores_at(i, slice(0, 2 * nbr), 0, T), ACT.Copy).then_inc(s_ra, 1)
                            act.wait_ge(s_ra, reads[i])
                            act.sem_inc(s_m, 1)
                        else:
                            _, h, m, br = e
                            c = p2_at[e]
                            lo, hi = span(br, m)
                            n = CP if br == 2 else P
                            act.wait_ge(s_s, i + 1)
                            if c >= NPR:
                                act.wait_ge(s_hi, c - NPR + 1)
                                low_done(act, c - NPR)
                            nc.scalar.activation(prob[c % NPR][0:n, lo:hi], scores_at(i, slice(0, n), lo, hi), ACT.Exp).then_inc(s_ra, 1)

                    take(NH - 1)

                @block.vector
                def _(dve):
                    def parts(c):
                        _, h, m, br = p2s[c]
                        lo, hi = span(br, m)
                        n = CP if br == 2 else P
                        dve.wait_ge(s_ra, reads[at[p2s[c]]])
                        if c >= NHL:
                            dve.wait_ge(s_pv, c - NHL + 1)
                        nc.vector.tensor_copy(ph[c % NHL][0:n, lo:hi], prob[c % NPR][0:n, lo:hi]).then_inc(s_hi, 1)
                        if not on_pool[c]:
                            dve.wait_ge(s_hi, c + 1)
                            nc.vector.tensor_tensor(pl[c % NHL][0:n, lo:hi], prob[c % NPR][0:n, lo:hi],
                                                    ph[c % NHL][0:n, lo:hi].bitcast(f32), ALU.subtract).then_inc(s_lod, 1)

                    def finish(h, stage, nmax):
                        base = LOG * h + nsa
                        tmp = [t[:, :] for t in lg_tmp]
                        if stage == 0:
                            dve.wait_ge(s_ra, reads[at[first[h][-1]]])
                            dve.wait_ge(s_max, nmax)
                            if h:
                                dve.wait_ge(s_spl, SPL * h)
                            log_parts(dve, lsum[:, :], sums[:, h % 2, :, :].rearrange("p n b -> p (n b)"), tmp, 0.5, s_log, base)
                        elif stage == 1:
                            log_polynomial(dve, lsum[:, :], tmp, s_log, base)
                        else:
                            n2 = negl2[:, :, :].rearrange("p n (b t) -> p n b t", t=2)
                            dve.wait_ge(s_log, base + sum(LOG_STEPS))
                            nc.vector.tensor_tensor(negl[:, :, :], negm[:, h % 2, :, :], lsum[:, :].rearrange("p (n b) -> p n b", b=nbr),
                                                    ALU.subtract).then_inc(s_spl, 1)
                            dve.wait_ge(s_spl, SPL * h + 1)
                            if nsa:
                                nc.vector.tensor_tensor(negl[:, :, :], negl[:, :, :], lgate[:, :, :, h], ALU.add).then_inc(s_spl, 1)
                                dve.wait_ge(s_spl, SPL * h + 2)
                            if h:
                                dve.wait_ge(s_m, h)
                            nc.vector.tensor_copy(n2[:, :, :, 0], negl[:, :, :]).then_inc(s_spl, 1)
                            dve.wait_ge(s_spl, SPL * (h + 1) - 1)
                            nc.vector.tensor_tensor(n2[:, :, :, 1], negl[:, :, :], n2[:, :, :, 0].bitcast(f32), ALU.subtract).then_inc(s_spl, 1)

                    nmax, ready, summed, finishing = 0, [], None, None
                    for e in events:
                        if e[0] == "p1":
                            _, h, n, br = e
                            i = at[e]
                            k1 = (n + 1 - (max(0, n - WIN_TILES) if br else 0)) * P
                            nm = negm[:, h % 2, n, :]
                            dve.wait_ge(s_s, i + 1)
                            if e == first[h][0] and h >= 2:
                                dve.wait_ge(s_spl, SPL * (h - 1))
                            if br and n == 0:
                                nc.vector.tensor_reduce(nm[:, 2:3], scores_at(i, slice(0, P), k1, k1 + CP), AX.X, ALU.max, negate=True).then_inc(s_log, 1)
                                dve.wait_ge(s_log, LOG * h + 1)
                                nc.vector.tensor_scalar(nm[:, 2:3], nm[:, 2:3], -FLOOR, None, ALU.min).then_inc(s_max, 1)
                            elif br:
                                nc.vector.tensor_reduce(nm[:, 2:3], scores_at(i, slice(0, P), k1, k1 + CP), AX.X, ALU.max, negate=True).then_inc(s_max, 1)
                            nc.vector.tensor_reduce(nm[:, br:br + 1], scores_at(i, slice(0, P), 0, k1), AX.X, ALU.max, negate=True).then_inc(s_max, 1)
                            nmax += 2 if br else 1
                        if e[0] in ("p1", "p2"):
                            for c in ready:
                                parts(c)
                            ready = [p2_at[e]] if e[0] == "p2" else []
                        if finishing is not None and e[0] in ("p2", "m"):
                            for stage in range(finishing, finishing + 1 if e[0] == "p2" else 3):
                                if stage >= 0:
                                    finish(summed, stage, nmax)
                                finishing = stage + 1 if stage < 2 else None
                        if e[0] == "p1" and e == first[e[1]][-1]:
                            summed, finishing = e[1], (-1 if nsa else 0)
                    for c in ready:
                        parts(c)
            scope.close()

        attention("nsa", o_nsa)
        scope_v.close()
        o_d = sbuf(top, "o_d", [P, NH // 2, T])
        raw_z = sbuf(top, "raw_z", [P, KT * P])
        s_raw_z = sem(top, "s_raw_z")
        attention("dil", o_d)

        scope = ExitStack()
        gh = sbuf(scope, "gh", [P, 2 * NH // 2, T], r32)
        gl = sbuf(scope, "gl", [P, 2 * NH // 2, T], r32)
        zg = sbuf(scope, "zg", [P, 2, T])
        raw = [raw_z] + [sbuf(scope, f"c_raw{i}", [P, KT * P]) for i in range(2)]
        wth, wtl = shared_w[0:2], shared_w[2:4]
        ot = [sbuf(scope, f"ot{i}", [P, D]) for i in range(2)]
        fstat = sbuf(scope, "fstat", [P, 4, NT])
        sg = [o_nsa[:, i, :] for i in range(2)]
        fgb, junk = o_nsa[:, 0, :], o_nsa[:, 1, :]
        woh, wol = xh, xl
        mhs, mls = wth, wtl

        def merged(k):
            return o_nsa[:, 2 + k, :] if k < 2 else zg[:, k - 2, :] if k < 4 else o_d[:, k - 4, :]

        merged_groups = ((0, 2, o_nsa[:, 2:4, :]), (2, 4, zg[:, :, :]), (4, KT - 1, o_d[:, 0:3, :]), (KT - 1, KT, o_d[:, 3:4, :]))
        NMG = len(merged_groups)
        s_raw = [s_raw_z] + [sem(scope, f"c_raw{i}") for i in range(2)]
        s_whi, s_wlo, s_mm = (sem(scope, f"c_{n}") for n in ("whi", "wlo", "mm"))
        s_zs, s_gf, s_gh, s_gl = (sem(scope, f"z_{n}") for n in ("zs", "gf", "gh", "gl"))
        s_sg, s_y, s_y_first, s_mrg, s_mrg_last = (sem(scope, f"m_{n}") for n in ("sg", "y", "y_first", "mrg", "mrg_last"))
        s_st = [sem(scope, f"f_st{i}") for i in range(2)]
        s_fg, s_mh, s_ml, s_h, s_sq, s_ms, s_rt, s_ri, s_fin = (sem(scope, f"f_{n}") for n in (
            "fg", "mh", "ml", "h", "sq", "ms", "rt", "ri", "fin"))
        NZ = NH
        NM = 3 * KT
        NPC = NZ + NM + KT
        z_cols = [C_ZN + P * i for i in range(4)] + [C_ZD + P * i for i in range(4)]
        br_v = [w[0].rearrange("(k p) c -> p k c", p=P) for w in (w_br_nsa, w_br_dil)]
        wo_v = w_out[0].rearrange("(k p) e -> p k e", p=P)

        def m_step(i):
            return divmod(i - NZ, 3)

        def loads(i):
            return 2 if NZ <= i < NZ + NM and m_step(i)[1] == 2 else 1

        def raw_count(i):
            return 16 * sum(loads(j) for j in range(i % 3, i + 1, 3))

        def used(i):
            if i < NZ:
                return i + 1
            m, part = m_step(i)
            return NZ + 4 * m + (1, 2, 4)[part]

        block = nc.Block()
        with block:
            @block.sync
            def _(sp):
                for i in range(1, NPC):
                    dst = raw[i % 3][:, :].rearrange("p (k c) -> p k c", k=KT)
                    if i >= 3:
                        sp.wait_ge(s_wlo, i - 2)
                    if i < NZ:
                        sp.dma_start(dst, w_in_v[:, :, z_cols[i]:z_cols[i] + P]).then_inc(s_raw[i % 3], 16)
                    elif i < NZ + NM:
                        m, part = m_step(i)
                        if part < 2:
                            col = C_MG + part * D + m * P
                            sp.dma_start(dst, w_in_v[:, :, col:col + P]).then_inc(s_raw[i % 3], 16)
                        else:
                            for b in range(2):
                                sp.dma_start(dst[:, 4 * b:4 * b + 4, :], br_v[b][:, :, m * P:(m + 1) * P]).then_inc(s_raw[i % 3], 16)
                    else:
                        sp.dma_start(raw[i % 3][:, :], wo_v[:, i - NZ - NM, :]).then_inc(s_raw[i % 3], 16)
                sp.wait_ge(s_mrg_last, 2)
                sp.dma_start(fgb, final_g.rearrange("(a d) -> a d", a=1).partition_broadcast(P)).then_inc(s_fg, 16)
                for n in range(NT):
                    i = NPC + n
                    if n < 3:
                        sp.wait_ge(s_wlo, i - 2)
                    else:
                        sp.wait_ge(s_h, n - 2)
                    sp.dma_start(raw[i % 3][:, :], x_v[n]).then_inc(s_raw[i % 3], 16)
                    if n >= 1:
                        sp.wait_ge(s_fin, n)
                        sp.dma_start(out_v[n - 1], ot[(n - 1) % 2][:, :]).then_inc(s_st[(n - 1) % 2], 16)
                sp.wait_ge(s_fin, NT)
                sp.dma_start(out_v[NT - 1], ot[(NT - 1) % 2][:, :]).then_inc(s_st[(NT - 1) % 2], 16)
                for i in range(2):
                    sp.wait_ge(s_st[i], 16 * NT // 2)

            @block.gpsimd
            def _(pool):
                for i in range(NZ):
                    pool.wait_ge(s_gh, i + 1)
                    nc.gpsimd.tensor_tensor(gl[:, i, :], zg[:, 1, :], gh[:, i, :].bitcast(f32), ALU.subtract).then_inc(s_gl, 1)
                for m in range(KT - 1):
                    pool.wait_ge(s_y, 2 * (m + 1))
                    nc.gpsimd.tensor_tensor(merged(m), sg[0], sg[1], ALU.add).then_inc(s_mrg, 1)

            @block.scalar
            def _(act):
                def split(i):
                    act.wait_ge(s_raw[i % 3], raw_count(i))
                    if i < NZ + NM:
                        if i >= 2:
                            act.wait_ge(s_mm, used(i - 2))
                        dst = wth[i % 2][:, :, :].rearrange("p k c -> p (k c)")
                    else:
                        if i == NZ + NM:
                            act.wait_ge(s_mm, used(NZ + NM - 2))
                        dst = woh[:, i - NZ - NM, :]
                    nc.scalar.activation(dst, raw[i % 3][:, :], ACT.Copy).then_inc(s_whi, 1)

                split(0)
                for i in range(NZ):
                    split(i + 1)
                    act.wait_ge(s_mm, i + 1)
                    if i:
                        act.wait_ge(s_gf, i)
                    nc.scalar.activation(zg[:, 0, :], ps[:, i % 4, :], ACT.Silu).then_inc(s_zs, 1)
                    act.wait_ge(s_gf, i + 1)
                    nc.scalar.activation(gh[:, i, :], zg[:, 1, :], ACT.Copy).then_inc(s_gh, 1)
                for i in range(NZ, NZ + NM):
                    m, part = m_step(i)
                    split(i + 1)
                    if part < 2:
                        act.wait_ge(s_mm, used(i))
                        if m:
                            act.wait_ge(s_mrg, m)
                        nc.scalar.activation(sg[part], ps[:, part, :], ACT.Sigmoid).then_inc(s_sg, 1)

                def msplit(n, groups):
                    if n:
                        act.wait_ge(s_mrg_last, 2)
                        act.wait_ge(s_mm, NZ + 4 * KT + n - 1)
                    for k0, k1, cols in groups:
                        nc.scalar.activation(mhs[n % 2][:, k0:k1, :], cols[:, :, n * P:(n + 1) * P], ACT.Copy).then_inc(s_mh, 1)

                act.wait_ge(s_mrg, KT - 1)
                msplit(0, merged_groups[:-1])
                for i in range(NZ + NM + 1, NZ + NM + 6):
                    split(i)
                act.wait_ge(s_mrg_last, 1)
                msplit(0, merged_groups[-1:])
                for i in range(NZ + NM + 6, NPC):
                    split(i)
                for n in range(NT):
                    if n + 1 < NT:
                        msplit(n + 1, merged_groups)
                    act.wait_ge(s_h, n + 1)
                    if n:
                        act.wait_ge(s_sq, n)
                    nc.scalar.activation(junk, ot[n % 2][:, :], ACT.Square, accum_out=fstat[:, 0, n:n + 1]).then_inc(s_sq, 1)
                    act.wait_ge(s_ms, n + 1)
                    nc.scalar.activation(fstat[:, 2, n:n + 1], fstat[:, 1, n:n + 1], ACT.Sqrt).then_inc(s_rt, 1)

            @block.vector
            def _(dve):
                def split(i):
                    dve.wait_ge(s_whi, i + 1)
                    if i < NZ + NM:
                        hi, lo = (w[i % 2][:, :, :].rearrange("p k c -> p (k c)") for w in (wth, wtl))
                    else:
                        hi, lo = woh[:, i - NZ - NM, :], wol[:, i - NZ - NM, :]
                    nc.vector.tensor_tensor(lo, raw[i % 3][:, :], hi.bitcast(f32), ALU.subtract).then_inc(s_wlo, 1)

                def msplit(n, g):
                    k0, k1, cols = merged_groups[g]
                    dve.wait_ge(s_mh, NMG * n + g + 1)
                    nc.vector.tensor_tensor(mls[n % 2][:, k0:k1, :], cols[:, :, n * P:(n + 1) * P], mhs[n % 2][:, k0:k1, :].bitcast(f32),
                                            ALU.subtract).then_inc(s_ml, 1)

                split(0)
                for i in range(NZ):
                    split(i + 1)
                    dve.wait_ge(s_zs, i + 1)
                    if i:
                        dve.wait_ge(s_gl, i)
                    o = o_nsa if i < 4 else o_d
                    nc.vector.tensor_tensor(zg[:, 1, :], o[:, i % 4, :], zg[:, 0, :], ALU.mult).then_inc(s_gf, 1)
                for i in range(NZ, NZ + NM):
                    m, part = m_step(i)
                    split(i + 1)
                    if i == NZ + NM - 1:
                        for g in range(NMG - 1):
                            msplit(0, g)
                    if part == 2 and m < KT - 1:
                        for b in range(2):
                            dve.wait_ge(s_sg, 2 * m + b + 1)
                            dve.wait_ge(s_mm, NZ + 4 * m + 3 + b)
                            nc.vector.tensor_tensor(sg[b], ps[:, 2 + b, :], sg[b], ALU.mult).then_inc(s_y, 1)
                for j in range(NZ + NM + 1, NZ + NM + 4):
                    split(j)
                dve.wait_ge(s_sg, 2 * KT)
                dve.wait_ge(s_mm, NZ + 4 * KT - 1)
                nc.vector.tensor_tensor(sg[0], ps[:, 2, :], sg[0], ALU.mult).then_inc(s_y, 1)
                split(NZ + NM + 4)
                dve.wait_ge(s_mm, NZ + 4 * KT)
                for j, (cols, gated, count) in enumerate(((slice(0, P), s_y_first, 1), (slice(P, T), s_y, 2 * KT))):
                    nc.vector.tensor_tensor(sg[1][:, cols], ps[:, 3, cols], sg[1][:, cols], ALU.mult).then_inc(gated, 1)
                    dve.wait_ge(gated, count)
                    if j == 0:
                        dve.wait_ge(s_y, 2 * KT - 1)
                    nc.vector.tensor_tensor(merged(KT - 1)[:, cols], sg[0][:, cols], sg[1][:, cols], ALU.add).then_inc(s_mrg_last, 1)
                    if j == 0:
                        msplit(0, NMG - 1)
                        for w in range(NZ + NM + 5, NPC):
                            split(w)
                dve.wait_ge(s_fg, 16)
                for n in range(NT):
                    for g in range(NMG if n + 1 < NT else 0):
                        msplit(n + 1, g)
                    dve.wait_ge(s_mm, NZ + 4 * KT + n + 1)
                    dve.wait_ge(s_raw[(NPC + n) % 3], raw_count(NPC + n))
                    if n >= 2:
                        dve.wait_ge(s_st[n % 2], 16 * (n // 2))
                    nc.vector.tensor_tensor(ot[n % 2][:, :], ps[:, n % 4, :], raw[(NPC + n) % 3][:, :], ALU.add).then_inc(s_h, 1)
                    dve.wait_ge(s_sq, n + 1)
                    nc.vector.tensor_scalar(fstat[:, 1, n:n + 1], fstat[:, 0, n:n + 1], 1.0 / D, EPS, ALU.mult, ALU.add).then_inc(s_ms, 1)
                    dve.wait_ge(s_rt, n + 1)
                    nc.vector.reciprocal(fstat[:, 3, n:n + 1], fstat[:, 2, n:n + 1]).then_inc(s_ri, 1)
                    dve.wait_ge(s_ri, n + 1)
                    nc.vector.scalar_tensor_tensor(ot[n % 2][:, :], ot[n % 2][:, :], fstat[:, 3, n:n + 1], fgb, ALU.mult, ALU.mult).then_inc(s_fin, 1)

            @block.tensor
            def _(pe):
                def product(slot, w, ks, right_h, right_l):
                    for half in range(2):
                        cols = slice(half * 512, half * 512 + 512)
                        for k in ks:
                            nc.tensor.matmul(ps[:, slot, cols], wth[w][:, k, :], right_h[:, k, cols], start=(k == ks[0]), stop=False)
                            nc.tensor.matmul(ps[:, slot, cols], wth[w][:, k, :], right_l[:, k, cols], start=False, stop=False)
                            last = nc.tensor.matmul(ps[:, slot, cols], wtl[w][:, k, :], right_h[:, k, cols], start=False, stop=(k == ks[-1]))
                    last.then_inc(s_mm, 1)

                for i in range(NZ):
                    pe.wait_ge(s_wlo, i + 1)
                    if i >= 4:
                        pe.wait_ge(s_zs, i - 3)
                    product(i % 4, i % 2, range(KT), xh, xl)
                for i in range(NZ, NZ + NM):
                    m, part = m_step(i)
                    pe.wait_ge(s_wlo, i + 1)
                    if part < 2:
                        if m:
                            pe.wait_ge(s_sg, 2 * (m - 1) + part + 1)
                        else:
                            pe.wait_ge(s_zs, NZ - 3 + part)
                        product(part, i % 2, range(KT), xh, xl)
                    else:
                        for b in range(2):
                            if m:
                                pe.wait_ge(s_y, 2 * (m - 1) + b + 1)
                            else:
                                pe.wait_ge(s_zs, NZ - 1 + b)
                                pe.wait_ge(s_gl, 4 * (b + 1))
                            product(2 + b, i % 2, range(4 * b, 4 * b + 4), gh, gl)
                for n in range(NT):
                    pe.wait_ge(s_ml, NMG * (n + 1))
                    if n < 2:
                        pe.wait_ge(s_sg, 2 * KT - 1 + n)
                    elif n < 4:
                        pe.wait_ge(s_y, 2 * KT - 3 + n)
                    else:
                        pe.wait_ge(s_h, n - 3)
                    for k in range(KT):
                        if n == 0:
                            pe.wait_ge(s_wlo, NZ + NM + k + 1)
                        for half in range(2):
                            cols = slice(half * 512, half * 512 + 512)
                            nc.tensor.matmul(ps[:, n % 4, cols], mhs[n % 2][:, k, :], woh[:, k, cols], start=(k == 0), stop=False)
                            nc.tensor.matmul(ps[:, n % 4, cols], mhs[n % 2][:, k, :], wol[:, k, cols], start=False, stop=False)
                            last = nc.tensor.matmul(ps[:, n % 4, cols], mls[n % 2][:, k, :], woh[:, k, cols], start=False, stop=(k == KT - 1))
                    last.then_inc(s_mm, 1)
        scope.close()


_INS = ['x', 'norm_g', 'w_in', 'cmp_pos_k', 'cmp_w1_k', 'cmp_w2_k', 'cmp_pos_v', 'cmp_w1_v', 'cmp_w2_v',
        'w_br_nsa', 'w_br_dil', 'w_out', 'final_g']


def constants():
    import numpy as np
    q, k = np.arange(P)[:, None], np.arange(P)[None, :]
    diag = np.where(k > q, NEG, 0.0)
    win = np.where(k <= q, NEG, 0.0)
    t = np.arange(T).reshape(NT, P)
    c = np.arange(CP)
    end = c * CMP_STRIDE + CMP_BLOCK - 1
    cmp = np.where((end[None, None] <= t[:, :, None]) & (c < NCMP)[None, None], 0.0, NEG)
    masks = np.concatenate([diag, win, cmp.transpose(1, 0, 2).reshape(P, NT * CP)], axis=1).astype(np.float32)

    def held(dist):
        return sum(((dist >= 0) & (dist % r == 0) & (dist <= w)).astype(np.int64) for w, r in ((128, 1), (512, 4), (2048, 16)))

    tiles = np.arange(NT)
    by_q = held(q[:, None] - k[:, None] + P * (NT - 1 - tiles)[None, :, None])
    by_k = held(k[:, None] - q[:, None] + P * tiles[None, :, None])
    dil_log = np.stack([np.where(n > 0, np.log(np.maximum(n, 1)), NEG).reshape(P, T) for n in (by_q, by_k)]).astype(np.float32)

    def keys(at, branch):
        local, tile = at % P, at // P
        one = (tile[None, :] == np.arange(NT)[:, None]).astype(np.float32)
        ones = np.ones((2, at.size))
        rows = np.zeros((MROW + 2 * KBR - DH, at.size))
        rows[:AUG] = np.concatenate([ones, np.stack([local, local]), one, one])
        rows[MROW - DH + 2 * branch:MROW - DH + 2 * branch + 2] = 1.0
        return rows.astype(np.float32)

    def cut(a):
        a = a.astype(np.float32)
        hi = ((a.view(np.uint32) + 0x800) & np.uint32(0xFFFFF000)).view(np.float32)
        return hi, a - hi

    n_all = 2 * NH
    s = (2.0 ** (-8.0 * np.arange(1, n_all + 1) / n_all)).astype(np.float32)
    tt = np.arange(T)
    rows = []
    for slope in np.concatenate([s[0::2], s[1::2]]):
        a, b = cut(-slope * (tt % P).astype(np.float32))
        c_, d = cut(np.full(T, slope))
        e, f = cut(-slope * (P * (tt[None, :] // P - np.arange(NT)[:, None])).astype(np.float32))
        rows.append(np.concatenate([a[None], b[None], c_[None], d[None], e, f, np.zeros((MROW - DH - AUG, T))]))
    return (np.eye(P, dtype=np.float32), masks, np.stack([keys(tt, 0), keys(tt, 1)]), keys(end, 2), np.stack(rows).astype(np.float32),
            np.stack(cut(dil_log)))


def kernel(**inputs):
    import numpy as _np
    import concourse.bacc as _bacc
    from concourse import mybir as _mybir
    from concourse.bass_utils import run_bass_kernel_spmd as _run

    nc = _bacc.Bacc("TRN2", target_bir_lowering=False, num_devices=1)
    arrays, args = {}, []
    given = [(name, _np.ascontiguousarray(inputs[name])) for name in _INS]
    given += list(zip(("ident", "masks", "kaug", "kaug_cmp", "qaug", "dil_log"), constants()))
    for name, a in given:
        arrays[f"in_{name}_dram"] = a
        args.append(nc.dram_tensor(f"in_{name}_dram", a.shape, _mybir.dt.from_np(a.dtype), kind="ExternalInput").ap())
    args.append(nc.dram_tensor("out_0_dram", (1, T, D), _mybir.dt.float32, kind="ExternalOutput").ap())
    program(nc, *args)
    r = _run(nc, [arrays], core_ids=[0])
    return r.results[0]["out_0_dram"]
```
